# Optimizing a Trainium2 kernel written in Bass

```python
import math
import jax, jax.numpy as jnp
from jax import lax
import numpy as np

D_MODEL = 1024
BATCH = 1
SEQ = 256
DEPTH = 1

HEAD_DIM = 64
FOX_HEADS = 4
MLA_HEADS = 6
DIL_HEADS = 6
MLA_Q_RANK = 384
MLA_KV_RANK = 256
MLA_NOPE_DIM = 64
MLA_ROPE_DIM = 32
MLA_QK_DIM = MLA_NOPE_DIM + MLA_ROPE_DIM
MLA_V_DIM = 64
ROT_DIM = HEAD_DIM // 4
ROPE_THETA = 500000.0
DILATED_PATTERNS = ((128, 1), (512, 4), (2048, 16))
Q_BLOCK = 128
FOX_WIDTH = FOX_HEADS * HEAD_DIM
MLA_WIDTH = MLA_HEADS * MLA_V_DIM
DIL_WIDTH = DIL_HEADS * HEAD_DIM
MIX_WIDTH = FOX_WIDTH + MLA_WIDTH + DIL_WIDTH
MEM_TOKENS = 256
MEM_HEADS = 4
MEM_WIDTH = MEM_HEADS * HEAD_DIM
N_EXPERTS = 32
TOP_K = 4
D_EXPERT = 1024
SWIGLU_ALPHA = 1.702
SWIGLU_LIMIT = 7.0
MOE_CHUNK = 512
RMS_EPS = 1e-6
IN_SPLIT_SIZES = (FOX_WIDTH, FOX_WIDTH, FOX_WIDTH, FOX_HEADS,
                  MLA_Q_RANK, MLA_KV_RANK, MLA_ROPE_DIM,
                  DIL_WIDTH, DIL_WIDTH, DIL_WIDTH)
IN_SPLIT_POINTS = tuple(int(v) for v in np.cumsum(IN_SPLIT_SIZES)[:-1])
IN_WIDTH = int(sum(IN_SPLIT_SIZES))

kernel_name = "hybrid_fox_mla_dilated_moe_block"

def rms_norm(x, g):
    xf = x.astype(jnp.float32)
    y = xf * lax.rsqrt(jnp.mean(xf * xf, axis=-1, keepdims=True) + RMS_EPS)
    return (y * g.astype(jnp.float32)).astype(x.dtype)

def rope_tables(positions, rot_dim):
    inv = ROPE_THETA ** (-jnp.arange(0, rot_dim, 2, dtype=jnp.float32) / rot_dim)
    ang = positions.astype(jnp.float32)[..., None] * inv
    return jnp.cos(ang)[:, :, None, :], jnp.sin(ang)[:, :, None, :]

def apply_rope(x, cos, sin):
    x1, x2 = jnp.split(x.astype(jnp.float32), 2, axis=-1)
    return jnp.concatenate([x1 * cos - x2 * sin, x2 * cos + x1 * sin], axis=-1).astype(x.dtype)

def causal_dense_attention(q, k, v, scale, cum_log_forget=None):
    B, S, H, _ = q.shape
    nb = S // Q_BLOCK
    q_blocks = q.reshape(B, nb, Q_BLOCK, H, -1).swapaxes(0, 1)
    key_pos = jnp.arange(S)
    if cum_log_forget is None:
        c_blocks, c_keys = None, None
    else:
        c_keys = cum_log_forget.transpose(0, 2, 1)
        c_blocks = cum_log_forget.reshape(B, nb, Q_BLOCK, H).transpose(1, 0, 3, 2)

    def block(args):
        i, q_i, c_i = args
        s = jnp.einsum("bqhd,bkhd->bhqk", q_i, k, preferred_element_type=jnp.float32) * scale
        if c_i is not None:
            s = s + (c_i[..., None] - c_keys[:, :, None, :])
        q_pos = i * Q_BLOCK + jnp.arange(Q_BLOCK)
        s = jnp.where(key_pos[None, :] <= q_pos[:, None], s, -jnp.inf)
        p = jax.nn.softmax(s, axis=-1).astype(v.dtype)
        return jnp.einsum("bhqk,bkhd->bqhd", p, v)

    out = lax.map(block, (jnp.arange(nb), q_blocks, c_blocks))
    return out.swapaxes(0, 1).reshape(B, S, H, -1)

def dilated_window_attention(q, k, v, window, dilation, scale):
    B, S, H, Dh = q.shape
    n = window // dilation
    L = S // dilation
    nb = -(-L // n)
    Lp = nb * n

    def to_blocks(t):
        t = t.reshape(B, L, dilation, H, Dh).transpose(0, 2, 1, 3, 4)
        t = jnp.pad(t, ((0, 0), (0, 0), (0, Lp - L), (0, 0), (0, 0)))
        return t.reshape(B, dilation, nb, n, H, Dh)

    def with_prev(t):
        prev = jnp.pad(t, ((0, 0), (0, 0), (1, 0), (0, 0), (0, 0), (0, 0)))[:, :, :-1]
        return jnp.concatenate([prev, t], axis=3)

    qb = to_blocks(q)
    kc = with_prev(to_blocks(k))
    vc = with_prev(to_blocks(v))
    s = jnp.einsum("bgcqhd,bgckhd->bgchqk", qb, kc, preferred_element_type=jnp.float32) * scale
    qq = jnp.arange(n)[:, None]
    kk = jnp.arange(2 * n)[None, :]
    rel = qq + n - kk
    blk = jnp.arange(nb)[:, None, None]
    valid = (rel >= 0) & (rel <= n) & (blk * n - n + kk >= 0)
    s = jnp.where(valid[:, None], s, -jnp.inf)
    lse = jax.nn.logsumexp(s, axis=-1)
    p = jnp.exp(s - lse[..., None]).astype(v.dtype)
    o = jnp.einsum("bgchqk,bgckhd->bgcqhd", p, vc)

    def from_blocks(t):
        t = t.reshape(B, dilation, Lp, H, -1)[:, :, :L]
        return t.transpose(0, 2, 1, 3, 4).reshape(B, S, H, -1)

    lse_seq = from_blocks(lse.transpose(0, 1, 2, 4, 3)[..., None])[..., 0]
    return from_blocks(o), lse_seq

def parallel_head_groups(h, positions, w_in, b_forget, g_qa, g_ka, g_cq, g_ckv, w_uq, w_ukv,
                         g_qb, g_kb, g_qc, g_kc, g_group, w_out):
    B, S, _ = h.shape
    proj = h @ w_in
    qa, ka, va, fa, cq, ckv, kr, qc, kc, vc = jnp.split(proj, IN_SPLIT_POINTS, axis=-1)

    qa = rms_norm(qa.reshape(B, S, FOX_HEADS, HEAD_DIM), g_qa)
    ka = rms_norm(ka.reshape(B, S, FOX_HEADS, HEAD_DIM), g_ka)
    va = va.reshape(B, S, FOX_HEADS, HEAD_DIM)
    log_f = jax.nn.log_sigmoid((fa + b_forget).astype(jnp.float32))
    cum = jnp.cumsum(log_f, axis=1)
    oa = causal_dense_attention(qa, ka, va, HEAD_DIM ** -0.5, cum)

    cq = rms_norm(cq, g_cq)
    ckv = rms_norm(ckv, g_ckv)
    qb = (cq @ w_uq).reshape(B, S, MLA_HEADS, MLA_QK_DIM)
    kvb = (ckv @ w_ukv).reshape(B, S, MLA_HEADS, MLA_NOPE_DIM + MLA_V_DIM)
    k_nope, vb = kvb[..., :MLA_NOPE_DIM], kvb[..., MLA_NOPE_DIM:]
    k_rope = jnp.broadcast_to(kr[:, :, None, :], (B, S, MLA_HEADS, MLA_ROPE_DIM))
    kb = jnp.concatenate([k_nope, k_rope], axis=-1)
    qb = rms_norm(qb, g_qb)
    kb = rms_norm(kb, g_kb)
    cos_b, sin_b = rope_tables(positions, MLA_ROPE_DIM)
    qb = jnp.concatenate([qb[..., :MLA_NOPE_DIM], apply_rope(qb[..., MLA_NOPE_DIM:], cos_b, sin_b)], axis=-1)
    kb = jnp.concatenate([kb[..., :MLA_NOPE_DIM], apply_rope(kb[..., MLA_NOPE_DIM:], cos_b, sin_b)], axis=-1)
    ob = causal_dense_attention(qb, kb, vb, MLA_QK_DIM ** -0.5)

    qc = rms_norm(qc.reshape(B, S, DIL_HEADS, HEAD_DIM), g_qc)
    kc = rms_norm(kc.reshape(B, S, DIL_HEADS, HEAD_DIM), g_kc)
    vc = vc.reshape(B, S, DIL_HEADS, HEAD_DIM)
    cos_c, sin_c = rope_tables(positions, ROT_DIM)
    qc = jnp.concatenate([apply_rope(qc[..., :ROT_DIM], cos_c, sin_c), qc[..., ROT_DIM:]], axis=-1)
    kc = jnp.concatenate([apply_rope(kc[..., :ROT_DIM], cos_c, sin_c), kc[..., ROT_DIM:]], axis=-1)
    outs, lses = [], []
    for window, dilation in DILATED_PATTERNS:
        o_i, lse_i = dilated_window_attention(qc, kc, vc, window, dilation, HEAD_DIM ** -0.5)
        outs.append(o_i)
        lses.append(lse_i)
    mix_w = jax.nn.softmax(jnp.stack(lses, axis=0), axis=0)
    oc = jnp.sum(mix_w[..., None] * jnp.stack(outs, axis=0).astype(jnp.float32), axis=0).astype(h.dtype)

    ga, gb, gc = jnp.split(g_group, [FOX_WIDTH, FOX_WIDTH + MLA_WIDTH])
    merged = jnp.concatenate([rms_norm(oa.reshape(B, S, FOX_WIDTH), ga),
                              rms_norm(ob.reshape(B, S, MLA_WIDTH), gb),
                              rms_norm(oc.reshape(B, S, DIL_WIDTH), gc)], axis=-1)
    return merged @ w_out

def memory_cross_attention(h, mem_n, w_mq, w_mkv, g_qm, g_km, w_mo):
    B, S, _ = h.shape
    M = mem_n.shape[1]
    q = rms_norm((h @ w_mq).reshape(B, S, MEM_HEADS, HEAD_DIM), g_qm)
    k, v = jnp.split(mem_n @ w_mkv, 2, axis=-1)
    k = rms_norm(k.reshape(B, M, MEM_HEADS, HEAD_DIM), g_km)
    v = v.reshape(B, M, MEM_HEADS, HEAD_DIM)
    s = jnp.einsum("bshd,bmhd->bhsm", q, k, preferred_element_type=jnp.float32) * HEAD_DIM ** -0.5
    p = jax.nn.softmax(s, axis=-1).astype(v.dtype)
    o = jnp.einsum("bhsm,bmhd->bshd", p, v).reshape(B, S, MEM_WIDTH)
    return o @ w_mo

def routed_expert_ffn(h, w_router, b_router, w_e1, b_e1, w_e2, b_e2):
    B, S, D = h.shape
    T = B * S
    ht = h.reshape(T, D)
    logits = (ht @ w_router + b_router).astype(jnp.float32)
    top_vals, top_idx = lax.top_k(logits, TOP_K)
    top_w = jax.nn.softmax(top_vals, axis=-1)
    gate = jnp.einsum("tk,tke->te", top_w, jax.nn.one_hot(top_idx, N_EXPERTS, dtype=jnp.float32))
    chunk = math.gcd(T, MOE_CHUNK)
    nc = T // chunk

    def expert_block(args):
        xc, gc = args
        hh = jnp.einsum("td,edf->tef", xc, w_e1) + b_e1
        glu = jnp.minimum(hh[..., 0::2], SWIGLU_LIMIT)
        lin = jnp.clip(hh[..., 1::2], -SWIGLU_LIMIT, SWIGLU_LIMIT)
        act = glu * jax.nn.sigmoid(SWIGLU_ALPHA * glu) * (lin + 1.0)
        act = act * gc[..., None].astype(act.dtype)
        return jnp.einsum("tef,efd->td", act, w_e2) + gc.astype(b_e2.dtype) @ b_e2

    y = lax.map(expert_block, (ht.reshape(nc, chunk, D), gate.reshape(nc, chunk, N_EXPERTS)))
    return y.reshape(B, S, D).astype(h.dtype)

def setup_inputs(seed: int = 0) -> dict:
    key = jax.random.key(seed)
    ks = iter(jax.random.split(key, 48))
    f32 = jnp.float32
    L, D = DEPTH, D_MODEL

    def w(shape, fan_in):
        return jax.random.normal(next(ks), shape, f32) * (fan_in ** -0.5)

    def gain(shape):
        return 1.0 + 0.02 * jax.random.normal(next(ks), shape, f32)

    def small(shape, scale=0.01):
        return scale * jax.random.normal(next(ks), shape, f32)

    x = jax.random.normal(next(ks), (BATCH, SEQ, D), f32)
    mem = jax.random.normal(next(ks), (BATCH, MEM_TOKENS, D), f32)
    positions = (jnp.arange(SEQ, dtype=jnp.int32)[None, :]
                 + jax.random.randint(next(ks), (BATCH, 1), 0, 1024, dtype=jnp.int32))
    return {
        "x": x, "mem": mem, "positions": positions,
        "g_mix": gain((L, D)),
        "w_in": w((L, D, IN_WIDTH), D),
        "b_forget": 3.0 + 0.1 * jax.random.normal(next(ks), (L, FOX_HEADS), f32),
        "g_qa": gain((L, HEAD_DIM)), "g_ka": gain((L, HEAD_DIM)),
        "g_cq": gain((L, MLA_Q_RANK)), "g_ckv": gain((L, MLA_KV_RANK)),
        "w_uq": w((L, MLA_Q_RANK, MLA_HEADS * MLA_QK_DIM), MLA_Q_RANK),
        "w_ukv": w((L, MLA_KV_RANK, MLA_HEADS * (MLA_NOPE_DIM + MLA_V_DIM)), MLA_KV_RANK),
        "g_qb": gain((L, MLA_QK_DIM)), "g_kb": gain((L, MLA_QK_DIM)),
        "g_qc": gain((L, HEAD_DIM)), "g_kc": gain((L, HEAD_DIM)),
        "g_group": gain((L, MIX_WIDTH)),
        "w_out": w((L, MIX_WIDTH, D), MIX_WIDTH),
        "g_xmem": gain((L, D)), "g_mem": gain((L, D)),
        "w_mq": w((L, D, MEM_WIDTH), D),
        "w_mkv": w((L, D, 2 * MEM_WIDTH), D),
        "g_qm": gain((L, HEAD_DIM)), "g_km": gain((L, HEAD_DIM)),
        "w_mo": w((L, MEM_WIDTH, D), MEM_WIDTH),
        "g_ffn": gain((L, D)),
        "w_router": w((L, D, N_EXPERTS), D),
        "b_router": small((L, N_EXPERTS)),
        "w_e1": w((L, N_EXPERTS, D, 2 * D_EXPERT), D),
        "b_e1": small((L, N_EXPERTS, 2 * D_EXPERT)),
        "w_e2": w((L, N_EXPERTS, D_EXPERT, D), D_EXPERT),
        "b_e2": small((L, N_EXPERTS, D)),
    }

def reference(x, mem, positions, g_mix, w_in, b_forget, g_qa, g_ka, g_cq, g_ckv, w_uq, w_ukv,
              g_qb, g_kb, g_qc, g_kc, g_group, w_out, g_xmem, g_mem, w_mq, w_mkv, g_qm, g_km,
              w_mo, g_ffn, w_router, b_router, w_e1, b_e1, w_e2, b_e2):
    for l in range(DEPTH):
        x = x + parallel_head_groups(rms_norm(x, g_mix[l]), positions, w_in[l], b_forget[l],
                                     g_qa[l], g_ka[l], g_cq[l], g_ckv[l], w_uq[l], w_ukv[l],
                                     g_qb[l], g_kb[l], g_qc[l], g_kc[l], g_group[l], w_out[l])
        x = x + memory_cross_attention(rms_norm(x, g_xmem[l]), rms_norm(mem, g_mem[l]),
                                       w_mq[l], w_mkv[l], g_qm[l], g_km[l], w_mo[l])
        x = x + routed_expert_ffn(rms_norm(x, g_ffn[l]), w_router[l], b_router[l],
                                  w_e1[l], b_e1[l], w_e2[l], b_e2[l])
    return x


_drawn_inputs = setup_inputs


def setup_inputs(seed=0):
    import zlib

    import numpy as np

    out = dict(_drawn_inputs(seed))
    spreads = {}
    factors = {'g_qa': 4.328,
     'g_ka': 3.602,
     'g_qc': 3.191,
     'g_kc': 3.296,
     'g_xmem': 5.226,
     'g_mem': 5.224,
     'g_qm': 7.517,
     'g_km': 8.0,
     'b_e1': 48.781,
     'b_e2': 56.505,
     'g_ffn': 5.079,
     'b_router': 8.0}
    for name, (base, spread) in spreads.items():
        noise = np.random.default_rng([zlib.crc32(name.encode()), seed]).standard_normal(out[name].shape)
        drawn = base * np.exp(spread * noise) if base else spread * noise
        out[name] = __import__('jax').numpy.asarray(drawn.astype(out[name].dtype))
    for name, factor in factors.items():
        out[name] = (out[name] * factor).astype(out[name].dtype)
    return out
```

```python
import math

import numpy as np

import concourse.bass as bass
from concourse import mybir

F32 = mybir.dt.float32
F32R = mybir.dt.float32r
I32 = mybir.dt.int32
ALU = mybir.AluOpType
ACT = mybir.ActivationFunctionType
AX = mybir.AxisListType

P = 128
D = 1024
T = 256
NT = T // P
KC = D // P
HD = 64
FOX_H, MLA_H, DIL_H, MEM_H = 4, 6, 6, 4
Q_RANK, KV_RANK = 384, 256
NOPE, ROPE = 64, 32
QK = NOPE + ROPE
ROT = HD // 4
THETA = 500000.0
EPS = 1e-6
BIG = 1e30
E = 32
TOPK = 4
F = 1024
SLOTS = 64
MAX_ROUNDS = T // SLOTS
STEPS = E * MAX_ROUNDS
ALPHA, LIMIT = 1.702, 7.0

WIDTHS = [("qa", 256), ("ka", 256), ("va", 256), ("fa", 4), ("cq", Q_RANK), ("ckv", KV_RANK),
          ("kr", ROPE), ("qc", 384), ("kc", 384), ("vc", 384)]
COL = {}
_at = 0
for _name, _w in WIDTHS:
    COL[_name] = (_at, _at + _w)
    _at += _w
IN_W = _at
CHUNKS = [("cq", "cq", 65536), ("ckv", "kr", 77824), ("qa", "ka", 0), ("va", "fa", 16384),
          ("qc", "qc", 24704), ("kc", "kc", 36992), ("vc", "vc", 49280)]
CHUNKS = [(COL[a][0], COL[b][1], at) for a, b, at in CHUNKS]

UNIT = 2048
W1_UNITS, W2_UNITS = KC, F // P // 2
UNITS = W1_UNITS + W2_UNITS
SPLIT_W1 = (0, 2, 4, 6)
WHOLE = W1_UNITS - len(SPLIT_W1)
MM_SELF = 29
MM_MEM = 67
SPLITS = len(SPLIT_W1) + W2_UNITS


def build(nc, x, mem, positions, g_mix, w_in, b_forget, g_qa, g_ka, g_cq, g_ckv, w_uq, w_ukv,
          g_qb, g_kb, g_qc, g_kc, g_group, w_out, g_xmem, g_mem, w_mq, w_mkv, g_qm, g_km,
          w_mo, g_ffn, w_router, b_router, w_e1, b_e1, w_e2, b_e2, out):
    base = 16512

    def at(name, shape, off, dt=F32):
        return nc.alloc_sbuf_tensor_at(name, shape, dt, offset=base + off)

    ring = at("ring", [P, UNITS, UNIT], 0)
    win = [at(f"w_in{n}", [P, KC, b - a], o) for n, (a, b, o) in enumerate(CHUNKS)]
    QKb = at("mla_qk", [P, 2, NT, MLA_H, QK], 87040)
    mlaT = at("mla_T", [P, 2, MLA_H, T], 65536)
    dilT = at("dil_T", [P, 2, 3, T], 77824)
    Vb = at("mla_v", [P, NT, MLA_H, HD], 83968)
    wout = at("w_out_sb", [P, KC, D], 0)
    wmq = at("w_mq_sb", [P, KC, 256], 32768)
    wmo = at("w_mo_sb", [P, 2, D], 40960)
    R = UNITS * UNIT * 4
    X = at("x_sb", [P, NT, D], R)
    H = at("h_sb", [P, NT, D], R + 8192)
    hT = at("h_T", [P, KC, T], R + 16384)
    proj = at("proj", [P, NT, IN_W], R + 24576)
    gain = at("gains", [P, 2, D], R + 45376)
    SG = {}
    small_at = 0
    small_list = [("g_qa", g_qa), ("g_ka", g_ka), ("g_qc", g_qc), ("g_kc", g_kc), ("g_qm", g_qm),
                  ("g_km", g_km), ("g_cq", g_cq), ("g_ckv", g_ckv), ("g_qb", g_qb), ("g_kb", g_kb),
                  ("b_router", b_router), ("b_forget", b_forget)]
    smalls = at("small_gains", [P, 1256], R + 53568)
    for n_, a_ in small_list:
        SG[n_] = smalls[:, small_at:small_at + a_.shape[-1]]
        small_at += a_.shape[-1]
    wuq = at("w_uq_sb", [P, 3, MLA_H * QK], R + 58592)
    rtmp = at("rope_tmp", [P, 2, 2, MLA_H, ROPE], R + 58592)
    wukv = at("w_ukv_sb", [P, 2, MLA_H * 128], R + 65504)
    wmkv = at("w_mkv_sb", [P, KC, 512], R + 71648)
    cqT = at("cq_T", [P, 3, T], R + 71648)
    ckvT = at("ckv_T", [P, 2, T], R + 74720)
    foxNB = at("fox_bias", [P, FOX_H, 384], R + 76768)
    foxT = at("fox_T", [P, 2, 2, T], R + 82912)
    KVm = at("mem_kv", [P, NT, 512], R + 88032)
    memT = at("mem_kT", [P, 2, T], R + 92128)
    NBs = at("mask_bias", [P, 2, 384], R + 94176)
    SCR = at("scratch", [P, 3072], R + 97248)
    Sb, Pb, PTb = (SCR[:, 1024 * k:1024 * k + 1024].rearrange("p (b n) -> p b n", b=2) for k in range(3))
    rope = at("rope_tab", [P, 8, NT, 16], R + 109536)
    U = at("upper", [P, 3, P], R + 110560)
    ident = at("ident", [P, P], R + 112096)
    stat = at("stat", [P, 448], R + 112608)
    router_w = at("w_router_sb", [P, KC, E], 49152)
    qm = at("mem_q", [P, NT, 256], 50176)
    qmT = at("mem_qT", [P, 2, T], 52224)
    om = at("mem_o", [P, NT, 256], 54272)
    omT = at("mem_oT", [P, 2, T], 56320)
    slot_of = at("slot_table", [P, NT, STEPS + 4], R + 8192)
    gate_of = at("gate_table", [P, NT, STEPS + 4], R + 9248)
    iota = at("iota", [P, P], R + 10304)
    pick = at("picked", [P, 3, NT], R + 10816)
    hotg = at("hot_gate", [P, NT, P], R + 11840)
    hotr = at("hot_r", [P, NT, SLOTS], R + 12864, F32R)
    hotT = at("hot_gate_T", [P, T], R + 13376)
    rt = at("route", [P, 12, NT, 36], R + 16384)
    b1s = at("b1_rows", [P, 512], R + 19840)
    b1T = at("b1_T", [P, E, 16], R + 21888)
    stack = at("stacked_ident", [P, SLOTS], R + 23936)
    XR = at("h_parts", [P, 2, NT, D], R + 24576, F32R)
    split = at("w_parts", [P, 2, 2, UNIT], R + 40960, F32R)
    xgr = at("xg_parts", [P, KC, 2, SLOTS], R + 73728, F32R)
    xgf = at("xg_full", [P, KC, 2, SLOTS], R + 77824)
    Hs = at("hidden", [P, 2 * F], R + 81920)
    glu = at("glu", [P, KC, SLOTS], R + 90112)
    lin = at("lin", [P, KC, SLOTS], R + 92160)
    sig = at("sig", [P, KC, SLOTS], R + 94208)
    act_f = at("act_full", [P, KC, SLOTS], R + 96256)
    actr = at("act_parts", [P, KC, 2, SLOTS], R + 98304, F32R)
    Ys = at("y_sb", [P, D], R + 102400)
    b2s = at("b2_sb", [E, D], R + 102400)
    more_i = at("more_steps", [P, 1], R + 106496, I32)
    PS = nc.alloc_psum_tensor("banks", [P, 8, 512], F32)

    sems = {}

    def S(name):
        if name not in sems:
            sems[name] = nc.alloc_semaphore(name)
        return sems[name]

    V, G, A, TE = nc.vector, nc.gpsimd, nc.scalar, nc.tensor

    REQ = [2, 2, 8, 4, 16, 24, 24, 6, 2, 8, 2]
    NREQ = sum(REQ)

    def cols_of(kind, k):
        a = kind * NREQ + sum(REQ[:k])
        return stat[:, a:a + REQ[k]]

    o = 4 * NREQ
    rowmax, rowsum, rowinv = stat[:, o:o + 4], stat[:, o + 4:o + 12], stat[:, o + 12:o + 16]
    logf, fz, fa2, cumq, fe = (stat[:, o + 16 + 8 * k:o + 24 + 8 * k].rearrange("p (t h) -> p t h", t=2)
                               for k in range(5))
    rowtmp = tmp4 = stat[:, 3 * NREQ:3 * NREQ + 4]
    logfb = SCR[:, 0:1024].rearrange("p (t h m) -> p t h m", t=2, h=4)

    def units():
        for h in range(FOX_H):
            r, j = 64 * (h % 2), h // 2
            yield (foxT[r:r + 64, 0, j, :], foxT[r:r + 64, 1, j, :],
                   [proj[:, t, COL["va"][0] + 64 * h:COL["va"][0] + 64 * h + 64] for t in range(NT)],
                   foxNB[:, h, :], HD ** -0.5, H[:, :, 64 * h:64 * h + 64])
        for h in range(MLA_H):
            yield (mlaT[0:QK, 0, h, :], mlaT[0:QK, 1, h, :], [Vb[:, t, h, :] for t in range(NT)],
                   NBs[:, 0, :], QK ** -0.5, H[:, :, 256 + 64 * h:320 + 64 * h])
        for h in range(DIL_H):
            r, j = 64 * (h % 2), h // 2
            yield (dilT[r:r + 64, 0, j, :], dilT[r:r + 64, 1, j, :],
                   [proj[:, t, COL["vc"][0] + 64 * h:COL["vc"][0] + 64 * h + 64] for t in range(NT)],
                   NBs[:, 1, :], HD ** -0.5, H[:, :, 640 + 64 * h:704 + 64 * h])

    SELF = list(units())
    MEM = [(qmT[64 * (h % 2):64 * (h % 2) + 64, h // 2, :], memT[64 * (h % 2):64 * (h % 2) + 64, h // 2, :],
            [KVm[:, t, 256 + 64 * h:320 + 64 * h] for t in range(NT)], None, HD ** -0.5,
            om[:, :, 64 * h:64 * h + 64]) for h in range(MEM_H)]

    memx = at("mem_sb", [P, NT, D], R + 24576 + 12288)
    mtmp = at("mask_tmp", [P, 8, 384], R + 24576)
    mtmp_i = at("mask_tmp_int", [P, 8, 384], R + 24576, I32)
    rope_i = at("rope_int", [P, 8, NT, 16], R + 109536, I32)
    pos_i = rope_i[:, 5, 0, 0:NT]
    rt_gateT = at("gate_T", [E, T], R + 16384 + 8 * 72 * 4)

    def order(n):
        for s in range(n + 3):
            if s < n:
                yield "score", s
            if 0 <= s - 2 < n:
                yield "turn", s - 2
            if 0 <= s - 3 < n:
                yield "value", s - 3

    class Banks:

        def __init__(self, first):
            self.first, self.n = first, 0

        def next(self):
            self.n += 1
            return PS[:, self.first + (self.n - 1) % 4, :]

    def tiles_of(src, col, width):
        return src[:, :, col:col + width]

    def heads(ap, h):
        return ap.rearrange("p t (h d) -> p t h d", h=h)

    def parts_of(i, s):
        return s + 1 if i == 0 else 8 * i - 4 + s + 1

    block = nc.Block()
    blk = block.__enter__()

    @blk.sync
    def _(sp):
        sp.dma_start(memx[:], mem[0].rearrange("(t p) d -> p t d", p=P)).then_inc(S("mem_in"), 16)
        sp.dma_start(X[:], x[0].rearrange("(t p) d -> p t d", p=P)).then_inc(S("x_in"), 16)
        sp.dma_start(wmkv[:], w_mkv[0].rearrange("(c p) n -> p c n", p=P)).then_inc(S("w_mkv_in"), 16)
        w_in_v = w_in[0].rearrange("(c p) n -> p c n", p=P)
        for n, (a, b, _) in enumerate(CHUNKS):
            sp.dma_start(win[n][:], w_in_v[:, :, a:b]).then_inc(S(f"w_in{n}_in"), 16)
            if n == 2:
                sp.dma_start(wuq[:], w_uq[0].rearrange("(c p) n -> p c n", p=P)).then_inc(S("w_uq_in"), 16)
                sp.dma_start(wukv[:], w_ukv[0].rearrange("(c p) n -> p c n", p=P)).then_inc(S("w_ukv_in"), 16)
        sp.wait_ge(S("projected"), 1)
        sp.dma_start(wout[:], w_out[0].rearrange("(c p) n -> p c n", p=P)).then_inc(S("w_out_in"), 16)
        sp.dma_start(wmq[:], w_mq[0].rearrange("(c p) n -> p c n", p=P)).then_inc(S("w_mq_in"), 16)
        sp.dma_start(wmo[:], w_mo[0].rearrange("(c p) n -> p c n", p=P)).then_inc(S("w_mo_in"), 16)
        sp.dma_start(router_w[:], w_router[0].rearrange("(c p) n -> p c n", p=P)).then_inc(S("router_in"), 16)

        def load_w1(e, c):
            sp.dma_start(ring[:, c, :], w1_v[e, c]).then_inc(S(f"landed{c}"), 16)

        def load_w2(e, k):
            sp.dma_start(ring[:, W1_UNITS + k, :].rearrange("p (j n) -> p j n", j=2),
                         w2_v[e, k]).then_inc(S(f"landed{W1_UNITS + k}"), 16)

        w1_v = w_e1[0].rearrange("e (c p) n -> e c p n", p=P)
        w2_v = w_e2[0].rearrange("e (k j p) n -> e k p j n", p=P, j=2)
        sp.wait_ge(S("merged_out"), 1)
        for c in range(4):
            load_w1(0, c)
        for k in range(W2_UNITS):
            load_w2(0, k)
        sp.wait_ge(S("mem_queried"), 1)
        load_w1(0, 4)
        sp.wait_ge(S("mem_out"), 1)
        load_w1(0, 5)
        sp.wait_ge(S("routed"), 1)
        sp.dma_start(b1s[:], b_e1[0].rearrange("e (q n) -> (e q) n", q=4)).then_inc(S("b1_in"), 16)
        sp.dma_start(b2s[:], b_e2[0]).then_inc(S("b2_in"), 16)
        load_w1(0, 6)
        load_w1(0, 7)

        def w1_free(j, c):
            if c in SPLIT_W1:
                s = SPLIT_W1.index(c)
                sp.wait_ge(S("parts_made"), parts_of(j, s) if isinstance(j, int) else 8 * j - 3 + s)
            else:
                sp.wait_ge(S("w1_used"), j * WHOLE + [u for u in range(W1_UNITS) if u not in SPLIT_W1].index(c) + 1)

        for c in range(W1_UNITS):
            w1_free(0, c)
            load_w1(1, c)

        sp.wait_ge(S("more_known"), 1)
        n = sp.value_load(more_i[0:1, 0:1], min_val=0, max_val=STEPS - E) + E
        with sp.Fori(1, n - 1) as j:
            for c in range(W1_UNITS):
                w1_free(j, c)
                load_w1(bass.ds((j + 1) % E, 1), c)
            for k in range(W2_UNITS):
                sp.wait_ge(S("parts_made"), 8 * j + k + 1)
                load_w2(bass.ds(j % E, 1), k)
        for k in range(W2_UNITS):
            sp.wait_ge(S("parts_made"), 8 * (n - 1) + k + 1)
            load_w2(E - 1, k)
        for t in range(NT):
            sp.wait_ge(S("added"), 2 * (n - 1) + t + 1)
            sp.dma_start(out[0, t * P:(t + 1) * P, :], X[:, t, :]).then_inc(S("stored"), 16)
        sp.wait_ge(S("stored"), 16 * NT)

    @blk.gpsimd
    def _(pool):
        n = [0]

        def link(ins):
            n[0] += 1
            ins.then_inc(S("pool_chain"), 1)
            pool.wait_ge(S("pool_chain"), n[0])

        inv = rope[:, 7, 0, :]
        for i in range(16):
            f = float(np.float32(THETA) ** np.float32(-2 * i / 32))
            G.memset(inv[:, i:i + 1], f)
        G.memset(U[:], 1.0)
        G.memset(NBs[:, 0, :], 0.0)
        G.memset(mtmp[:, 3, :], 1.0)
        G.iota(mtmp_i[:, 0, 0:P], pattern=[[-1, P]], base=1024, channel_multiplier=1)
        G.iota(mtmp_i[:, 0, P:3 * P], pattern=[[-1, 2 * P]], base=1024 + P, channel_multiplier=1)
        link(G.memset(ident[:], 0.0))
        G.affine_select(out=ident[:], in_=ident[:], pattern=[[-1, P]], compare_op=ALU.not_equal, fill=1.0,
                        base=0, channel_multiplier=1)
        G.affine_select(out=NBs[:, 0, 0:P], in_=NBs[:, 0, 0:P], pattern=[[-1, P]], compare_op=ALU.is_ge,
                        fill=BIG, base=0, channel_multiplier=1)
        G.affine_select(out=NBs[:, 0, P:], in_=NBs[:, 0, P:], pattern=[[-1, 2 * P]], compare_op=ALU.is_ge,
                        fill=BIG, base=P, channel_multiplier=1)
        G.affine_select(out=mtmp[:, 3, P:], in_=mtmp[:, 3, P:], pattern=[[1, 2 * P]], compare_op=ALU.is_ge,
                        fill=0.0, base=0, channel_multiplier=-1)
        G.affine_select(out=U[:, 0, :], in_=U[:, 0, :], pattern=[[1, P]], compare_op=ALU.is_ge, fill=0.0,
                        base=0, channel_multiplier=-1)
        G.affine_select(out=U[:, 1, :], in_=U[:, 1, :], pattern=[[1, P]], compare_op=ALU.is_ge, fill=0.0,
                        base=-1, channel_multiplier=-1).then_inc(S("constants"), 1)

        def rotate(xv, cosv, sinv, a, b, width):
            half = width // 2
            G.tensor_tensor(a, xv, cosv, ALU.mult)
            link(G.tensor_tensor(b, xv, sinv, ALU.mult))
            G.tensor_tensor(xv[:, :, 0, :], a[:, :, 0, :], b[:, :, 1, :], ALU.subtract)
            return G.tensor_tensor(xv[:, :, 1, :], a[:, :, 1, :], b[:, :, 0, :], ALU.add)

        pool.wait_ge(S("rope_tables"), 1)
        pool.wait_ge(S("mla_normed"), 1)
        for w in range(2):
            for t in range(NT):
                xv = QKb[:, w, t, :, NOPE:].rearrange("p h (a r) -> p h a r", a=2)
                cosv, sinv = (rope[:, k, t, :].unsqueeze(1).unsqueeze(1).to_broadcast([P, MLA_H, 2, 16])
                              for k in (6, 4))
                a, b = (rtmp[:, k, (2 * w + t) % 2].rearrange("p h (a r) -> p h a r", a=2) for k in (0, 1))
                last = rotate(xv, cosv, sinv, a, b, 32)
                if (w, t) == (1, 1):
                    last.then_inc(S("mla_rotated"), 1)
                else:
                    link(last)
        pool.wait_ge(S("dil_normed"), 1)
        pool.wait_ge(S("mla_rotated"), 1)
        q0 = COL["qc"][0]
        for t in range(NT):
            xv = proj[:, t, q0:q0 + 768].rearrange("p (h d) -> p h d", d=HD)[:, :, 0:ROT] \
                .rearrange("p h (a r) -> p h a r", a=2)
            cosv, sinv = (rope[:, k, t, 0:16:2].unsqueeze(1).unsqueeze(1).to_broadcast([P, 12, 2, 8])
                          for k in (6, 4))
            a, b = (rtmp[:, k, t].rearrange("p h r -> p (h r)").rearrange("p (h a r) -> p h a r", a=2, r=8)
                    for k in (0, 1))
            last = rotate(xv, cosv, sinv, a, b, 16)
            if t == 1:
                last.then_inc(S("dil_rotated"), 1)
            else:
                link(last)

        pool.wait_ge(S("h_used"), 1)
        pool.wait_ge(S("h_turned"), 1)
        G.iota(iota[:], pattern=[[0, 2], [1, SLOTS]], base=0, channel_multiplier=0,
               allow_small_or_imprecise_dtypes=True)
        G.memset(slot_of[:], -5.0)
        G.memset(gate_of[:], 0.0)
        G.memset(xgf[:], 0.0)
        pool.wait_ge(S("routed"), 1)
        G.tensor_tensor(stack[:], ident[:, 0:SLOTS], ident[:, SLOTS:], ALU.add).then_inc(S("tables_clear"), 1)
        pool.wait_ge(S("tables_clear"), 1)
        pool.wait_ge(S("tables_made"), 1)

        def hot_for_gather(i):
            if not (isinstance(i, int) and i == 0):
                pool.wait_ge(S("gathered"), i)
            G.tensor_copy(pick[:, 0, :], slot_of[:, :, bass.ds(i, 1)].rearrange("p t a -> p (t a)"))
            pool.drain()
            for t in range(NT):
                ins = G.tensor_scalar(hotr[:, t, :], iota[:, 0:SLOTS], pick[:, 0, t:t + 1], None, ALU.is_equal)
            ins.then_inc(S("hot_made"), 1)

        def hot_for_scatter(i, first=False):
            if not first:
                pool.wait_ge(S("hot_turned"), i)
            G.tensor_copy(pick[:, 1, :], slot_of[:, :, bass.ds(i, 1)].rearrange("p t a -> p (t a)"))
            G.tensor_copy(pick[:, 2, :], gate_of[:, :, bass.ds(i, 1)].rearrange("p t a -> p (t a)"))
            pool.drain()
            for t in range(NT):
                ins = G.tensor_scalar(hotg[:, t, :], iota[:], pick[:, 1, t:t + 1], pick[:, 2, t:t + 1],
                                      ALU.is_equal, ALU.mult)
            ins.then_inc(S("hotg_made"), 1)

        hot_for_gather(0)
        hot_for_gather(1)
        hot_for_gather(2)
        hot_for_scatter(0, first=True)
        nn = pool.value_load(more_i[0:1, 0:1], min_val=0, max_val=STEPS - E) + E
        with pool.Fori(2, nn) as i:
            hot_for_gather(i + 1)
            hot_for_scatter(i - 1)
        hot_for_scatter(nn - 1)

    @blk.scalar
    def _(act):
        turned = Banks(0)
        roots = [0]
        n = [0]

        def link(ins):
            n[0] += 1
            ins.then_inc(S("act_chain"), 1)
            act.wait_ge(S("act_chain"), n[0])

        act.dma_start(pos_i[:], positions[0].rearrange("(t p) -> p t", p=P),
                      allow_slow_non_contiguous=True).then_inc(S("pos_in"), 16)
        act.dma_start(gain[:, 0, :], g_mem[0].partition_broadcast(P)).then_inc(S("g_mem_in"), 16)
        act.dma_start(gain[:, 1, :], g_mix[0].partition_broadcast(P)).then_inc(S("g_mix_in"), 16)
        for name, a in small_list:
            act.dma_start(SG[name], a[0].partition_broadcast(P)).then_inc(S("smalls_in"), 16)

        def leave(out_ap, k, cols, rows=P):
            src = turned.next()
            act.wait_ge(S("turned"), turned.n)
            A.copy(out_ap, src[0:rows, 0:cols] if k is None else
                   src[0:rows, 0:cols].rearrange("p (a b) -> p a b", a=k)).then_inc(S("turned_out"), 1)

        def root(cols):
            k = roots[0]
            roots[0] += 1
            act.wait_ge(S("var_ready"), k + 1)
            link(A.activation(cols_of(2, k), cols_of(1, k), ACT.Ln))
            A.activation(cols_of(2, k), cols_of(2, k), ACT.Exp, scale=-0.5).then_inc(S("root_ready"), 1)

        def whole_squares(src, k):
            for t in range(NT):
                ins = A.activation(SCR[:, 1024 * t:1024 * t + 1024], src[:, t, :], ACT.Square,
                                   accum_out=cols_of(0, k)[:, t:t + 1])
            ins.then_inc(S("squared"), 1)

        def turned_rows():
            for t in range(NT):
                for half in range(2):
                    leave(hT[:, 4 * half:4 * half + 4, t * P:(t + 1) * P], 4, 512)

        act.wait_ge(S("angles"), 1)
        A.activation(rope[:, 5], rope[:, 3], ACT.Sin, scale=0.5)
        A.activation(rope[:, 4], rope[:, 3], ACT.Sin).then_inc(S("sines"), 1)
        act.wait_ge(S("mem_in"), 16)
        whole_squares(memx, 0)
        root(2)
        act.wait_ge(S("x_in"), 16)
        whole_squares(X, 1)
        root(2)
        turned_rows()
        act.dma_start(gain[:, 0, :], g_group[0].partition_broadcast(P)).then_inc(S("g_group_in"), 16)
        act.wait_ge(S("mem_kv_ready"), 1)
        act.wait_ge(S("squared"), 2)
        A.activation(SCR[:, 0:512].rearrange("p (t n) -> p t n", t=2), KVm[:, :, 0:256],
                     ACT.Square).then_inc(S("squared"), 1)
        act.wait_ge(S("mem_projected"), 1)
        turned_rows()
        act.dma_start(gain[:, 1, :], g_xmem[0].partition_broadcast(P)).then_inc(S("g_xmem_in"), 16)
        root(8)
        leave(memT[:], 2, 512)
        act.wait_ge(S("latents_ready"), 1)
        act.wait_ge(S("squares_read"), 1)
        for t in range(NT):
            A.activation(SCR[:, 512 * t:512 * t + Q_RANK], proj[:, t, COL["cq"][0]:COL["cq"][1]], ACT.Square,
                         accum_out=cols_of(0, 3)[:, t:t + 1])
            ins = A.activation(SCR[:, 1024 + 512 * t:1024 + 512 * t + KV_RANK],
                               proj[:, t, COL["ckv"][0]:COL["ckv"][1]], ACT.Square,
                               accum_out=cols_of(0, 3)[:, 2 + t:3 + t])
        ins.then_inc(S("squared"), 1)
        root(4)
        act.wait_ge(S("mem_projected"), 1)
        for t in range(NT):
            leave(cqT[:, :, t * P:(t + 1) * P], 3, Q_RANK)
        leave(ckvT[:], 2, 512)
        act.wait_ge(S("fox_ready"), 1)
        act.wait_ge(S("squared"), 4)
        A.activation(SCR[:, 0:1024].rearrange("p (t n) -> p t n", t=2), proj[:, :, 0:512],
                     ACT.Square).then_inc(S("squared"), 1)
        root(16)
        act.wait_ge(S("forget_abs"), 1)
        link(A.activation(fe, fe, ACT.Exp, scale=-1.0))
        A.activation(fe, fe, ACT.Ln, bias=1.0).then_inc(S("forget_log"), 1)
        act.wait_ge(S("mla_ready"), 1)
        act.wait_ge(S("squares_read"), 2)
        A.activation(SCR[:, 0:2304], QKb[:].rearrange("p w t h d -> p (w t h d)"), ACT.Square) \
            .then_inc(S("squared"), 1)
        leave(foxT[:, 0], 2, 512)
        leave(foxT[:, 1], 2, 512)
        root(24)
        for w in range(2):
            for pair in range(3):
                if (w, pair) == (0, 0):
                    act.wait_ge(S("latents_projected"), 1)
                leave(mlaT[0:QK, w, 2 * pair:2 * pair + 2, :], 2, 512, QK)
        act.wait_ge(S("dil_ready"), 1)
        act.wait_ge(S("squares_read"), 3)
        A.activation(SCR[:, 0:1536].rearrange("p (t n) -> p t n", t=2),
                     proj[:, :, COL["qc"][0]:COL["kc"][1]], ACT.Square).then_inc(S("squared"), 1)
        root(24)
        for w in range(2):
            leave(dilT[:, w, 0:2, :], 2, 512)
            leave(dilT[:, w, 2, :], None, 256)

        scored = [0]

        def attend(units_, cols, mm_before):
            mm, at_value = mm_before, {}
            for what, u in order(len(units_)):
                if what != "turn":
                    mm += 1
                if what == "value":
                    at_value[u] = mm
            spans = [(0, cols - 256), (cols - 256, cols)]
            for s in range(len(units_) + 2):
                if 0 <= s - 2 < len(units_):
                    if s - 4 >= 0:
                        act.wait_ge(S("mm_done"), at_value[s - 4])
                    leave(PTb[:, s % 2, 0:cols], None, cols)
                if s < len(units_):
                    scored[0] += 1
                    act.wait_ge(S("scored"), scored[0])
                    if s >= 2:
                        act.wait_ge(S("turned"), turned.n)
                    for t, (a, b) in enumerate(spans):
                        c = 2 * (s % 2) + t
                        ins = A.activation(Pb[:, s % 2, a:b], Sb[:, s % 2, a:b], ACT.Exp,
                                           bias=rowmax[:, c:c + 1], accum_out=rowsum[:, 2 * (s % 4) + t:2 * (s % 4) + t + 1])
                    ins.then_inc(S("exped"), 1)

        act.wait_ge(S("fox_bias_made"), 1)
        attend(SELF, 384, MM_SELF)
        act.wait_ge(S("self_done"), 1)
        for t in range(NT):
            for k, (a, b) in enumerate(((0, 256), (256, 640), (640, 1024))):
                ins = A.activation(SCR[:, 1024 * t + a:1024 * t + b], H[:, t, a:b], ACT.Square,
                                   accum_out=cols_of(0, 7)[:, 2 * k + t:2 * k + t + 1])
        ins.then_inc(S("squared"), 1)
        root(6)
        turned_rows()
        act.dma_start(gain[:, 0, :], g_ffn[0].partition_broadcast(P)).then_inc(S("g_ffn_in"), 16)
        act.wait_ge(S("x1_ready"), 1)
        act.wait_ge(S("squared"), 8)
        whole_squares(X, 8)
        root(2)
        act.wait_ge(S("merged_out"), 1)
        turned_rows()
        act.wait_ge(S("mem_q_ready"), 1)
        act.wait_ge(S("squared"), 9)
        A.activation(SCR[:, 0:512].rearrange("p (t n) -> p t n", t=2), qm[:], ACT.Square) \
            .then_inc(S("squared"), 1)
        root(8)
        leave(qmT[:], 2, 512)
        attend(MEM, 512, MM_MEM)
        leave(omT[:], 2, 512)
        act.wait_ge(S("x2_ready"), 1)
        whole_squares(X, 10)
        root(2)
        turned_rows()
        act.wait_ge(S("h_ready"), 1)
        for t in range(NT):
            ins = A.copy(XR[:, 0, t, :], H[:, t, :])
        ins.then_inc(S("h_high"), 1)
        act.wait_ge(S("logits_ready"), 1)
        for t in range(NT):
            ins = A.activation(rt[:, 4, t, 0:E], rt[:, 0, t, 0:E], ACT.Exp, bias=rt[:, 2, t, 0:1])
        ins.then_inc(S("gates_exped"), 1)
        leave(rt_gateT[:], None, 256, E)
        leave(b1T[:].rearrange("p e (q k) -> p k (e q)", q=4), 4, 512)

        def high(slot, i, count, landed, first=False):
            act.wait_ge(S(f"landed{slot}"), landed)
            if not first:
                act.wait_ge(S("parts_used"), count - 2)
            b = i % 2
            A.copy(split[:, b, 0, :], ring[:, slot, :]).then_inc(S("high_made"), 1)

        def step(i, w1, w2, tail=0):
            first = isinstance(i, int) and i == 0

            def w1_high(s):
                cnt = s + 1 if first else 8 * i - 3 + s
                high(SPLIT_W1[s], s, cnt, 16 * (i + 1), first and s < 2)

            if w1:
                w1_high(0)
                w1_high(1)
            if w2:
                act.wait_ge(S("glu_ready"), i)
                A.activation(sig[:], glu[:], ACT.Sigmoid, scale=ALPHA).then_inc(S("sig_ready"), 1)
            if w1:
                w1_high(2)
                w1_high(3)
            if w2:
                for k in range(2):
                    high(W1_UNITS + k, k, 8 * i + k + 1 - tail, 16 * i)
            if w1:
                act.wait_ge(S("w1_used"), WHOLE * (i + 1))
                if not first:
                    act.wait_ge(S("hidden_turned"), i)
                A.copy(Hs[:, 0:1024], PS[:, 0:2, :].rearrange("p b n -> p (b n)")).then_inc(S("hidden_out"), 1)
            if w2:
                for k in range(2, 4):
                    high(W1_UNITS + k, k, 8 * i + k + 1 - tail, 16 * i)
                act.wait_ge(S("parts_used"), 8 * i + 4 - tail)
                if not (isinstance(i, int) and i == 1):
                    act.wait_ge(S("scattered"), 2 * (i - 1))
                A.copy(Ys[:], PS[:, 6:8, :].rearrange("p b n -> p (b n)")).then_inc(S("y_out"), 1)
                act.wait_ge(S("hot_turned"), i)
                A.copy(hotT[:], PS[:, 0, 0:T]).then_inc(S("hotT_out"), 1)

        step(0, True, False)
        step(1, True, True)
        nn = act.value_load(more_i[0:1, 0:1], min_val=0, max_val=STEPS - E) + E
        with act.Fori(2, nn) as i:
            step(i, True, True)
        step(nn, False, True, tail=4)

    @blk.vector
    def _(dve):
        product = Banks(4)
        chain = [0]
        req = [0, 0]

        def link(ins):
            chain[0] += 1
            ins.then_inc(S("dve_chain"), 1)
            dve.wait_ge(S("dve_chain"), chain[0])

        def take():
            bank = product.next()
            dve.wait_ge(S("mm_done"), product.n)
            return bank

        def leave(out_ap, in_ap):
            V.tensor_copy(out_ap, in_ap).then_inc(S("mm_out"), 1)

        def after_leaving():
            dve.wait_ge(S("mm_out"), product.n)

        def variance(parts):
            k = req[0]
            req[0] += 1
            for n, (a, b, count) in enumerate(parts):
                ins = V.tensor_scalar(cols_of(1, k)[:, a:b], cols_of(0, k)[:, a:b], 1.0 / count, EPS,
                                      ALU.mult, ALU.add)
            ins.then_inc(S("var_ready"), 1)

        def newton():
            k = req[1]
            req[1] += 1
            y, v, w = cols_of(2, k), cols_of(1, k), cols_of(3, k)
            dve.wait_ge(S("root_ready"), k + 1)
            link(V.tensor_tensor(w, y, y, ALU.mult))
            link(V.tensor_tensor(w, w, v, ALU.mult))
            link(V.tensor_scalar(w, w, -0.5, 1.5, ALU.mult, ALU.add))
            link(V.tensor_tensor(y, y, w, ALU.mult))
            return y

        def norm_rows(src, y, g, sem):
            for t in range(NT):
                ins = V.scalar_tensor_tensor(out=H[:, t, :], in0=src[:, t, :], scalar=y[:, t:t + 1],
                                             in1=gain[:, g, :], op0=ALU.mult, op1=ALU.mult)
            ins.then_inc(S(sem), 1)

        ang, ki, kf, r = rope[:, 0], rope_i[:, 1], rope[:, 2], rope[:, 3]
        dve.wait_ge(S("pos_in"), 16)
        dve.wait_ge(S("constants"), 1)
        link(V.tensor_copy(kf[:, :, 0], pos_i[:]))
        link(V.tensor_tensor(ang, kf[:, :, 0:1].to_broadcast([P, NT, 16]),
                             rope[:, 7, 0:1, :].to_broadcast([P, NT, 16]), ALU.mult))
        link(V.tensor_scalar(kf, ang, 1.0 / (2 * math.pi), None, ALU.mult))
        link(V.tensor_copy(ki, kf))
        link(V.tensor_copy(kf, ki))
        c1 = 6.28125
        c2 = float(np.float32(np.floor((2 * math.pi - c1) * 2 ** 20) / 2 ** 20))
        c3 = 2 * math.pi - c1 - c2
        link(V.scalar_tensor_tensor(out=r, in0=kf, scalar=-c1, in1=ang, op0=ALU.mult, op1=ALU.add))
        link(V.scalar_tensor_tensor(out=r, in0=kf, scalar=-c2, in1=r, op0=ALU.mult, op1=ALU.add))
        link(V.scalar_tensor_tensor(out=r, in0=kf, scalar=-c3, in1=r, op0=ALU.mult, op1=ALU.add))
        V.tensor_scalar(r, r, 3.1415925, -3.1415925, ALU.min, ALU.max).then_inc(S("angles"), 1)
        V.tensor_scalar(mtmp_i[:, 1, :], mtmp_i[:, 0, :], 3, None, ALU.bitwise_and)
        link(V.tensor_scalar(mtmp_i[:, 2, :], mtmp_i[:, 0, :], 15, None, ALU.bitwise_and))
        V.tensor_scalar(mtmp[:, 4, :], mtmp_i[:, 1, :], 0.0, None, ALU.is_equal)
        link(V.tensor_scalar(mtmp[:, 5, :], mtmp_i[:, 2, :], 0.0, None, ALU.is_equal))
        link(V.tensor_tensor(mtmp[:, 3, :], mtmp[:, 3, :], mtmp[:, 4, :], ALU.add))
        link(V.tensor_tensor(mtmp[:, 3, :], mtmp[:, 3, :], mtmp[:, 5, :], ALU.add))
        V.tensor_scalar(mtmp[:, 4, :], mtmp[:, 3, :], 0.0, BIG, ALU.is_equal, ALU.mult)
        V.tensor_scalar(mtmp[:, 5, :], mtmp[:, 3, :], 2.0, -math.log(2), ALU.is_equal, ALU.mult)
        link(V.tensor_scalar(mtmp[:, 6, :], mtmp[:, 3, :], 3.0, -math.log(3), ALU.is_equal, ALU.mult))
        link(V.tensor_tensor(mtmp[:, 4, :], mtmp[:, 4, :], mtmp[:, 5, :], ALU.add))
        link(V.tensor_tensor(mtmp[:, 4, :], mtmp[:, 4, :], mtmp[:, 6, :], ALU.add))
        link(V.tensor_tensor(NBs[:, 1, :], NBs[:, 0, :], mtmp[:, 4, :], ALU.add))
        dve.wait_ge(S("sines"), 1)
        link(V.tensor_tensor(rope[:, 6], rope[:, 5], rope[:, 5], ALU.mult))
        V.tensor_scalar(rope[:, 6], rope[:, 6], -2.0, 1.0, ALU.mult, ALU.add).then_inc(S("rope_tables"), 1)

        dve.wait_ge(S("squared"), 1)
        variance([(0, 2, D)])
        dve.wait_ge(S("squared"), 2)
        variance([(0, 2, D)])
        y = newton()
        dve.wait_ge(S("g_mem_in"), 16)
        norm_rows(memx, y, 0, "rows_ready")
        y = newton()
        dve.wait_ge(S("turned"), 4)
        dve.wait_ge(S("g_mix_in"), 16)
        norm_rows(X, y, 1, "rows_ready")
        dve.wait_ge(S("smalls_in"), 16 * len(small_list))
        for t in range(NT):
            leave(KVm[:, t, :], take())
        after_leaving()
        dve.sem_inc(S("mem_kv_ready"), 1)

        def head_sums(k, src, out_ap, squared):
            dve.wait_ge(S("squared"), squared)
            V.tensor_reduce(out_ap, src, AX.X, ALU.add).then_inc(S("squares_read"), 1)
            head_sums.n += 1
            dve.wait_ge(S("squares_read"), head_sums.n)
        head_sums.n = 0

        def scale_heads(ap, y, h, d):
            link(V.tensor_tensor(ap, ap, y.rearrange("p (t h) -> p t h", t=NT).unsqueeze(3)
                                 .to_broadcast([P, NT, h, d]), ALU.mult))

        def gain_heads(ap, g, h, d):
            return V.tensor_tensor(ap, ap, g.unsqueeze(1).unsqueeze(1).to_broadcast([P, NT, h, d]), ALU.mult)

        def project(n):
            a, b, _ = CHUNKS[n]
            for t in range(NT):
                leave(proj[:, t, a:b], take()[:, 0:b - a])

        head_sums(2, SCR[:, 0:512].rearrange("p (t h d) -> p t h d", t=NT, h=MEM_H),
                  cols_of(0, 2).rearrange("p (t h) -> p t h", t=NT), 3)
        variance([(0, 8, HD)])
        dve.wait_ge(S("rows_ready"), 2)
        project(0)
        project(1)
        after_leaving()
        dve.sem_inc(S("latents_ready"), 1)
        y = newton()
        kv = heads(KVm[:, :, 0:256], MEM_H)
        scale_heads(kv, y, MEM_H, HD)
        gain_heads(kv, SG["g_km"], MEM_H, HD).then_inc(S("mem_keys_normed"), 1)
        dve.wait_ge(S("squared"), 4)
        variance([(0, 2, Q_RANK), (2, 4, KV_RANK)])
        project(2)
        after_leaving()
        dve.sem_inc(S("fox_ready"), 1)
        y = newton()
        for t in range(NT):
            for k, name, w in ((0, "cq", Q_RANK), (2, "ckv", KV_RANK)):
                ap = proj[:, t, COL[name][0]:COL[name][1]]
                ins = V.scalar_tensor_tensor(out=ap, in0=ap, scalar=y[:, k + t:k + t + 1], in1=SG["g_" + name],
                                             op0=ALU.mult, op1=ALU.mult)
        ins.then_inc(S("latents_normed"), 1)
        head_sums(4, SCR[:, 0:1024].rearrange("p (t h d) -> p t h d", t=NT, h=8),
                  cols_of(0, 4).rearrange("p (t h) -> p t h", t=NT), 5)
        variance([(0, 16, HD)])
        project(3)
        after_leaving()
        link(V.tensor_tensor(fz, proj[:, :, COL["fa"][0]:COL["fa"][1]],
                             SG["b_forget"].unsqueeze(1).to_broadcast([P, NT, FOX_H]), ALU.add))
        link(V.tensor_scalar(fa2, fz, -1.0, None, ALU.mult))
        V.tensor_tensor(fe, fz, fa2, ALU.max).then_inc(S("forget_abs"), 1)
        y = newton()
        fox = heads(proj[:, :, 0:512], 8)
        scale_heads(fox, y, 8, HD)
        gain_heads(fox[:, :, 0:4], SG["g_qa"], 4, HD)
        gain_heads(fox[:, :, 4:8], SG["g_ka"], 4, HD).then_inc(S("fox_normed"), 1)
        link(V.tensor_scalar(fz, fz, 0.0, None, ALU.min))
        dve.wait_ge(S("forget_log"), 1)
        V.tensor_tensor(logf, fz, fe, ALU.subtract).then_inc(S("logf_ready"), 1)
        for t in range(NT):
            for half in range(2):
                leave(QKb[:, 0, t, 3 * half:3 * half + 3, :], take()[:, 0:3 * QK].rearrange("p (h d) -> p h d", d=QK))
        for t in range(NT):
            for half in range(2):
                b = take()[:, 0:384].rearrange("p (h d) -> p h d", d=128)
                V.tensor_copy(QKb[:, 1, t, 3 * half:3 * half + 3, 0:NOPE], b[:, :, 0:NOPE])
                leave(Vb[:, t, 3 * half:3 * half + 3, :], b[:, :, NOPE:])
        V.tensor_copy(QKb[:, 1, :, :, NOPE:], proj[:, :, COL["kr"][0]:COL["kr"][1]].unsqueeze(2)
                      .to_broadcast([P, NT, MLA_H, ROPE])).then_inc(S("mla_ready"), 1)
        head_sums(5, SCR[:, 0:2304].rearrange("p (w h d) -> p w h d", w=2, d=QK),
                  cols_of(0, 5).rearrange("p (w h) -> p w h", w=2), 6)
        variance([(0, 24, QK)])
        project(4)
        y = newton()
        for w, g in ((0, "g_qb"), (1, "g_kb")):
            ap = QKb[:, w]
            link(V.tensor_tensor(ap, ap, y[:, 12 * w:12 * w + 12].rearrange("p (t h) -> p t h", t=NT).unsqueeze(3)
                                 .to_broadcast([P, NT, MLA_H, QK]), ALU.mult))
            ins = gain_heads(ap, SG[g], MLA_H, QK)
        ins.then_inc(S("mla_normed"), 1)
        project(5)
        after_leaving()
        dve.sem_inc(S("dil_ready"), 1)
        dve.wait_ge(S("logf_ready"), 1)
        dve.wait_ge(S("squares_read"), 3)
        head_sums(6, SCR[:, 0:1536].rearrange("p (t h d) -> p t h d", t=NT, h=12),
                  cols_of(0, 6).rearrange("p (t h) -> p t h", t=NT), 7)
        variance([(0, 24, HD)])
        V.tensor_copy(logfb, logf.unsqueeze(3).to_broadcast([P, NT, FOX_H, P])).then_inc(S("logf_wide"), 1)
        project(6)
        leave(cumq, take()[:, 0:8].rearrange("p (t h) -> p t h", t=NT))
        after_leaving()
        y = newton()
        dil = heads(proj[:, :, COL["qc"][0]:COL["kc"][1]], 12)
        scale_heads(dil, y, 12, HD)
        gain_heads(dil[:, :, 0:6], SG["g_qc"], 6, HD)
        gain_heads(dil[:, :, 6:12], SG["g_kc"], 6, HD).then_inc(S("dil_normed"), 1)
        for h in range(FOX_H):
            b = take()
            V.scalar_tensor_tensor(out=foxNB[:, h, 0:P], in0=b[:, 0:P], scalar=cumq[:, 0, h:h + 1],
                                   in1=NBs[:, 0, 0:P], op0=ALU.subtract, op1=ALU.add)
            V.scalar_tensor_tensor(out=foxNB[:, h, P:], in0=b[:, 0:2 * P], scalar=cumq[:, 1, h:h + 1],
                                   in1=NBs[:, 0, P:], op0=ALU.subtract, op1=ALU.add).then_inc(S("mm_out"), 1)
        after_leaving()
        dve.sem_inc(S("fox_bias_made"), 1)

        scored = [0]

        def attend(units_, cols):
            first = scored[0]
            spans = [(0, cols - 256), (cols - 256, cols)]
            for what, u in order(len(units_)):
                q, k, v, nb, scale, o_ap = units_[u]
                c = 2 * (u % 2)
                if what == "score":
                    b = take()
                    if first + u >= 2:
                        dve.wait_ge(S("exped"), first + u - 1)
                    if nb is None:
                        V.tensor_scalar(Sb[:, u % 2, 0:cols], b[:, 0:cols], scale, None,
                                        ALU.mult).then_inc(S("mm_out"), 1)
                    else:
                        V.scalar_tensor_tensor(out=Sb[:, u % 2, 0:cols], in0=b[:, 0:cols], scalar=scale, in1=nb,
                                               op0=ALU.mult, op1=ALU.subtract).then_inc(S("mm_out"), 1)
                    after_leaving()
                    for t, (a, e) in enumerate(spans):
                        ins = V.tensor_reduce(rowtmp[:, c + t:c + t + 1], Sb[:, u % 2, a:e], AX.X, ALU.max)
                    link(ins)
                    V.tensor_scalar(rowmax[:, c:c + 2], rowtmp[:, c:c + 2], -1.0, None,
                                    ALU.mult).then_inc(S("scored"), 1)
                    scored[0] += 1
                if what == "value":
                    b = take()
                    link(V.reciprocal(rowinv[:, c:c + 2], rowsum[:, 2 * (u % 4):2 * (u % 4) + 2]))
                    V.tensor_tensor(o_ap, b[:, 0:2 * HD].rearrange("p (t d) -> p t d", t=NT),
                                    rowinv[:, c:c + 2].unsqueeze(2).to_broadcast([P, NT, HD]),
                                    ALU.mult).then_inc(S("mm_out"), 1)
            after_leaving()

        dve.wait_ge(S("turned"), 8)
        attend(SELF, 384)
        dve.sem_inc(S("self_done"), 1)
        dve.wait_ge(S("squared"), 8)
        variance([(0, 2, 256), (2, 4, 384), (4, 6, 384)])
        y = newton()
        dve.wait_ge(S("g_group_in"), 16)
        for t in range(NT):
            for k, (a, e) in enumerate(((0, 256), (256, 640), (640, 1024))):
                ins = V.scalar_tensor_tensor(out=H[:, t, a:e], in0=H[:, t, a:e], scalar=y[:, 2 * k + t:2 * k + t + 1],
                                             in1=gain[:, 0, a:e], op0=ALU.mult, op1=ALU.mult)
        ins.then_inc(S("rows_ready"), 1)

        def add_rows(sem):
            for t in range(NT):
                for half in range(2):
                    b = take()
                    ap = X[:, t, 512 * half:512 * half + 512]
                    V.tensor_tensor(ap, ap, b, ALU.add).then_inc(S("mm_out"), 1)
            after_leaving()
            dve.sem_inc(S(sem), 1)

        add_rows("x1_ready")
        dve.wait_ge(S("squared"), 9)
        variance([(0, 2, D)])
        y = newton()
        dve.wait_ge(S("g_xmem_in"), 16)
        dve.wait_ge(S("merged_out"), 1)
        norm_rows(X, y, 1, "rows_ready")
        for t in range(NT):
            leave(qm[:, t, :], take()[:, 0:256])
        after_leaving()
        dve.sem_inc(S("mem_q_ready"), 1)
        head_sums(9, SCR[:, 0:512].rearrange("p (t h d) -> p t h d", t=NT, h=MEM_H),
                  cols_of(0, 9).rearrange("p (t h) -> p t h", t=NT), 10)
        variance([(0, 8, HD)])
        y = newton()
        q4 = heads(qm[:], MEM_H)
        scale_heads(q4, y, MEM_H, HD)
        gain_heads(q4, SG["g_qm"], MEM_H, HD).then_inc(S("mem_q_normed"), 1)
        attend(MEM, 512)
        dve.sem_inc(S("mem_attended"), 1)
        add_rows("x2_ready")
        dve.wait_ge(S("squared"), 11)
        variance([(0, 2, D)])
        y = newton()
        dve.wait_ge(S("g_ffn_in"), 16)
        norm_rows(X, y, 0, "h_ready")
        dve.wait_ge(S("h_high"), 1)
        for t in range(NT):
            ins = V.tensor_tensor(XR[:, 1, t, :], H[:, t, :], XR[:, 0, t, :].bitcast(F32), ALU.subtract)
        ins.then_inc(S("h_used"), 1)

        L, top, rep, ex, mask, gate, rank = rt[:, 0], rt[:, 1], rt[:, 3], rt[:, 4], rt[:, 5], rt[:, 6], rt[:, 7]
        for t in range(NT):
            V.tensor_tensor(L[:, t, 0:E], take()[:, 0:E], SG["b_router"], ALU.add).then_inc(S("mm_out"), 1)
        link(V.memset(L[:, :, E:], 3e38))
        for t in range(NT):
            ins = V.max(out=top[:, t, 0:8], in_=L[:, t, :])
        link(ins)
        for t in range(NT):
            V.match_replace(out=rep[:, t, :], in_to_replace=top[:, t, 0:8], in_values=L[:, t, :], imm_value=-3e38)
        V.tensor_scalar(rt[:, 2, :, 0:1], top[:, :, 4:5], -1.0, None, ALU.mult).then_inc(S("logits_ready"), 1)
        dve.wait_ge(S("logits_ready"), 1)
        V.tensor_tensor(mask[:, :, 0:E], L[:, :, 0:E], rep[:, :, 0:E], ALU.not_equal).then_inc(S("mask_ready"), 1)
        dve.wait_ge(S("mask_ready"), 1)
        dve.wait_ge(S("gates_exped"), 1)
        link(V.tensor_tensor(ex[:, :, 0:E], ex[:, :, 0:E], mask[:, :, 0:E], ALU.mult))
        link(V.tensor_reduce(rt[:, 2, :, 8], ex[:, :, 0:E], AX.X, ALU.add))
        link(V.reciprocal(rt[:, 2, :, 9], rt[:, 2, :, 8]))
        V.tensor_tensor(gate[:, :, 0:E], ex[:, :, 0:E], rt[:, 2, :, 9:10].to_broadcast([P, NT, E]),
                        ALU.mult).then_inc(S("gate_ready"), 1)
        b = take()
        link(V.scalar_tensor_tensor(out=rank[:, :, 0:E], in0=b[:, 0:2 * E].rearrange("p (t e) -> p t e", t=NT),
                                    scalar=1.0, in1=mask[:, :, 0:E], op0=ALU.add, op1=ALU.mult))
        most = rt[:, 2, 0, 12:20]
        link(V.tensor_reduce(most[:, 0:1], b[:, 2 * E:3 * E], AX.X, ALU.max))
        for r in range(1, MAX_ROUNDS):
            ins = V.tensor_scalar(most[:, r:r + 1], most[:, 0:1], SLOTS * r + 0.5, float(E), ALU.is_gt, ALU.mult)
        link(ins)
        link(V.tensor_tensor(most[:, 4:5], most[:, 1:2], most[:, 2:3], ALU.add))
        V.tensor_tensor(more_i[:], most[:, 4:5], most[:, 3:4], ALU.add).then_inc(S("more_known"), 1)
        dve.wait_ge(S("tables_clear"), 1)
        dve.wait_ge(S("gate_ready"), 1)
        for r in range(MAX_ROUNDS):
            V.tensor_scalar(slot_of[:, :, E * r:E * r + E], rank[:, :, 0:E], -1.0 - SLOTS * r, None, ALU.add)
            ins = V.tensor_copy(gate_of[:, :, E * r:E * r + E], gate[:, :, 0:E])
        ins.then_inc(S("tables_made"), 1)
        dve.wait_ge(S("more_known"), 1)
        dve.sem_inc(S("mm_out"), 1)
        add_rows("b2_added")

        def low(b, count):
            dve.wait_ge(S("high_made"), count)
            return b, count

        def make_low(slot, b, count):
            low(b, count)
            V.tensor_tensor(split[:, b, 1, :], ring[:, slot, :], split[:, b, 0, :].bitcast(F32),
                            ALU.subtract).then_inc(S("parts_made"), 1)

        def gathered_out(i):
            dve.wait_ge(S("gathered"), i + 1)
            V.tensor_copy(xgr[:].rearrange("p c w s -> p (c w s)"),
                          PS[:, 4:6, :].rearrange("p b n -> p (b n)")).then_inc(S("xg_parts_out"), 1)
            dve.wait_ge(S("xg_parts_out"), i + 1)
            V.tensor_tensor(xgf[:, :, 0, :], xgr[:, :, 0, :].bitcast(F32), xgr[:, :, 1, :].bitcast(F32),
                            ALU.add).then_inc(S("xg_ready"), 1)

        def glu_sum(j):
            e = j % E
            n = j + 1
            bias = [b1T[:, bass.ds(e, 1), par:16:2].rearrange("p a c -> p (a c)").unsqueeze(2)
                    .to_broadcast([P, KC, SLOTS]) for par in range(2)]
            turned = [PS[:, 4 + par, :].rearrange("p (c s) -> p c s", c=KC) for par in range(2)]
            dve.wait_ge(S("hidden_turned"), n)
            V.tensor_tensor(glu[:], turned[0], bias[0], ALU.add).then_inc(S("glu_summed"), 1)
            V.tensor_tensor(lin[:], turned[1], bias[1], ALU.add).then_inc(S("lin_summed"), 1)
            dve.wait_ge(S("glu_summed"), n)
            V.tensor_scalar(glu[:], glu[:], LIMIT, None, ALU.min).then_inc(S("glu_ready"), 1)
            dve.wait_ge(S("lin_summed"), n)
            V.tensor_scalar(lin[:], lin[:], LIMIT, -LIMIT, ALU.min, ALU.max).then_inc(S("lin_ready"), 1)
            dve.wait_ge(S("lin_ready"), n)
            V.scalar_tensor_tensor(out=act_f[:], in0=lin[:], scalar=1.0, in1=glu[:], op0=ALU.add,
                                   op1=ALU.mult).then_inc(S("glu_lin_ready"), 1)

        def activate(j):
            n = j + 1
            dve.wait_ge(S("sig_ready"), n)
            dve.wait_ge(S("glu_lin_ready"), n)
            V.tensor_tensor(act_f[:], act_f[:], sig[:], ALU.mult).then_inc(S("act_full_ready"), 1)
            dve.wait_ge(S("act_full_ready"), n)
            V.tensor_copy(actr[:, :, 0, :], act_f[:]).then_inc(S("act_high_ready"), 1)
            dve.wait_ge(S("act_high_ready"), n)
            V.tensor_tensor(actr[:, :, 1, :], act_f[:], actr[:, :, 0, :].bitcast(F32),
                            ALU.subtract).then_inc(S("act_ready"), 1)

        def add(j, t):
            dve.wait_ge(S("scattered"), 2 * j + t + 1)
            V.tensor_tensor(X[:, t, :], X[:, t, :], PS[:, 6:8, :].rearrange("p b n -> p (b n)"),
                            ALU.add).then_inc(S("added"), 1)

        def step(i, w1, w2, scat, tail=0):
            first = isinstance(i, int) and i == 0

            def w1_low(s):
                make_low(SPLIT_W1[s], s % 2, s + 1 if first else 8 * i - 3 + s)

            if w1:
                w1_low(0)
            if w2:
                glu_sum(i - 1)
            if w1:
                w1_low(1)
            if w2:
                activate(i - 1)
            if scat:
                add(i - 2, 0)
            if w1:
                w1_low(2)
            if scat:
                add(i - 2, 1)
            if w1:
                w1_low(3)
            if w2:
                for k in range(2):
                    make_low(W1_UNITS + k, k, 8 * i + k + 1 - tail)
            if w1:
                dve.wait_ge(S("w1_used"), WHOLE * (i + 1))
                if not first:
                    dve.wait_ge(S("hidden_turned"), i)
                V.tensor_copy(Hs[:, 1024:], PS[:, 2:4, :].rearrange("p b n -> p (b n)")) \
                    .then_inc(S("hidden_out"), 1)
                gathered_out(i + 1)
            if w2:
                for k in range(2, 4):
                    make_low(W1_UNITS + k, k % 2, 8 * i + k + 1 - tail)

        dve.wait_ge(S("tables_clear"), 1)
        gathered_out(0)
        step(0, True, False, False)
        step(1, True, True, False)
        nn = dve.value_load(more_i[0:1, 0:1], min_val=0, max_val=STEPS - E) + E
        with dve.Fori(2, nn) as i:
            step(i, True, True, True)
        step(nn, False, True, True, tail=4)
        add(nn - 1, 0)
        add(nn - 1, 1)

    @blk.tensor
    def _(pe):
        product, turn = Banks(4), Banks(0)

        def into():
            bank = product.next()
            if product.n > 4:
                pe.wait_ge(S("mm_out"), product.n - 4)
            return bank

        def turn_into():
            bank = turn.next()
            if turn.n > 4:
                pe.wait_ge(S("turned_out"), turn.n - 4)
            return bank

        def turn_blocks(blocks, rows=P):
            bank = turn_into()
            for k, src in enumerate(blocks):
                ins = TE.transpose(bank[0:rows, P * k:P * k + P], src, ident[:])
            ins.then_inc(S("turned"), 1)

        def turn_rows(src):
            for t in range(NT):
                for half in range(2):
                    turn_blocks([src[:, t, P * c:P * c + P] for c in range(4 * half, 4 * half + 4)])

        def multiply(lhs, rhs, n, out_cols=None):
            bank = into()
            for c in range(n):
                l, r = lhs(c), rhs(c)
                ins = TE.matmul(bank[:, 0:r.shape[-1]], l, r, start=(c == 0), stop=(c == n - 1))
            ins.then_inc(S("mm_done"), 1)

        def rows(t):
            return lambda c: hT[:, c, t * P:(t + 1) * P]

        def signal(sem):
            pe.wait_ge(S("mm_done"), product.n)
            pe.sem_inc(S(sem), 1)

        pe.wait_ge(S("constants"), 1)
        pe.wait_ge(S("rows_ready"), 1)
        turn_rows(H)
        pe.wait_ge(S("turned_out"), 4)
        pe.wait_ge(S("w_mkv_in"), 16)
        for t in range(NT):
            multiply(rows(t), lambda c: wmkv[:, c, :], KC)
        signal("mem_projected")
        pe.wait_ge(S("rows_ready"), 2)
        turn_rows(H)
        pe.wait_ge(S("turned_out"), 8)

        def project(n):
            pe.wait_ge(S(f"w_in{n}_in"), 16)
            for t in range(NT):
                multiply(rows(t), lambda c: win[n][:, c, :], KC)

        project(0)
        project(1)
        pe.wait_ge(S("mem_keys_normed"), 1)
        turn_blocks([KVm[:, t, P * j:P * j + P] for j in range(2) for t in range(NT)])
        project(2)
        pe.wait_ge(S("latents_normed"), 1)
        cq0, ckv0 = COL["cq"][0], COL["ckv"][0]
        for t in range(NT):
            turn_blocks([proj[:, t, cq0 + P * c:cq0 + P * c + P] for c in range(3)])
        turn_blocks([proj[:, t, ckv0 + P * c:ckv0 + P * c + P] for c in range(2) for t in range(NT)])
        project(3)
        pe.wait_ge(S("turned_out"), turn.n)
        pe.wait_ge(S("w_uq_in"), 16)
        for t in range(NT):
            for half in range(2):
                multiply(lambda c: cqT[:, c, t * P:(t + 1) * P],
                         lambda c: wuq[:, c, 288 * half:288 * half + 288], 3)
        pe.wait_ge(S("w_ukv_in"), 16)
        for t in range(NT):
            for half in range(2):
                multiply(lambda c: ckvT[:, c, t * P:(t + 1) * P],
                         lambda c: wukv[:, c, 384 * half:384 * half + 384], 2)
        signal("latents_projected")
        project(4)
        pe.wait_ge(S("fox_normed"), 1)
        for w in range(2):
            turn_blocks([proj[:, t, 256 * w + P * j:256 * w + P * j + P] for j in range(2) for t in range(NT)])
        project(5)
        pe.wait_ge(S("mla_rotated"), 1)
        for w in range(2):
            for pair in range(3):
                turn_blocks([QKb[:, w, t, h, :] for h in (2 * pair, 2 * pair + 1) for t in range(NT)], QK)
        project(6)
        signal("projected")
        pe.wait_ge(S("logf_wide"), 1)
        bank = into()
        TE.matmul(bank[:, 0:4], U[:, 0, :], logf[:, 0, :], start=True, stop=True)
        TE.matmul(bank[:, 4:8], U[:, 2, :], logf[:, 0, :], start=True, stop=False)
        TE.matmul(bank[:, 4:8], U[:, 0, :], logf[:, 1, :], start=False, stop=True).then_inc(S("mm_done"), 1)
        for h in range(FOX_H):
            bank = into()
            TE.matmul(bank[:, 0:P], logfb[:, 0, h, :], U[:, 0, :], start=True, stop=True)
            TE.matmul(bank[:, P:2 * P], logfb[:, 0, h, :], U[:, 2, :], start=True, stop=False)
            TE.matmul(bank[:, P:2 * P], logfb[:, 1, h, :], U[:, 0, :], start=False,
                      stop=True).then_inc(S("mm_done"), 1)
        pe.wait_ge(S("dil_rotated"), 1)
        q0 = COL["qc"][0]
        for w in range(2):
            turn_blocks([proj[:, t, q0 + 384 * w + P * j:q0 + 384 * w + P * j + P] for j in range(2)
                         for t in range(NT)])
            turn_blocks([proj[:, t, q0 + 384 * w + 2 * P:q0 + 384 * w + 3 * P] for t in range(NT)])
        pe.wait_ge(S("turned_out"), turn.n)

        exped = [0]

        def attend(units_, cols):
            first = exped[0]
            turned_at = {}
            full = cols == 512
            for what, u in order(len(units_)):
                q, k, v, nb, scale, o_ap = units_[u]
                if what == "score":
                    bank = into()
                    TE.matmul(bank[:, 0:cols - 256], q[:, 0:P], k[:, 0:cols - 256], start=True, stop=True)
                    TE.matmul(bank[:, cols - 256:cols], q[:, P:2 * P], k[:, 0:256], start=True,
                              stop=True).then_inc(S("mm_done"), 1)
                if what == "turn":
                    pe.wait_ge(S("exped"), first + u + 1)
                    turn_blocks([Pb[:, u % 2, a:a + P] for a in range(0, cols, P)])
                    turned_at[u] = turn.n
                if what == "value":
                    pe.wait_ge(S("turned_out"), turned_at[u])
                    bank = into()
                    n0 = 2 if full else 1
                    for t, n_, at_ in ((0, n0, 0), (1, 2, n0)):
                        for c in range(n_):
                            a = P * (at_ + c)
                            ins = TE.matmul(bank[:, HD * t:HD * t + HD], PTb[:, u % 2, a:a + P], v[c],
                                            start=(c == 0), stop=(c == n_ - 1))
                    ins.then_inc(S("mm_done"), 1)
            exped[0] += len(units_)

        assert product.n == MM_SELF
        attend(SELF, 384)
        pe.wait_ge(S("rows_ready"), 3)
        turn_rows(H)
        pe.wait_ge(S("turned_out"), turn.n)
        pe.wait_ge(S("w_out_in"), 16)
        for t in range(NT):
            for half in range(2):
                multiply(rows(t), lambda c: wout[:, c, 512 * half:512 * half + 512], KC)
        signal("merged_out")
        pe.wait_ge(S("rows_ready"), 4)
        turn_rows(H)
        pe.wait_ge(S("turned_out"), turn.n)
        pe.wait_ge(S("w_mq_in"), 16)
        for t in range(NT):
            multiply(rows(t), lambda c: wmq[:, c, :], KC)
        signal("mem_queried")
        pe.wait_ge(S("mem_q_normed"), 1)
        turn_blocks([qm[:, t, P * j:P * j + P] for j in range(2) for t in range(NT)])
        pe.wait_ge(S("turned_out"), turn.n)
        assert product.n == MM_MEM
        attend(MEM, 512)
        pe.wait_ge(S("mem_attended"), 1)
        turn_blocks([om[:, t, P * j:P * j + P] for j in range(2) for t in range(NT)])
        pe.wait_ge(S("turned_out"), turn.n)
        pe.wait_ge(S("w_mo_in"), 16)
        for t in range(NT):
            for half in range(2):
                multiply(lambda c: omT[:, c, t * P:(t + 1) * P],
                         lambda c: wmo[:, c, 512 * half:512 * half + 512], 2)
        signal("mem_out")
        pe.wait_ge(S("h_ready"), 1)
        turn_rows(H)
        pe.wait_ge(S("turned_out"), turn.n)
        pe.sem_inc(S("h_turned"), 1)
        pe.wait_ge(S("router_in"), 16)
        for t in range(NT):
            multiply(rows(t), lambda c: router_w[:, c, :], KC)
        signal("routed")
        pe.wait_ge(S("mask_ready"), 1)
        mask = rt[:, 5]
        bank = into()
        TE.matmul(bank[:, 0:E], U[:, 1, :], mask[:, 0, 0:E], start=True, stop=True)
        TE.matmul(bank[:, E:2 * E], U[:, 2, :], mask[:, 0, 0:E], start=True, stop=False)
        TE.matmul(bank[:, E:2 * E], U[:, 1, :], mask[:, 1, 0:E], start=False, stop=True)
        TE.matmul(bank[:, 2 * E:3 * E], U[:, 2, :], mask[:, 0, 0:E], start=True, stop=False)
        TE.matmul(bank[:, 2 * E:3 * E], U[:, 2, :], mask[:, 1, 0:E], start=False,
                  stop=True).then_inc(S("mm_done"), 1)
        pe.wait_ge(S("gate_ready"), 1)
        turn_blocks([rt[:, 6, t, 0:E] for t in range(NT)], E)
        pe.wait_ge(S("b1_in"), 16)
        turn_blocks([b1s[:, 256 * c + par:256 * c + 256:2] for c in range(2) for par in range(2)])
        pe.wait_ge(S("turned_out"), turn.n)
        pe.wait_ge(S("b2_in"), 16)
        for t in range(NT):
            for half in range(2):
                multiply(lambda c: rt_gateT[:, t * P:(t + 1) * P],
                         lambda c: b2s[:, 512 * half:512 * half + 512], 1)

        def gather(i):
            pe.wait_ge(S("hot_made"), i + 1)
            for c in range(KC):
                for w in range(2):
                    a = P * (c % 4) + SLOTS * w
                    for t in range(NT):
                        ins = TE.matmul(PS[:, 4 + c // 4, a:a + SLOTS], XR[:, w, t, P * c:P * c + P], hotr[:, t, :],
                                        start=(t == 0), stop=(t == NT - 1))
            ins.then_inc(S("gathered"), 1)

        def scatter(j, t):
            pe.wait_ge(S("hotT_out"), j + 1)
            pe.wait_ge(S("y_out"), j + 1)
            if t:
                pe.wait_ge(S("added"), 2 * j + 1)
            for b in range(2):
                ins = TE.matmul(PS[:, 6 + b, :], hotT[:, t * P:(t + 1) * P], Ys[:, 512 * b:512 * b + 512],
                                start=True, stop=True)
            ins.then_inc(S("scattered"), 1)

        def step(i, w1, w2, scat, tail=0):
            first = isinstance(i, int) and i == 0
            second = isinstance(i, int) and i == 1
            if w1:
                pe.wait_ge(S("xg_ready"), i + 1)
                if not first:
                    pe.wait_ge(S("hidden_out"), 2 * i)
                if not (first or second):
                    pe.wait_ge(S("hotT_out"), i - 1)
                for c in range(W1_UNITS):
                    if c in SPLIT_W1:
                        s = SPLIT_W1.index(c)
                        pe.wait_ge(S("parts_made"), s + 1 if first else 8 * i - 3 + s)
                        for w in range(2):
                            for b in range(4):
                                ins = TE.matmul(PS[:, b, :], xgr[:, c].rearrange("p w s -> p (w s)"),
                                                split[:, s % 2, w, 512 * b:512 * b + 512],
                                                start=(c == 0 and w == 0), stop=(c == W1_UNITS - 1 and w == 1))
                        ins.then_inc(S("parts_used"), 1)
                    else:
                        pe.wait_ge(S(f"landed{c}"), 16 * (i + 1))
                        for b in range(4):
                            ins = TE.matmul(PS[:, b, :], xgf[:, c].rearrange("p w s -> p (w s)"),
                                            ring[:, c, 512 * b:512 * b + 512],
                                            start=(c == 0), stop=(c == W1_UNITS - 1))
                        ins.then_inc(S("w1_used"), 1)
                    if scat and c in (1, 3):
                        scatter(i - 2, c // 2)
                if not first:
                    pe.wait_ge(S("act_ready"), i)
                gather(i + 1)
            elif scat:
                scatter(i - 2, 0)
                scatter(i - 2, 1)
            if w2:
                pe.wait_ge(S("act_ready"), i)
                if scat:
                    pe.wait_ge(S("added"), 2 * (i - 1))
                for k in range(W2_UNITS):
                    pe.wait_ge(S("parts_made"), 8 * i + k + 1 - tail)
                    for j2 in range(2):
                        cc = 2 * k + j2
                        for w in range(2):
                            for b in range(2):
                                ins = TE.matmul(PS[:, 6 + b, :], actr[:, cc].rearrange("p w s -> p (w s)"),
                                                split[:, k % 2, w, D * j2 + 512 * b:D * j2 + 512 * b + 512],
                                                start=(cc == 0 and w == 0), stop=(cc == KC - 1 and w == 1))
                    ins.then_inc(S("parts_used"), 1)
            if w1:
                pe.wait_ge(S("hidden_out"), 2 * i + 2)
            if w2:
                pe.wait_ge(S("hotg_made"), i)
                for t in range(NT):
                    ins = TE.transpose(PS[:, 0, t * P:(t + 1) * P], hotg[:, t, :], ident[:])
                ins.then_inc(S("hot_turned"), 1)
            if w1:
                pe.wait_ge(S("xg_parts_out"), i + 2)
                for c in range(KC):
                    for par in range(2):
                        ins = TE.matmul(PS[:, 4 + par, SLOTS * c:SLOTS * c + SLOTS],
                                        Hs[:, 256 * c + par:256 * c + 256:2], stack[:], start=True, stop=True)
                ins.then_inc(S("hidden_turned"), 1)

        pe.wait_ge(S("tables_clear"), 1)
        pe.wait_ge(S("h_used"), 1)
        pe.wait_ge(S("b2_added"), 1)
        pe.wait_ge(S("turned_out"), turn.n)
        gather(0)
        step(0, True, False, False)
        step(1, True, True, False)
        nn = pe.value_load(more_i[0:1, 0:1], min_val=0, max_val=STEPS - E) + E
        with pe.Fori(2, nn) as i:
            step(i, True, True, True)
        step(nn, False, True, True, tail=4)
        scatter(nn - 1, 0)
        scatter(nn - 1, 1)

    block.__exit__(None, None, None)


_INS = ["x", "mem", "positions", "g_mix", "w_in", "b_forget", "g_qa", "g_ka", "g_cq", "g_ckv", "w_uq", "w_ukv",
        "g_qb", "g_kb", "g_qc", "g_kc", "g_group", "w_out", "g_xmem", "g_mem", "w_mq", "w_mkv", "g_qm", "g_km",
        "w_mo", "g_ffn", "w_router", "b_router", "w_e1", "b_e1", "w_e2", "b_e2"]
_OUTS = [((1, T, D), "float32")]


def kernel(**inputs):
    import numpy as _np
    import concourse.bacc as _bacc
    from concourse import mybir as _mybir
    from concourse.bass_utils import run_bass_kernel_spmd as _run

    nc = _bacc.Bacc("TRN2", target_bir_lowering=False, num_devices=1)
    arrays, args = {}, []
    for name in _INS:
        a = _np.ascontiguousarray(inputs[name])
        arrays[f"in_{name}_dram"] = a
        args.append(nc.dram_tensor(f"in_{name}_dram", a.shape, _mybir.dt.from_np(a.dtype), kind="ExternalInput").ap())
    for i, (shape, dtype) in enumerate(_OUTS):
        dt = _mybir.dt.from_np(_np.dtype(dtype))
        args.append(nc.dram_tensor(f"out_{i}_dram", shape, dt, kind="ExternalOutput").ap())
    build(nc, *args)
    r = _run(nc, [arrays], core_ids=[0])
    got = tuple(r.results[0][f"out_{i}_dram"] for i in range(len(_OUTS)))
    return got[0]
```

```python
import math

import numpy as np

import concourse.bass as bass
from concourse import mybir

F32 = mybir.dt.float32
F32R = mybir.dt.float32r
I32 = mybir.dt.int32
ALU = mybir.AluOpType
ACT = mybir.ActivationFunctionType
AX = mybir.AxisListType

P = 128
D = 1024
T = 256
NT = T // P
KC = D // P
HD = 64
FOX_H, MLA_H, DIL_H, MEM_H = 4, 6, 6, 4
Q_RANK, KV_RANK = 384, 256
NOPE, ROPE = 64, 32
QK = NOPE + ROPE
ROT = HD // 4
THETA = 500000.0
EPS = 1e-6
BIG = 1e30
E = 32
TOPK = 4
F = 1024
SLOTS = 64
MAX_ROUNDS = T // SLOTS
STEPS = E * MAX_ROUNDS
ALPHA, LIMIT = 1.702, 7.0

WIDTHS = [("qa", 256), ("ka", 256), ("va", 256), ("fa", 4), ("cq", Q_RANK), ("ckv", KV_RANK),
          ("kr", ROPE), ("qc", 384), ("kc", 384), ("vc", 384)]
COL = {}
_at = 0
for _name, _w in WIDTHS:
    COL[_name] = (_at, _at + _w)
    _at += _w
IN_W = _at
CHUNKS = [("cq", "cq", 65536), ("ckv", "kr", 77824), ("qa", "ka", 0), ("va", "fa", 16384),
          ("qc", "qc", 24704), ("kc", "kc", 36992), ("vc", "vc", 49280)]
CHUNKS = [(COL[a][0], COL[b][1], at) for a, b, at in CHUNKS]

UNIT = 2048
W1_UNITS, W2_UNITS = KC, F // P // 2
UNITS = W1_UNITS + W2_UNITS
MM_SELF = 29
MM_MEM = 67
HALF = UNIT // 2
PARTS_W1, PARTS_W2 = 2 * W1_UNITS, 2 * W2_UNITS
PARTS = PARTS_W1 + PARTS_W2
BUFFERS = 6
assert PARTS % BUFFERS == 0
AT_TURN, AT_SCATTER, GIVE = 2, (4, 8), (10, 14)


def build(nc, x, mem, positions, g_mix, w_in, b_forget, g_qa, g_ka, g_cq, g_ckv, w_uq, w_ukv,
          g_qb, g_kb, g_qc, g_kc, g_group, w_out, g_xmem, g_mem, w_mq, w_mkv, g_qm, g_km,
          w_mo, g_ffn, w_router, b_router, w_e1, b_e1, w_e2, b_e2, out):
    base = 16512

    def at(name, shape, off, dt=F32):
        return nc.alloc_sbuf_tensor_at(name, shape, dt, offset=base + off)

    ring = at("ring", [P, UNITS, UNIT], 0)
    win = [at(f"w_in{n}", [P, KC, b - a], o) for n, (a, b, o) in enumerate(CHUNKS)]
    QKb = at("mla_qk", [P, 2, NT, MLA_H, QK], 87040)
    mlaT = at("mla_T", [P, 2, MLA_H, T], 65536)
    dilT = at("dil_T", [P, 2, 3, T], 77824)
    Vb = at("mla_v", [P, NT, MLA_H, HD], 83968)
    wout = at("w_out_sb", [P, KC, D], 0)
    wmq = at("w_mq_sb", [P, KC, 256], 32768)
    wmo = at("w_mo_sb", [P, 2, D], 40960)
    R = UNITS * UNIT * 4
    X = at("x_sb", [P, NT, D], R)
    H = at("h_sb", [P, NT, D], R + 8192)
    hT = at("h_T", [P, KC, T], R + 16384)
    proj = at("proj", [P, NT, IN_W], R + 24576)
    gain = at("gains", [P, 2, D], R + 45376)
    SG = {}
    small_at = 0
    small_list = [("g_qa", g_qa), ("g_ka", g_ka), ("g_qc", g_qc), ("g_kc", g_kc), ("g_qm", g_qm),
                  ("g_km", g_km), ("g_cq", g_cq), ("g_ckv", g_ckv), ("g_qb", g_qb), ("g_kb", g_kb),
                  ("b_router", b_router), ("b_forget", b_forget)]
    smalls = at("small_gains", [P, 1256], R + 53568)
    for n_, a_ in small_list:
        SG[n_] = smalls[:, small_at:small_at + a_.shape[-1]]
        small_at += a_.shape[-1]
    wuq = at("w_uq_sb", [P, 3, MLA_H * QK], R + 58592)
    rtmp = at("rope_tmp", [P, 2, 2, MLA_H, ROPE], R + 58592)
    wukv = at("w_ukv_sb", [P, 2, MLA_H * 128], R + 65504)
    wmkv = at("w_mkv_sb", [P, KC, 512], R + 71648)
    cqT = at("cq_T", [P, 3, T], R + 71648)
    ckvT = at("ckv_T", [P, 2, T], R + 74720)
    foxNB = at("fox_bias", [P, FOX_H, 384], R + 76768)
    foxT = at("fox_T", [P, 2, 2, T], R + 82912)
    KVm = at("mem_kv", [P, NT, 512], R + 88032)
    memT = at("mem_kT", [P, 2, T], R + 92128)
    NBs = at("mask_bias", [P, 2, 384], R + 94176)
    SCR = at("scratch", [P, 3072], R + 97248)
    Sb, Pb, PTb = (SCR[:, 1024 * k:1024 * k + 1024].rearrange("p (b n) -> p b n", b=2) for k in range(3))
    rope = at("rope_tab", [P, 8, NT, 16], R + 109536)
    U = at("upper", [P, 3, P], R + 110560)
    ident = at("ident", [P, P], R + 113888)
    stat = at("stat", [P, 448], R + 112096)
    router_w = at("w_router_sb", [P, KC, E], 49152)
    qm = at("mem_q", [P, NT, 256], 50176)
    qmT = at("mem_qT", [P, 2, T], 52224)
    om = at("mem_o", [P, NT, 256], 54272)
    omT = at("mem_oT", [P, 2, T], 56320)
    slot_of = at("slot_table", [P, NT, STEPS + 4], R + 8192)
    gate_of = at("gate_table", [P, NT, STEPS + 4], R + 9248)
    iota = at("iota", [P, P], R + 10304)
    pick = at("picked", [P, 3, NT], R + 10816)
    hotg = at("hot_gate", [P, NT, P], R + 11840)
    hotr = at("hot_r", [P, NT, SLOTS], R + 12864, F32R)
    hotT = at("hot_gate_T", [P, T], R + 13376)
    rt = at("route", [P, 12, NT, 36], R + 16384)
    Ys = at("y_sb", [P, D], R + 14400)
    given = at("given", [P, D], R + 18496)
    b1s = at("b1_rows", [P, 512], R + 19840)
    b1T = at("b1_T", [P, E, 16], R + 22592)
    XR = at("h_parts", [P, 2, NT, D], R + 24640, F32R)
    split = at("w_parts", [P, BUFFERS, 2, HALF], R + 41024, F32R)
    xgr = at("xg_parts", [P, KC, 2, SLOTS], R + 90176, F32R)
    Hs = at("hidden", [P, 2 * F], R + 94272)
    glu = at("glu", [P, KC, SLOTS], R + 102464)
    lin = at("lin", [P, KC, SLOTS], R + 104512)
    actr = at("act_parts", [P, KC, 2, SLOTS], R + 106560, F32R)
    sig = at("sig", [P, KC, SLOTS], R + 110656)
    stack = at("stacked_ident", [P, SLOTS], R + 112704)
    more_i = at("more_steps", [P, 1], R + 112960, I32)
    b2s = at("b2_sb", [E, D], R + 104448)
    PS = nc.alloc_psum_tensor("banks", [P, 8, 512], F32)

    sems = {}

    def S(name):
        if name not in sems:
            sems[name] = nc.alloc_semaphore(name)
        return sems[name]

    V, G, A, TE = nc.vector, nc.gpsimd, nc.scalar, nc.tensor

    REQ = [2, 2, 8, 4, 16, 24, 24, 6, 2, 8, 2]
    NREQ = sum(REQ)

    def cols_of(kind, k):
        a = kind * NREQ + sum(REQ[:k])
        return stat[:, a:a + REQ[k]]

    o = 4 * NREQ
    rowmax, rowsum, rowinv = stat[:, o:o + 4], stat[:, o + 4:o + 12], stat[:, o + 12:o + 16]
    logf, fz, fa2, cumq, fe = (stat[:, o + 16 + 8 * k:o + 24 + 8 * k].rearrange("p (t h) -> p t h", t=2)
                               for k in range(5))
    rowtmp = tmp4 = stat[:, 3 * NREQ:3 * NREQ + 4]
    logfb = SCR[:, 0:1024].rearrange("p (t h m) -> p t h m", t=2, h=4)

    def units():
        for h in range(FOX_H):
            r, j = 64 * (h % 2), h // 2
            yield (foxT[r:r + 64, 0, j, :], foxT[r:r + 64, 1, j, :],
                   [proj[:, t, COL["va"][0] + 64 * h:COL["va"][0] + 64 * h + 64] for t in range(NT)],
                   foxNB[:, h, :], HD ** -0.5, H[:, :, 64 * h:64 * h + 64])
        for h in range(MLA_H):
            yield (mlaT[0:QK, 0, h, :], mlaT[0:QK, 1, h, :], [Vb[:, t, h, :] for t in range(NT)],
                   NBs[:, 0, :], QK ** -0.5, H[:, :, 256 + 64 * h:320 + 64 * h])
        for h in range(DIL_H):
            r, j = 64 * (h % 2), h // 2
            yield (dilT[r:r + 64, 0, j, :], dilT[r:r + 64, 1, j, :],
                   [proj[:, t, COL["vc"][0] + 64 * h:COL["vc"][0] + 64 * h + 64] for t in range(NT)],
                   NBs[:, 1, :], HD ** -0.5, H[:, :, 640 + 64 * h:704 + 64 * h])

    SELF = list(units())
    MEM = [(qmT[64 * (h % 2):64 * (h % 2) + 64, h // 2, :], memT[64 * (h % 2):64 * (h % 2) + 64, h // 2, :],
            [KVm[:, t, 256 + 64 * h:320 + 64 * h] for t in range(NT)], None, HD ** -0.5,
            om[:, :, 64 * h:64 * h + 64]) for h in range(MEM_H)]

    memx = at("mem_sb", [P, NT, D], R + 24576 + 12288)
    mtmp = at("mask_tmp", [P, 8, 384], R + 24576)
    mtmp_i = at("mask_tmp_int", [P, 8, 384], R + 24576, I32)
    rope_i = at("rope_int", [P, 8, NT, 16], R + 109536, I32)
    pos_i = rope_i[:, 5, 0, 0:NT]
    rt_gateT = at("gate_T", [E, T], R + 16384 + 8 * 72 * 4)

    def order(n):
        for s in range(n + 3):
            if s < n:
                yield "score", s
            if 0 <= s - 2 < n:
                yield "turn", s - 2
            if 0 <= s - 3 < n:
                yield "value", s - 3

    class Banks:

        def __init__(self, first):
            self.first, self.n = first, 0

        def next(self):
            self.n += 1
            return PS[:, self.first + (self.n - 1) % 4, :]

    def tiles_of(src, col, width):
        return src[:, :, col:col + width]

    def heads(ap, h):
        return ap.rearrange("p t (h d) -> p t h d", h=h)

    def part(i, k, w2=False, last=False):
        if isinstance(i, int) and i == 0:
            return k + 1, k % BUFFERS
        k += PARTS_W1 if w2 and not last else 0
        return PARTS * i - PARTS_W2 + k + 1, (k - PARTS_W2) % BUFFERS

    block = nc.Block()
    blk = block.__enter__()

    @blk.sync
    def _(sp):
        sp.dma_start(memx[:], mem[0].rearrange("(t p) d -> p t d", p=P)).then_inc(S("mem_in"), 16)
        sp.dma_start(X[:], x[0].rearrange("(t p) d -> p t d", p=P)).then_inc(S("x_in"), 16)
        sp.dma_start(wmkv[:], w_mkv[0].rearrange("(c p) n -> p c n", p=P)).then_inc(S("w_mkv_in"), 16)
        w_in_v = w_in[0].rearrange("(c p) n -> p c n", p=P)
        for n, (a, b, _) in enumerate(CHUNKS):
            sp.dma_start(win[n][:], w_in_v[:, :, a:b]).then_inc(S(f"w_in{n}_in"), 16)
            if n == 2:
                sp.dma_start(wuq[:], w_uq[0].rearrange("(c p) n -> p c n", p=P)).then_inc(S("w_uq_in"), 16)
                sp.dma_start(wukv[:], w_ukv[0].rearrange("(c p) n -> p c n", p=P)).then_inc(S("w_ukv_in"), 16)
        sp.wait_ge(S("projected"), 1)
        sp.dma_start(wout[:], w_out[0].rearrange("(c p) n -> p c n", p=P)).then_inc(S("w_out_in"), 16)
        sp.dma_start(wmq[:], w_mq[0].rearrange("(c p) n -> p c n", p=P)).then_inc(S("w_mq_in"), 16)
        sp.dma_start(wmo[:], w_mo[0].rearrange("(c p) n -> p c n", p=P)).then_inc(S("w_mo_in"), 16)
        sp.dma_start(router_w[:], w_router[0].rearrange("(c p) n -> p c n", p=P)).then_inc(S("router_in"), 16)

        def load_w1(e, c):
            sp.dma_start(ring[:, c, :], w1_v[e, c]).then_inc(S(f"landed{c}"), 16)

        def load_w2(e, k):
            sp.dma_start(ring[:, W1_UNITS + k, :].rearrange("p (j n) -> p j n", j=2),
                         w2_v[e, k]).then_inc(S(f"landed{W1_UNITS + k}"), 16)

        w1_v = w_e1[0].rearrange("e (c p) n -> e c p n", p=P)
        w2_v = w_e2[0].rearrange("e (k j p) n -> e k p j n", p=P, j=2)
        sp.wait_ge(S("merged_out"), 1)
        for c in range(4):
            load_w1(0, c)
        for k in range(W2_UNITS):
            load_w2(0, k)
        sp.wait_ge(S("mem_queried"), 1)
        load_w1(0, 4)
        sp.wait_ge(S("mem_out"), 1)
        load_w1(0, 5)
        sp.wait_ge(S("routed"), 1)
        sp.dma_start(b1s[:], b_e1[0].rearrange("e (q n) -> (e q) n", q=4)).then_inc(S("b1_in"), 16)
        sp.dma_start(b2s[:], b_e2[0]).then_inc(S("b2_in"), 16)
        load_w1(0, 6)
        load_w1(0, 7)

        def w1_free(j, c):
            sp.wait_ge(S("parts_made"), part(j, 2 * c + 1)[0])

        for c in range(W1_UNITS):
            w1_free(0, c)
            load_w1(1, c)

        sp.wait_ge(S("more_known"), 1)
        n = sp.value_load(more_i[0:1, 0:1], min_val=0, max_val=STEPS - E) + E
        with sp.Fori(1, n - 1) as j:
            for c in range(W1_UNITS):
                w1_free(j, c)
                load_w1(bass.ds((j + 1) % E, 1), c)
            for k in range(W2_UNITS):
                sp.wait_ge(S("parts_made"), part(j, 2 * k + 1, True)[0])
                load_w2(bass.ds(j % E, 1), k)
        for k in range(W2_UNITS):
            sp.wait_ge(S("parts_made"), part(n - 1, 2 * k + 1, True)[0])
            load_w2(E - 1, k)
        for t in range(NT):
            sp.wait_ge(S("added"), 2 * (n - 1) + t + 1)
            sp.dma_start(out[0, t * P:(t + 1) * P, :], X[:, t, :]).then_inc(S("stored"), 16)
        sp.wait_ge(S("stored"), 16 * NT)

    @blk.gpsimd
    def _(pool):
        n = [0]

        def link(ins):
            n[0] += 1
            ins.then_inc(S("pool_chain"), 1)
            pool.wait_ge(S("pool_chain"), n[0])

        inv = rope[:, 7, 0, :]
        for i in range(16):
            f = float(np.float32(THETA) ** np.float32(-2 * i / 32))
            G.memset(inv[:, i:i + 1], f)
        G.memset(U[:], 1.0)
        G.memset(NBs[:, 0, :], 0.0)
        G.memset(mtmp[:, 3, :], 1.0)
        G.iota(mtmp_i[:, 0, 0:P], pattern=[[-1, P]], base=1024, channel_multiplier=1)
        G.iota(mtmp_i[:, 0, P:3 * P], pattern=[[-1, 2 * P]], base=1024 + P, channel_multiplier=1)
        link(G.memset(ident[:], 0.0))
        G.affine_select(out=ident[:], in_=ident[:], pattern=[[-1, P]], compare_op=ALU.not_equal, fill=1.0,
                        base=0, channel_multiplier=1)
        G.affine_select(out=NBs[:, 0, 0:P], in_=NBs[:, 0, 0:P], pattern=[[-1, P]], compare_op=ALU.is_ge,
                        fill=BIG, base=0, channel_multiplier=1)
        G.affine_select(out=NBs[:, 0, P:], in_=NBs[:, 0, P:], pattern=[[-1, 2 * P]], compare_op=ALU.is_ge,
                        fill=BIG, base=P, channel_multiplier=1)
        G.affine_select(out=mtmp[:, 3, P:], in_=mtmp[:, 3, P:], pattern=[[1, 2 * P]], compare_op=ALU.is_ge,
                        fill=0.0, base=0, channel_multiplier=-1)
        G.affine_select(out=U[:, 0, :], in_=U[:, 0, :], pattern=[[1, P]], compare_op=ALU.is_ge, fill=0.0,
                        base=0, channel_multiplier=-1)
        G.affine_select(out=U[:, 1, :], in_=U[:, 1, :], pattern=[[1, P]], compare_op=ALU.is_ge, fill=0.0,
                        base=-1, channel_multiplier=-1).then_inc(S("constants"), 1)

        def rotate(xv, cosv, sinv, a, b, width):
            half = width // 2
            G.tensor_tensor(a, xv, cosv, ALU.mult)
            link(G.tensor_tensor(b, xv, sinv, ALU.mult))
            G.tensor_tensor(xv[:, :, 0, :], a[:, :, 0, :], b[:, :, 1, :], ALU.subtract)
            return G.tensor_tensor(xv[:, :, 1, :], a[:, :, 1, :], b[:, :, 0, :], ALU.add)

        pool.wait_ge(S("rope_tables"), 1)
        pool.wait_ge(S("mla_normed"), 1)
        for w in range(2):
            for t in range(NT):
                xv = QKb[:, w, t, :, NOPE:].rearrange("p h (a r) -> p h a r", a=2)
                cosv, sinv = (rope[:, k, t, :].unsqueeze(1).unsqueeze(1).to_broadcast([P, MLA_H, 2, 16])
                              for k in (6, 4))
                a, b = (rtmp[:, k, (2 * w + t) % 2].rearrange("p h (a r) -> p h a r", a=2) for k in (0, 1))
                last = rotate(xv, cosv, sinv, a, b, 32)
                if (w, t) == (1, 1):
                    last.then_inc(S("mla_rotated"), 1)
                else:
                    link(last)
        pool.wait_ge(S("dil_normed"), 1)
        pool.wait_ge(S("mla_rotated"), 1)
        q0 = COL["qc"][0]
        for t in range(NT):
            xv = proj[:, t, q0:q0 + 768].rearrange("p (h d) -> p h d", d=HD)[:, :, 0:ROT] \
                .rearrange("p h (a r) -> p h a r", a=2)
            cosv, sinv = (rope[:, k, t, 0:16:2].unsqueeze(1).unsqueeze(1).to_broadcast([P, 12, 2, 8])
                          for k in (6, 4))
            a, b = (rtmp[:, k, t].rearrange("p h r -> p (h r)").rearrange("p (h a r) -> p h a r", a=2, r=8)
                    for k in (0, 1))
            last = rotate(xv, cosv, sinv, a, b, 16)
            if t == 1:
                last.then_inc(S("dil_rotated"), 1)
            else:
                link(last)

        pool.wait_ge(S("h_used"), 1)
        pool.wait_ge(S("h_turned"), 1)
        G.iota(iota[:], pattern=[[0, 2], [1, SLOTS]], base=0, channel_multiplier=0,
               allow_small_or_imprecise_dtypes=True)
        G.memset(slot_of[:], -5.0)
        G.memset(gate_of[:], 0.0)
        pool.wait_ge(S("routed"), 1)
        G.tensor_tensor(stack[:], ident[:, 0:SLOTS], ident[:, SLOTS:], ALU.add).then_inc(S("tables_clear"), 1)
        pool.wait_ge(S("tables_clear"), 1)
        pool.wait_ge(S("tables_made"), 1)

        def hot_for_gather(i):
            if not (isinstance(i, int) and i == 0):
                pool.wait_ge(S("gathered"), i)
            G.tensor_copy(pick[:, 0, :], slot_of[:, :, bass.ds(i, 1)].rearrange("p t a -> p (t a)"))
            pool.drain()
            for t in range(NT):
                ins = G.tensor_scalar(hotr[:, t, :], iota[:, 0:SLOTS], pick[:, 0, t:t + 1], None, ALU.is_equal)
            ins.then_inc(S("hot_made"), 1)

        def hot_for_scatter(i, first=False):
            if not first:
                pool.wait_ge(S("hot_turned"), i)
            G.tensor_copy(pick[:, 1, :], slot_of[:, :, bass.ds(i, 1)].rearrange("p t a -> p (t a)"))
            G.tensor_copy(pick[:, 2, :], gate_of[:, :, bass.ds(i, 1)].rearrange("p t a -> p (t a)"))
            pool.drain()
            for t in range(NT):
                ins = G.tensor_scalar(hotg[:, t, :], iota[:], pick[:, 1, t:t + 1], pick[:, 2, t:t + 1],
                                      ALU.is_equal, ALU.mult)
            ins.then_inc(S("hotg_made"), 1)

        hot_for_gather(0)
        hot_for_gather(1)
        hot_for_gather(2)
        hot_for_scatter(0, first=True)
        pool.wait_ge(S("b2_added"), 1)

        def add(j, t):
            pool.wait_ge(S("given_out"), 2 * j + t + 1)
            G.tensor_tensor(X[:, t, :], X[:, t, :], given[:], ALU.add).then_inc(S("added"), 1)

        nn = pool.value_load(more_i[0:1, 0:1], min_val=0, max_val=STEPS - E) + E
        with pool.Fori(2, nn) as i:
            hot_for_gather(i + 1)
            hot_for_scatter(i - 1)
            for t in range(NT):
                add(i - 2, t)
        hot_for_scatter(nn - 1)
        for j in (nn - 2, nn - 1):
            for t in range(NT):
                add(j, t)

    @blk.scalar
    def _(act):
        turned = Banks(0)
        roots = [0]
        n = [0]

        def link(ins):
            n[0] += 1
            ins.then_inc(S("act_chain"), 1)
            act.wait_ge(S("act_chain"), n[0])

        act.dma_start(pos_i[:], positions[0].rearrange("(t p) -> p t", p=P),
                      allow_slow_non_contiguous=True).then_inc(S("pos_in"), 16)
        act.dma_start(gain[:, 0, :], g_mem[0].partition_broadcast(P)).then_inc(S("g_mem_in"), 16)
        act.dma_start(gain[:, 1, :], g_mix[0].partition_broadcast(P)).then_inc(S("g_mix_in"), 16)
        for name, a in small_list:
            act.dma_start(SG[name], a[0].partition_broadcast(P)).then_inc(S("smalls_in"), 16)

        def leave(out_ap, k, cols, rows=P):
            src = turned.next()
            act.wait_ge(S("turned"), turned.n)
            A.copy(out_ap, src[0:rows, 0:cols] if k is None else
                   src[0:rows, 0:cols].rearrange("p (a b) -> p a b", a=k)).then_inc(S("turned_out"), 1)

        def root(cols):
            k = roots[0]
            roots[0] += 1
            act.wait_ge(S("var_ready"), k + 1)
            link(A.activation(cols_of(2, k), cols_of(1, k), ACT.Ln))
            A.activation(cols_of(2, k), cols_of(2, k), ACT.Exp, scale=-0.5).then_inc(S("root_ready"), 1)

        def whole_squares(src, k):
            for t in range(NT):
                ins = A.activation(SCR[:, 1024 * t:1024 * t + 1024], src[:, t, :], ACT.Square,
                                   accum_out=cols_of(0, k)[:, t:t + 1])
            ins.then_inc(S("squared"), 1)

        def turned_rows():
            for t in range(NT):
                for half in range(2):
                    leave(hT[:, 4 * half:4 * half + 4, t * P:(t + 1) * P], 4, 512)

        act.wait_ge(S("angles"), 1)
        A.activation(rope[:, 5], rope[:, 3], ACT.Sin, scale=0.5)
        A.activation(rope[:, 4], rope[:, 3], ACT.Sin).then_inc(S("sines"), 1)
        act.wait_ge(S("mem_in"), 16)
        whole_squares(memx, 0)
        root(2)
        act.wait_ge(S("x_in"), 16)
        whole_squares(X, 1)
        root(2)
        turned_rows()
        act.dma_start(gain[:, 0, :], g_group[0].partition_broadcast(P)).then_inc(S("g_group_in"), 16)
        act.wait_ge(S("mem_kv_ready"), 1)
        act.wait_ge(S("squared"), 2)
        A.activation(SCR[:, 0:512].rearrange("p (t n) -> p t n", t=2), KVm[:, :, 0:256],
                     ACT.Square).then_inc(S("squared"), 1)
        act.wait_ge(S("mem_projected"), 1)
        turned_rows()
        act.dma_start(gain[:, 1, :], g_xmem[0].partition_broadcast(P)).then_inc(S("g_xmem_in"), 16)
        root(8)
        leave(memT[:], 2, 512)
        act.wait_ge(S("latents_ready"), 1)
        act.wait_ge(S("squares_read"), 1)
        for t in range(NT):
            A.activation(SCR[:, 512 * t:512 * t + Q_RANK], proj[:, t, COL["cq"][0]:COL["cq"][1]], ACT.Square,
                         accum_out=cols_of(0, 3)[:, t:t + 1])
            ins = A.activation(SCR[:, 1024 + 512 * t:1024 + 512 * t + KV_RANK],
                               proj[:, t, COL["ckv"][0]:COL["ckv"][1]], ACT.Square,
                               accum_out=cols_of(0, 3)[:, 2 + t:3 + t])
        ins.then_inc(S("squared"), 1)
        root(4)
        act.wait_ge(S("mem_projected"), 1)
        for t in range(NT):
            leave(cqT[:, :, t * P:(t + 1) * P], 3, Q_RANK)
        leave(ckvT[:], 2, 512)
        act.wait_ge(S("fox_ready"), 1)
        act.wait_ge(S("squared"), 4)
        A.activation(SCR[:, 0:1024].rearrange("p (t n) -> p t n", t=2), proj[:, :, 0:512],
                     ACT.Square).then_inc(S("squared"), 1)
        root(16)
        act.wait_ge(S("forget_abs"), 1)
        link(A.activation(fe, fe, ACT.Exp, scale=-1.0))
        A.activation(fe, fe, ACT.Ln, bias=1.0).then_inc(S("forget_log"), 1)
        act.wait_ge(S("mla_ready"), 1)
        act.wait_ge(S("squares_read"), 2)
        A.activation(SCR[:, 0:2304], QKb[:].rearrange("p w t h d -> p (w t h d)"), ACT.Square) \
            .then_inc(S("squared"), 1)
        leave(foxT[:, 0], 2, 512)
        leave(foxT[:, 1], 2, 512)
        root(24)
        for w in range(2):
            for pair in range(3):
                if (w, pair) == (0, 0):
                    act.wait_ge(S("latents_projected"), 1)
                leave(mlaT[0:QK, w, 2 * pair:2 * pair + 2, :], 2, 512, QK)
        act.wait_ge(S("dil_ready"), 1)
        act.wait_ge(S("squares_read"), 3)
        A.activation(SCR[:, 0:1536].rearrange("p (t n) -> p t n", t=2),
                     proj[:, :, COL["qc"][0]:COL["kc"][1]], ACT.Square).then_inc(S("squared"), 1)
        root(24)
        for w in range(2):
            leave(dilT[:, w, 0:2, :], 2, 512)
            leave(dilT[:, w, 2, :], None, 256)

        scored = [0]

        def attend(units_, cols, mm_before):
            mm, at_value = mm_before, {}
            for what, u in order(len(units_)):
                if what != "turn":
                    mm += 1
                if what == "value":
                    at_value[u] = mm
            spans = [(0, cols - 256), (cols - 256, cols)]
            for s in range(len(units_) + 2):
                if 0 <= s - 2 < len(units_):
                    if s - 4 >= 0:
                        act.wait_ge(S("mm_done"), at_value[s - 4])
                    leave(PTb[:, s % 2, 0:cols], None, cols)
                if s < len(units_):
                    scored[0] += 1
                    act.wait_ge(S("scored"), scored[0])
                    if s >= 2:
                        act.wait_ge(S("turned"), turned.n)
                    for t, (a, b) in enumerate(spans):
                        c = 2 * (s % 2) + t
                        ins = A.activation(Pb[:, s % 2, a:b], Sb[:, s % 2, a:b], ACT.Exp,
                                           bias=rowmax[:, c:c + 1], accum_out=rowsum[:, 2 * (s % 4) + t:2 * (s % 4) + t + 1])
                    ins.then_inc(S("exped"), 1)

        act.wait_ge(S("fox_bias_made"), 1)
        attend(SELF, 384, MM_SELF)
        act.wait_ge(S("self_done"), 1)
        for t in range(NT):
            for k, (a, b) in enumerate(((0, 256), (256, 640), (640, 1024))):
                ins = A.activation(SCR[:, 1024 * t + a:1024 * t + b], H[:, t, a:b], ACT.Square,
                                   accum_out=cols_of(0, 7)[:, 2 * k + t:2 * k + t + 1])
        ins.then_inc(S("squared"), 1)
        root(6)
        turned_rows()
        act.dma_start(gain[:, 0, :], g_ffn[0].partition_broadcast(P)).then_inc(S("g_ffn_in"), 16)
        act.wait_ge(S("x1_ready"), 1)
        act.wait_ge(S("squared"), 8)
        whole_squares(X, 8)
        root(2)
        act.wait_ge(S("merged_out"), 1)
        turned_rows()
        act.wait_ge(S("mem_q_ready"), 1)
        act.wait_ge(S("squared"), 9)
        A.activation(SCR[:, 0:512].rearrange("p (t n) -> p t n", t=2), qm[:], ACT.Square) \
            .then_inc(S("squared"), 1)
        root(8)
        leave(qmT[:], 2, 512)
        attend(MEM, 512, MM_MEM)
        leave(omT[:], 2, 512)
        act.wait_ge(S("x2_ready"), 1)
        whole_squares(X, 10)
        root(2)
        turned_rows()
        act.wait_ge(S("h_ready"), 1)
        for t in range(NT):
            ins = A.copy(XR[:, 0, t, :], H[:, t, :])
        ins.then_inc(S("h_high"), 1)
        act.wait_ge(S("logits_ready"), 1)
        for t in range(NT):
            ins = A.activation(rt[:, 4, t, 0:E], rt[:, 0, t, 0:E], ACT.Exp, bias=rt[:, 2, t, 0:1])
        ins.then_inc(S("gates_exped"), 1)
        leave(rt_gateT[:], None, 256, E)
        leave(b1T[:].rearrange("p e (q k) -> p k (e q)", q=4), 4, 512)

        def high(i, k, w2=False, last=False):
            slot = k // 2 + (W1_UNITS if w2 else 0)
            n, b = part(i, k, w2, last)
            act.wait_ge(S(f"landed{slot}"), 16 * (i if w2 else i + 1))
            if not isinstance(n, int) or n > BUFFERS:
                act.wait_ge(S("parts_used"), n - BUFFERS)
            A.copy(split[:, b, 0, :], ring[:, slot, HALF * (k % 2):HALF * (k % 2) + HALF]) \
                .then_inc(S("high_made"), 1)

        def y_leaves(j, last=False):
            act.wait_ge(S("parts_used"), part(j + 1, PARTS_W2 - 1, True, last)[0])
            if not (isinstance(j, int) and j == 0):
                act.wait_ge(S("scattered"), 2 * j)
            A.copy(Ys[:], PS[:, 6:8, :].rearrange("p b n -> p (b n)")).then_inc(S("y_out"), 1)

        def hot_leaves(j):
            act.wait_ge(S("hot_turned"), j + 1)
            A.copy(hotT[:], PS[:, 6, 0:T]).then_inc(S("hotT_out"), 1)

        def given_leaves(j, t):
            act.wait_ge(S("scattered"), 2 * j + t + 1)
            if t or not (isinstance(j, int) and j == 0):
                act.wait_ge(S("added"), 2 * j + t)
            A.copy(given[:], PS[:, 6:8, :].rearrange("p b n -> p (b n)")).then_inc(S("given_out"), 1)

        def step(i, w1, w2, scat, last=False):
            def highs(a, b, w2_=False):
                for k in range(a, b):
                    if w1 or w2_:
                        high(i, k, w2_, last)

            highs(0, 5)
            if scat:
                y_leaves(i - 2)
            highs(5, 6)
            if w2:
                act.wait_ge(S("glu_ready"), i)
                A.activation(sig[:], glu[:], ACT.Sigmoid, scale=ALPHA).then_inc(S("sig_ready"), 1)
            highs(6, 7)
            if scat:
                hot_leaves(i - 2)
            highs(7, GIVE[0])
            if scat:
                given_leaves(i - 2, 0)
            highs(GIVE[0], GIVE[1])
            if scat:
                given_leaves(i - 2, 1)
            highs(GIVE[1], PARTS_W1)
            if w2:
                highs(0, 5, True)
            if w1:
                act.wait_ge(S("parts_used"), part(i, PARTS_W1 - 1)[0])
                if not (isinstance(i, int) and i == 0):
                    act.wait_ge(S("hidden_turned"), i)
                A.copy(Hs[:], PS[:, 0:4, :].rearrange("p b n -> p (b n)")).then_inc(S("hidden_out"), 1)
                act.wait_ge(S("gathered"), i + 2)
                A.copy(xgr[:].rearrange("p c w s -> p (c w s)"),
                       PS[:, 4:6, :].rearrange("p b n -> p (b n)")).then_inc(S("xg_parts_out"), 1)
            if w2:
                highs(5, PARTS_W2, True)

        act.wait_ge(S("gathered"), 1)
        A.copy(xgr[:].rearrange("p c w s -> p (c w s)"),
               PS[:, 4:6, :].rearrange("p b n -> p (b n)")).then_inc(S("xg_parts_out"), 1)
        step(0, True, False, False)
        step(1, True, True, False)
        nn = act.value_load(more_i[0:1, 0:1], min_val=0, max_val=STEPS - E) + E
        with act.Fori(2, nn) as i:
            step(i, True, True, True)
        step(nn, False, True, True, last=True)
        y_leaves(nn - 1, last=True)
        hot_leaves(nn - 1)
        for t in range(NT):
            given_leaves(nn - 1, t)

    @blk.vector
    def _(dve):
        product = Banks(4)
        chain = [0]
        req = [0, 0]

        def link(ins):
            chain[0] += 1
            ins.then_inc(S("dve_chain"), 1)
            dve.wait_ge(S("dve_chain"), chain[0])

        def take():
            bank = product.next()
            dve.wait_ge(S("mm_done"), product.n)
            return bank

        def leave(out_ap, in_ap):
            V.tensor_copy(out_ap, in_ap).then_inc(S("mm_out"), 1)

        def after_leaving():
            dve.wait_ge(S("mm_out"), product.n)

        def variance(parts):
            k = req[0]
            req[0] += 1
            for n, (a, b, count) in enumerate(parts):
                ins = V.tensor_scalar(cols_of(1, k)[:, a:b], cols_of(0, k)[:, a:b], 1.0 / count, EPS,
                                      ALU.mult, ALU.add)
            ins.then_inc(S("var_ready"), 1)

        def newton():
            k = req[1]
            req[1] += 1
            y, v, w = cols_of(2, k), cols_of(1, k), cols_of(3, k)
            dve.wait_ge(S("root_ready"), k + 1)
            link(V.tensor_tensor(w, y, y, ALU.mult))
            link(V.tensor_tensor(w, w, v, ALU.mult))
            link(V.tensor_scalar(w, w, -0.5, 1.5, ALU.mult, ALU.add))
            link(V.tensor_tensor(y, y, w, ALU.mult))
            return y

        def norm_rows(src, y, g, sem):
            for t in range(NT):
                ins = V.scalar_tensor_tensor(out=H[:, t, :], in0=src[:, t, :], scalar=y[:, t:t + 1],
                                             in1=gain[:, g, :], op0=ALU.mult, op1=ALU.mult)
            ins.then_inc(S(sem), 1)

        ang, ki, kf, r = rope[:, 0], rope_i[:, 1], rope[:, 2], rope[:, 3]
        dve.wait_ge(S("pos_in"), 16)
        dve.wait_ge(S("constants"), 1)
        link(V.tensor_copy(kf[:, :, 0], pos_i[:]))
        link(V.tensor_tensor(ang, kf[:, :, 0:1].to_broadcast([P, NT, 16]),
                             rope[:, 7, 0:1, :].to_broadcast([P, NT, 16]), ALU.mult))
        link(V.tensor_scalar(kf, ang, 1.0 / (2 * math.pi), None, ALU.mult))
        link(V.tensor_copy(ki, kf))
        link(V.tensor_copy(kf, ki))
        c1 = 6.28125
        c2 = float(np.float32(np.floor((2 * math.pi - c1) * 2 ** 20) / 2 ** 20))
        c3 = 2 * math.pi - c1 - c2
        link(V.scalar_tensor_tensor(out=r, in0=kf, scalar=-c1, in1=ang, op0=ALU.mult, op1=ALU.add))
        link(V.scalar_tensor_tensor(out=r, in0=kf, scalar=-c2, in1=r, op0=ALU.mult, op1=ALU.add))
        link(V.scalar_tensor_tensor(out=r, in0=kf, scalar=-c3, in1=r, op0=ALU.mult, op1=ALU.add))
        V.tensor_scalar(r, r, 3.1415925, -3.1415925, ALU.min, ALU.max).then_inc(S("angles"), 1)
        V.tensor_scalar(mtmp_i[:, 1, :], mtmp_i[:, 0, :], 3, None, ALU.bitwise_and)
        link(V.tensor_scalar(mtmp_i[:, 2, :], mtmp_i[:, 0, :], 15, None, ALU.bitwise_and))
        V.tensor_scalar(mtmp[:, 4, :], mtmp_i[:, 1, :], 0.0, None, ALU.is_equal)
        link(V.tensor_scalar(mtmp[:, 5, :], mtmp_i[:, 2, :], 0.0, None, ALU.is_equal))
        link(V.tensor_tensor(mtmp[:, 3, :], mtmp[:, 3, :], mtmp[:, 4, :], ALU.add))
        link(V.tensor_tensor(mtmp[:, 3, :], mtmp[:, 3, :], mtmp[:, 5, :], ALU.add))
        V.tensor_scalar(mtmp[:, 4, :], mtmp[:, 3, :], 0.0, BIG, ALU.is_equal, ALU.mult)
        V.tensor_scalar(mtmp[:, 5, :], mtmp[:, 3, :], 2.0, -math.log(2), ALU.is_equal, ALU.mult)
        link(V.tensor_scalar(mtmp[:, 6, :], mtmp[:, 3, :], 3.0, -math.log(3), ALU.is_equal, ALU.mult))
        link(V.tensor_tensor(mtmp[:, 4, :], mtmp[:, 4, :], mtmp[:, 5, :], ALU.add))
        link(V.tensor_tensor(mtmp[:, 4, :], mtmp[:, 4, :], mtmp[:, 6, :], ALU.add))
        link(V.tensor_tensor(NBs[:, 1, :], NBs[:, 0, :], mtmp[:, 4, :], ALU.add))
        dve.wait_ge(S("sines"), 1)
        link(V.tensor_tensor(rope[:, 6], rope[:, 5], rope[:, 5], ALU.mult))
        V.tensor_scalar(rope[:, 6], rope[:, 6], -2.0, 1.0, ALU.mult, ALU.add).then_inc(S("rope_tables"), 1)

        dve.wait_ge(S("squared"), 1)
        variance([(0, 2, D)])
        dve.wait_ge(S("squared"), 2)
        variance([(0, 2, D)])
        y = newton()
        dve.wait_ge(S("g_mem_in"), 16)
        norm_rows(memx, y, 0, "rows_ready")
        y = newton()
        dve.wait_ge(S("turned"), 4)
        dve.wait_ge(S("g_mix_in"), 16)
        norm_rows(X, y, 1, "rows_ready")
        dve.wait_ge(S("smalls_in"), 16 * len(small_list))
        for t in range(NT):
            leave(KVm[:, t, :], take())
        after_leaving()
        dve.sem_inc(S("mem_kv_ready"), 1)

        def head_sums(k, src, out_ap, squared):
            dve.wait_ge(S("squared"), squared)
            V.tensor_reduce(out_ap, src, AX.X, ALU.add).then_inc(S("squares_read"), 1)
            head_sums.n += 1
            dve.wait_ge(S("squares_read"), head_sums.n)
        head_sums.n = 0

        def scale_heads(ap, y, h, d):
            link(V.tensor_tensor(ap, ap, y.rearrange("p (t h) -> p t h", t=NT).unsqueeze(3)
                                 .to_broadcast([P, NT, h, d]), ALU.mult))

        def gain_heads(ap, g, h, d):
            return V.tensor_tensor(ap, ap, g.unsqueeze(1).unsqueeze(1).to_broadcast([P, NT, h, d]), ALU.mult)

        def project(n):
            a, b, _ = CHUNKS[n]
            for t in range(NT):
                leave(proj[:, t, a:b], take()[:, 0:b - a])

        head_sums(2, SCR[:, 0:512].rearrange("p (t h d) -> p t h d", t=NT, h=MEM_H),
                  cols_of(0, 2).rearrange("p (t h) -> p t h", t=NT), 3)
        variance([(0, 8, HD)])
        dve.wait_ge(S("rows_ready"), 2)
        project(0)
        project(1)
        after_leaving()
        dve.sem_inc(S("latents_ready"), 1)
        y = newton()
        kv = heads(KVm[:, :, 0:256], MEM_H)
        scale_heads(kv, y, MEM_H, HD)
        gain_heads(kv, SG["g_km"], MEM_H, HD).then_inc(S("mem_keys_normed"), 1)
        dve.wait_ge(S("squared"), 4)
        variance([(0, 2, Q_RANK), (2, 4, KV_RANK)])
        project(2)
        after_leaving()
        dve.sem_inc(S("fox_ready"), 1)
        y = newton()
        for t in range(NT):
            for k, name, w in ((0, "cq", Q_RANK), (2, "ckv", KV_RANK)):
                ap = proj[:, t, COL[name][0]:COL[name][1]]
                ins = V.scalar_tensor_tensor(out=ap, in0=ap, scalar=y[:, k + t:k + t + 1], in1=SG["g_" + name],
                                             op0=ALU.mult, op1=ALU.mult)
        ins.then_inc(S("latents_normed"), 1)
        head_sums(4, SCR[:, 0:1024].rearrange("p (t h d) -> p t h d", t=NT, h=8),
                  cols_of(0, 4).rearrange("p (t h) -> p t h", t=NT), 5)
        variance([(0, 16, HD)])
        project(3)
        after_leaving()
        link(V.tensor_tensor(fz, proj[:, :, COL["fa"][0]:COL["fa"][1]],
                             SG["b_forget"].unsqueeze(1).to_broadcast([P, NT, FOX_H]), ALU.add))
        link(V.tensor_scalar(fa2, fz, -1.0, None, ALU.mult))
        V.tensor_tensor(fe, fz, fa2, ALU.max).then_inc(S("forget_abs"), 1)
        y = newton()
        fox = heads(proj[:, :, 0:512], 8)
        scale_heads(fox, y, 8, HD)
        gain_heads(fox[:, :, 0:4], SG["g_qa"], 4, HD)
        gain_heads(fox[:, :, 4:8], SG["g_ka"], 4, HD).then_inc(S("fox_normed"), 1)
        link(V.tensor_scalar(fz, fz, 0.0, None, ALU.min))
        dve.wait_ge(S("forget_log"), 1)
        V.tensor_tensor(logf, fz, fe, ALU.subtract).then_inc(S("logf_ready"), 1)
        for t in range(NT):
            for half in range(2):
                leave(QKb[:, 0, t, 3 * half:3 * half + 3, :], take()[:, 0:3 * QK].rearrange("p (h d) -> p h d", d=QK))
        for t in range(NT):
            for half in range(2):
                b = take()[:, 0:384].rearrange("p (h d) -> p h d", d=128)
                V.tensor_copy(QKb[:, 1, t, 3 * half:3 * half + 3, 0:NOPE], b[:, :, 0:NOPE])
                leave(Vb[:, t, 3 * half:3 * half + 3, :], b[:, :, NOPE:])
        V.tensor_copy(QKb[:, 1, :, :, NOPE:], proj[:, :, COL["kr"][0]:COL["kr"][1]].unsqueeze(2)
                      .to_broadcast([P, NT, MLA_H, ROPE])).then_inc(S("mla_ready"), 1)
        head_sums(5, SCR[:, 0:2304].rearrange("p (w h d) -> p w h d", w=2, d=QK),
                  cols_of(0, 5).rearrange("p (w h) -> p w h", w=2), 6)
        variance([(0, 24, QK)])
        project(4)
        y = newton()
        for w, g in ((0, "g_qb"), (1, "g_kb")):
            ap = QKb[:, w]
            link(V.tensor_tensor(ap, ap, y[:, 12 * w:12 * w + 12].rearrange("p (t h) -> p t h", t=NT).unsqueeze(3)
                                 .to_broadcast([P, NT, MLA_H, QK]), ALU.mult))
            ins = gain_heads(ap, SG[g], MLA_H, QK)
        ins.then_inc(S("mla_normed"), 1)
        project(5)
        after_leaving()
        dve.sem_inc(S("dil_ready"), 1)
        dve.wait_ge(S("logf_ready"), 1)
        dve.wait_ge(S("squares_read"), 3)
        head_sums(6, SCR[:, 0:1536].rearrange("p (t h d) -> p t h d", t=NT, h=12),
                  cols_of(0, 6).rearrange("p (t h) -> p t h", t=NT), 7)
        variance([(0, 24, HD)])
        V.tensor_copy(logfb, logf.unsqueeze(3).to_broadcast([P, NT, FOX_H, P])).then_inc(S("logf_wide"), 1)
        project(6)
        leave(cumq, take()[:, 0:8].rearrange("p (t h) -> p t h", t=NT))
        after_leaving()
        y = newton()
        dil = heads(proj[:, :, COL["qc"][0]:COL["kc"][1]], 12)
        scale_heads(dil, y, 12, HD)
        gain_heads(dil[:, :, 0:6], SG["g_qc"], 6, HD)
        gain_heads(dil[:, :, 6:12], SG["g_kc"], 6, HD).then_inc(S("dil_normed"), 1)
        for h in range(FOX_H):
            b = take()
            V.scalar_tensor_tensor(out=foxNB[:, h, 0:P], in0=b[:, 0:P], scalar=cumq[:, 0, h:h + 1],
                                   in1=NBs[:, 0, 0:P], op0=ALU.subtract, op1=ALU.add)
            V.scalar_tensor_tensor(out=foxNB[:, h, P:], in0=b[:, 0:2 * P], scalar=cumq[:, 1, h:h + 1],
                                   in1=NBs[:, 0, P:], op0=ALU.subtract, op1=ALU.add).then_inc(S("mm_out"), 1)
        after_leaving()
        dve.sem_inc(S("fox_bias_made"), 1)

        scored = [0]

        def attend(units_, cols):
            first = scored[0]
            spans = [(0, cols - 256), (cols - 256, cols)]
            for what, u in order(len(units_)):
                q, k, v, nb, scale, o_ap = units_[u]
                c = 2 * (u % 2)
                if what == "score":
                    b = take()
                    if first + u >= 2:
                        dve.wait_ge(S("exped"), first + u - 1)
                    if nb is None:
                        V.tensor_scalar(Sb[:, u % 2, 0:cols], b[:, 0:cols], scale, None,
                                        ALU.mult).then_inc(S("mm_out"), 1)
                    else:
                        V.scalar_tensor_tensor(out=Sb[:, u % 2, 0:cols], in0=b[:, 0:cols], scalar=scale, in1=nb,
                                               op0=ALU.mult, op1=ALU.subtract).then_inc(S("mm_out"), 1)
                    after_leaving()
                    for t, (a, e) in enumerate(spans):
                        ins = V.tensor_reduce(rowtmp[:, c + t:c + t + 1], Sb[:, u % 2, a:e], AX.X, ALU.max)
                    link(ins)
                    V.tensor_scalar(rowmax[:, c:c + 2], rowtmp[:, c:c + 2], -1.0, None,
                                    ALU.mult).then_inc(S("scored"), 1)
                    scored[0] += 1
                if what == "value":
                    b = take()
                    link(V.reciprocal(rowinv[:, c:c + 2], rowsum[:, 2 * (u % 4):2 * (u % 4) + 2]))
                    V.tensor_tensor(o_ap, b[:, 0:2 * HD].rearrange("p (t d) -> p t d", t=NT),
                                    rowinv[:, c:c + 2].unsqueeze(2).to_broadcast([P, NT, HD]),
                                    ALU.mult).then_inc(S("mm_out"), 1)
            after_leaving()

        dve.wait_ge(S("turned"), 8)
        attend(SELF, 384)
        dve.sem_inc(S("self_done"), 1)
        dve.wait_ge(S("squared"), 8)
        variance([(0, 2, 256), (2, 4, 384), (4, 6, 384)])
        y = newton()
        dve.wait_ge(S("g_group_in"), 16)
        for t in range(NT):
            for k, (a, e) in enumerate(((0, 256), (256, 640), (640, 1024))):
                ins = V.scalar_tensor_tensor(out=H[:, t, a:e], in0=H[:, t, a:e], scalar=y[:, 2 * k + t:2 * k + t + 1],
                                             in1=gain[:, 0, a:e], op0=ALU.mult, op1=ALU.mult)
        ins.then_inc(S("rows_ready"), 1)

        def add_rows(sem):
            for t in range(NT):
                for half in range(2):
                    b = take()
                    ap = X[:, t, 512 * half:512 * half + 512]
                    V.tensor_tensor(ap, ap, b, ALU.add).then_inc(S("mm_out"), 1)
            after_leaving()
            dve.sem_inc(S(sem), 1)

        add_rows("x1_ready")
        dve.wait_ge(S("squared"), 9)
        variance([(0, 2, D)])
        y = newton()
        dve.wait_ge(S("g_xmem_in"), 16)
        dve.wait_ge(S("merged_out"), 1)
        norm_rows(X, y, 1, "rows_ready")
        for t in range(NT):
            leave(qm[:, t, :], take()[:, 0:256])
        after_leaving()
        dve.sem_inc(S("mem_q_ready"), 1)
        head_sums(9, SCR[:, 0:512].rearrange("p (t h d) -> p t h d", t=NT, h=MEM_H),
                  cols_of(0, 9).rearrange("p (t h) -> p t h", t=NT), 10)
        variance([(0, 8, HD)])
        y = newton()
        q4 = heads(qm[:], MEM_H)
        scale_heads(q4, y, MEM_H, HD)
        gain_heads(q4, SG["g_qm"], MEM_H, HD).then_inc(S("mem_q_normed"), 1)
        attend(MEM, 512)
        dve.sem_inc(S("mem_attended"), 1)
        add_rows("x2_ready")
        dve.wait_ge(S("squared"), 11)
        variance([(0, 2, D)])
        y = newton()
        dve.wait_ge(S("g_ffn_in"), 16)
        norm_rows(X, y, 0, "h_ready")
        dve.wait_ge(S("h_high"), 1)
        for t in range(NT):
            ins = V.tensor_tensor(XR[:, 1, t, :], H[:, t, :], XR[:, 0, t, :].bitcast(F32), ALU.subtract)
        ins.then_inc(S("h_used"), 1)

        L, top, rep, ex, mask, gate, rank = rt[:, 0], rt[:, 1], rt[:, 3], rt[:, 4], rt[:, 5], rt[:, 6], rt[:, 7]
        for t in range(NT):
            V.tensor_tensor(L[:, t, 0:E], take()[:, 0:E], SG["b_router"], ALU.add).then_inc(S("mm_out"), 1)
        link(V.memset(L[:, :, E:], 3e38))
        for t in range(NT):
            ins = V.max(out=top[:, t, 0:8], in_=L[:, t, :])
        link(ins)
        for t in range(NT):
            V.match_replace(out=rep[:, t, :], in_to_replace=top[:, t, 0:8], in_values=L[:, t, :], imm_value=-3e38)
        V.tensor_scalar(rt[:, 2, :, 0:1], top[:, :, 4:5], -1.0, None, ALU.mult).then_inc(S("logits_ready"), 1)
        dve.wait_ge(S("logits_ready"), 1)
        V.tensor_tensor(mask[:, :, 0:E], L[:, :, 0:E], rep[:, :, 0:E], ALU.not_equal).then_inc(S("mask_ready"), 1)
        dve.wait_ge(S("mask_ready"), 1)
        dve.wait_ge(S("gates_exped"), 1)
        link(V.tensor_tensor(ex[:, :, 0:E], ex[:, :, 0:E], mask[:, :, 0:E], ALU.mult))
        link(V.tensor_reduce(rt[:, 2, :, 8], ex[:, :, 0:E], AX.X, ALU.add))
        link(V.reciprocal(rt[:, 2, :, 9], rt[:, 2, :, 8]))
        V.tensor_tensor(gate[:, :, 0:E], ex[:, :, 0:E], rt[:, 2, :, 9:10].to_broadcast([P, NT, E]),
                        ALU.mult).then_inc(S("gate_ready"), 1)
        b = take()
        link(V.scalar_tensor_tensor(out=rank[:, :, 0:E], in0=b[:, 0:2 * E].rearrange("p (t e) -> p t e", t=NT),
                                    scalar=1.0, in1=mask[:, :, 0:E], op0=ALU.add, op1=ALU.mult))
        most = rt[:, 2, 0, 12:20]
        link(V.tensor_reduce(most[:, 0:1], b[:, 2 * E:3 * E], AX.X, ALU.max))
        for r in range(1, MAX_ROUNDS):
            ins = V.tensor_scalar(most[:, r:r + 1], most[:, 0:1], SLOTS * r + 0.5, float(E), ALU.is_gt, ALU.mult)
        link(ins)
        link(V.tensor_tensor(most[:, 4:5], most[:, 1:2], most[:, 2:3], ALU.add))
        V.tensor_tensor(more_i[:], most[:, 4:5], most[:, 3:4], ALU.add).then_inc(S("more_known"), 1)
        dve.wait_ge(S("tables_clear"), 1)
        dve.wait_ge(S("gate_ready"), 1)
        for r in range(MAX_ROUNDS):
            V.tensor_scalar(slot_of[:, :, E * r:E * r + E], rank[:, :, 0:E], -1.0 - SLOTS * r, None, ALU.add)
            ins = V.tensor_copy(gate_of[:, :, E * r:E * r + E], gate[:, :, 0:E])
        ins.then_inc(S("tables_made"), 1)
        dve.wait_ge(S("more_known"), 1)
        dve.sem_inc(S("mm_out"), 1)
        add_rows("b2_added")

        def low(i, k, w2=False, last=False):
            slot = k // 2 + (W1_UNITS if w2 else 0)
            n, b = part(i, k, w2, last)
            dve.wait_ge(S("high_made"), n)
            V.tensor_tensor(split[:, b, 1, :], ring[:, slot, HALF * (k % 2):HALF * (k % 2) + HALF],
                            split[:, b, 0, :].bitcast(F32), ALU.subtract).then_inc(S("parts_made"), 1)

        def glu_sum(j):
            e = j % E
            n = j + 1
            bias = [b1T[:, bass.ds(e, 1), par:16:2].rearrange("p a c -> p (a c)").unsqueeze(2)
                    .to_broadcast([P, KC, SLOTS]) for par in range(2)]
            turned = [PS[:, 4 + par, :].rearrange("p (c s) -> p c s", c=KC) for par in range(2)]
            dve.wait_ge(S("hidden_turned"), n)
            V.tensor_tensor(glu[:], turned[0], bias[0], ALU.add).then_inc(S("glu_summed"), 1)
            V.tensor_tensor(lin[:], turned[1], bias[1], ALU.add).then_inc(S("lin_summed"), 1)
            dve.wait_ge(S("glu_summed"), n)
            V.tensor_scalar(glu[:], glu[:], LIMIT, None, ALU.min).then_inc(S("glu_ready"), 1)

        def glu_times_lin(j):
            n = j + 1
            dve.wait_ge(S("lin_summed"), n)
            V.tensor_scalar(lin[:], lin[:], LIMIT, -LIMIT, ALU.min, ALU.max).then_inc(S("lin_ready"), 1)
            dve.wait_ge(S("lin_ready"), n)
            dve.wait_ge(S("glu_ready"), n)
            V.scalar_tensor_tensor(out=lin[:], in0=lin[:], scalar=1.0, in1=glu[:], op0=ALU.add,
                                   op1=ALU.mult).then_inc(S("glu_lin_ready"), 1)

        def activate(j):
            n = j + 1
            dve.wait_ge(S("sig_ready"), n)
            dve.wait_ge(S("glu_lin_ready"), n)
            V.tensor_tensor(lin[:], lin[:], sig[:], ALU.mult).then_inc(S("act_full_ready"), 1)
            dve.wait_ge(S("act_full_ready"), n)
            V.tensor_copy(actr[:, :, 0, :], lin[:]).then_inc(S("act_high_ready"), 1)
            dve.wait_ge(S("act_high_ready"), n)
            V.tensor_tensor(actr[:, :, 1, :], lin[:], actr[:, :, 0, :].bitcast(F32),
                            ALU.subtract).then_inc(S("act_ready"), 1)

        def step(i, w1, w2, last=False):
            def lows(a, b, w2_=False):
                for k in range(a, b):
                    if w1 or w2_:
                        low(i, k, w2_, last)

            lows(0, 4)
            if w2:
                glu_sum(i - 1)
            lows(4, 5)
            if w2:
                glu_times_lin(i - 1)
            lows(5, 8)
            if w2:
                activate(i - 1)
            lows(8, PARTS_W1)
            if w2:
                lows(0, PARTS_W2, True)

        dve.wait_ge(S("tables_clear"), 1)
        step(0, True, False)
        step(1, True, True)
        nn = dve.value_load(more_i[0:1, 0:1], min_val=0, max_val=STEPS - E) + E
        with dve.Fori(2, nn) as i:
            step(i, True, True)
        step(nn, False, True, last=True)

    @blk.tensor
    def _(pe):
        product, turn = Banks(4), Banks(0)

        def into():
            bank = product.next()
            if product.n > 4:
                pe.wait_ge(S("mm_out"), product.n - 4)
            return bank

        def turn_into():
            bank = turn.next()
            if turn.n > 4:
                pe.wait_ge(S("turned_out"), turn.n - 4)
            return bank

        def turn_blocks(blocks, rows=P):
            bank = turn_into()
            for k, src in enumerate(blocks):
                ins = TE.transpose(bank[0:rows, P * k:P * k + P], src, ident[:])
            ins.then_inc(S("turned"), 1)

        def turn_rows(src):
            for t in range(NT):
                for half in range(2):
                    turn_blocks([src[:, t, P * c:P * c + P] for c in range(4 * half, 4 * half + 4)])

        def multiply(lhs, rhs, n, out_cols=None):
            bank = into()
            for c in range(n):
                l, r = lhs(c), rhs(c)
                ins = TE.matmul(bank[:, 0:r.shape[-1]], l, r, start=(c == 0), stop=(c == n - 1))
            ins.then_inc(S("mm_done"), 1)

        def rows(t):
            return lambda c: hT[:, c, t * P:(t + 1) * P]

        def signal(sem):
            pe.wait_ge(S("mm_done"), product.n)
            pe.sem_inc(S(sem), 1)

        pe.wait_ge(S("constants"), 1)
        pe.wait_ge(S("rows_ready"), 1)
        turn_rows(H)
        pe.wait_ge(S("turned_out"), 4)
        pe.wait_ge(S("w_mkv_in"), 16)
        for t in range(NT):
            multiply(rows(t), lambda c: wmkv[:, c, :], KC)
        signal("mem_projected")
        pe.wait_ge(S("rows_ready"), 2)
        turn_rows(H)
        pe.wait_ge(S("turned_out"), 8)

        def project(n):
            pe.wait_ge(S(f"w_in{n}_in"), 16)
            for t in range(NT):
                multiply(rows(t), lambda c: win[n][:, c, :], KC)

        project(0)
        project(1)
        pe.wait_ge(S("mem_keys_normed"), 1)
        turn_blocks([KVm[:, t, P * j:P * j + P] for j in range(2) for t in range(NT)])
        project(2)
        pe.wait_ge(S("latents_normed"), 1)
        cq0, ckv0 = COL["cq"][0], COL["ckv"][0]
        for t in range(NT):
            turn_blocks([proj[:, t, cq0 + P * c:cq0 + P * c + P] for c in range(3)])
        turn_blocks([proj[:, t, ckv0 + P * c:ckv0 + P * c + P] for c in range(2) for t in range(NT)])
        project(3)
        pe.wait_ge(S("turned_out"), turn.n)
        pe.wait_ge(S("w_uq_in"), 16)
        for t in range(NT):
            for half in range(2):
                multiply(lambda c: cqT[:, c, t * P:(t + 1) * P],
                         lambda c: wuq[:, c, 288 * half:288 * half + 288], 3)
        pe.wait_ge(S("w_ukv_in"), 16)
        for t in range(NT):
            for half in range(2):
                multiply(lambda c: ckvT[:, c, t * P:(t + 1) * P],
                         lambda c: wukv[:, c, 384 * half:384 * half + 384], 2)
        signal("latents_projected")
        project(4)
        pe.wait_ge(S("fox_normed"), 1)
        for w in range(2):
            turn_blocks([proj[:, t, 256 * w + P * j:256 * w + P * j + P] for j in range(2) for t in range(NT)])
        project(5)
        pe.wait_ge(S("mla_rotated"), 1)
        for w in range(2):
            for pair in range(3):
                turn_blocks([QKb[:, w, t, h, :] for h in (2 * pair, 2 * pair + 1) for t in range(NT)], QK)
        project(6)
        signal("projected")
        pe.wait_ge(S("logf_wide"), 1)
        bank = into()
        TE.matmul(bank[:, 0:4], U[:, 0, :], logf[:, 0, :], start=True, stop=True)
        TE.matmul(bank[:, 4:8], U[:, 2, :], logf[:, 0, :], start=True, stop=False)
        TE.matmul(bank[:, 4:8], U[:, 0, :], logf[:, 1, :], start=False, stop=True).then_inc(S("mm_done"), 1)
        for h in range(FOX_H):
            bank = into()
            TE.matmul(bank[:, 0:P], logfb[:, 0, h, :], U[:, 0, :], start=True, stop=True)
            TE.matmul(bank[:, P:2 * P], logfb[:, 0, h, :], U[:, 2, :], start=True, stop=False)
            TE.matmul(bank[:, P:2 * P], logfb[:, 1, h, :], U[:, 0, :], start=False,
                      stop=True).then_inc(S("mm_done"), 1)
        pe.wait_ge(S("dil_rotated"), 1)
        q0 = COL["qc"][0]
        for w in range(2):
            turn_blocks([proj[:, t, q0 + 384 * w + P * j:q0 + 384 * w + P * j + P] for j in range(2)
                         for t in range(NT)])
            turn_blocks([proj[:, t, q0 + 384 * w + 2 * P:q0 + 384 * w + 3 * P] for t in range(NT)])
        pe.wait_ge(S("turned_out"), turn.n)

        exped = [0]

        def attend(units_, cols):
            first = exped[0]
            turned_at = {}
            full = cols == 512
            for what, u in order(len(units_)):
                q, k, v, nb, scale, o_ap = units_[u]
                if what == "score":
                    bank = into()
                    TE.matmul(bank[:, 0:cols - 256], q[:, 0:P], k[:, 0:cols - 256], start=True, stop=True)
                    TE.matmul(bank[:, cols - 256:cols], q[:, P:2 * P], k[:, 0:256], start=True,
                              stop=True).then_inc(S("mm_done"), 1)
                if what == "turn":
                    pe.wait_ge(S("exped"), first + u + 1)
                    turn_blocks([Pb[:, u % 2, a:a + P] for a in range(0, cols, P)])
                    turned_at[u] = turn.n
                if what == "value":
                    pe.wait_ge(S("turned_out"), turned_at[u])
                    bank = into()
                    n0 = 2 if full else 1
                    for t, n_, at_ in ((0, n0, 0), (1, 2, n0)):
                        for c in range(n_):
                            a = P * (at_ + c)
                            ins = TE.matmul(bank[:, HD * t:HD * t + HD], PTb[:, u % 2, a:a + P], v[c],
                                            start=(c == 0), stop=(c == n_ - 1))
                    ins.then_inc(S("mm_done"), 1)
            exped[0] += len(units_)

        assert product.n == MM_SELF
        attend(SELF, 384)
        pe.wait_ge(S("rows_ready"), 3)
        turn_rows(H)
        pe.wait_ge(S("turned_out"), turn.n)
        pe.wait_ge(S("w_out_in"), 16)
        for t in range(NT):
            for half in range(2):
                multiply(rows(t), lambda c: wout[:, c, 512 * half:512 * half + 512], KC)
        signal("merged_out")
        pe.wait_ge(S("rows_ready"), 4)
        turn_rows(H)
        pe.wait_ge(S("turned_out"), turn.n)
        pe.wait_ge(S("w_mq_in"), 16)
        for t in range(NT):
            multiply(rows(t), lambda c: wmq[:, c, :], KC)
        signal("mem_queried")
        pe.wait_ge(S("mem_q_normed"), 1)
        turn_blocks([qm[:, t, P * j:P * j + P] for j in range(2) for t in range(NT)])
        pe.wait_ge(S("turned_out"), turn.n)
        assert product.n == MM_MEM
        attend(MEM, 512)
        pe.wait_ge(S("mem_attended"), 1)
        turn_blocks([om[:, t, P * j:P * j + P] for j in range(2) for t in range(NT)])
        pe.wait_ge(S("turned_out"), turn.n)
        pe.wait_ge(S("w_mo_in"), 16)
        for t in range(NT):
            for half in range(2):
                multiply(lambda c: omT[:, c, t * P:(t + 1) * P],
                         lambda c: wmo[:, c, 512 * half:512 * half + 512], 2)
        signal("mem_out")
        pe.wait_ge(S("h_ready"), 1)
        turn_rows(H)
        pe.wait_ge(S("turned_out"), turn.n)
        pe.sem_inc(S("h_turned"), 1)
        pe.wait_ge(S("router_in"), 16)
        for t in range(NT):
            multiply(rows(t), lambda c: router_w[:, c, :], KC)
        signal("routed")
        pe.wait_ge(S("mask_ready"), 1)
        mask = rt[:, 5]
        bank = into()
        TE.matmul(bank[:, 0:E], U[:, 1, :], mask[:, 0, 0:E], start=True, stop=True)
        TE.matmul(bank[:, E:2 * E], U[:, 2, :], mask[:, 0, 0:E], start=True, stop=False)
        TE.matmul(bank[:, E:2 * E], U[:, 1, :], mask[:, 1, 0:E], start=False, stop=True)
        TE.matmul(bank[:, 2 * E:3 * E], U[:, 2, :], mask[:, 0, 0:E], start=True, stop=False)
        TE.matmul(bank[:, 2 * E:3 * E], U[:, 2, :], mask[:, 1, 0:E], start=False,
                  stop=True).then_inc(S("mm_done"), 1)
        pe.wait_ge(S("gate_ready"), 1)
        turn_blocks([rt[:, 6, t, 0:E] for t in range(NT)], E)
        pe.wait_ge(S("b1_in"), 16)
        turn_blocks([b1s[:, 256 * c + par:256 * c + 256:2] for c in range(2) for par in range(2)])
        pe.wait_ge(S("turned_out"), turn.n)
        pe.wait_ge(S("b2_in"), 16)
        for t in range(NT):
            for half in range(2):
                multiply(lambda c: rt_gateT[:, t * P:(t + 1) * P],
                         lambda c: b2s[:, 512 * half:512 * half + 512], 1)

        def gather(i, c):
            if c == 0:
                pe.wait_ge(S("hot_made"), i + 1)
                if not (isinstance(i, int) and i < 2):
                    pe.wait_ge(S("act_ready"), i - 1)
            for w in range(2):
                a = P * (c % 4) + SLOTS * w
                for t in range(NT):
                    ins = TE.matmul(PS[:, 4 + c // 4, a:a + SLOTS], XR[:, w, t, P * c:P * c + P], hotr[:, t, :],
                                    start=(t == 0), stop=(t == NT - 1))
            if c == KC - 1:
                ins.then_inc(S("gathered"), 1)

        def turn_hot(j):
            pe.wait_ge(S("y_out"), j + 1)
            pe.wait_ge(S("hotg_made"), j + 1)
            for t in range(NT):
                ins = TE.transpose(PS[:, 6, t * P:(t + 1) * P], hotg[:, t, :], ident[:])
            ins.then_inc(S("hot_turned"), 1)

        def scatter(j, t):
            pe.wait_ge(S("hotT_out"), j + 1)
            if t:
                pe.wait_ge(S("given_out"), 2 * j + 1)
            for b in range(2):
                ins = TE.matmul(PS[:, 6 + b, :], hotT[:, t * P:(t + 1) * P], Ys[:, 512 * b:512 * b + 512],
                                start=True, stop=True)
            ins.then_inc(S("scattered"), 1)

        def multiply_parts(n, buf, left, bank, first, final):
            pe.wait_ge(S("parts_made"), n)
            for w in range(2):
                for b in range(2):
                    ins = TE.matmul(PS[:, bank + b, :], left.rearrange("p w s -> p (w s)"),
                                    split[:, buf, w, 512 * b:512 * b + 512],
                                    start=(first and w == 0), stop=(final and w == 1))
            ins.then_inc(S("parts_used"), 1)

        def turn_hidden(i, c):
            if c == 0:
                pe.wait_ge(S("hidden_out"), i + 1)
                pe.wait_ge(S("xg_parts_out"), i + 2)
            for par in range(2):
                ins = TE.matmul(PS[:, 4 + par, SLOTS * c:SLOTS * c + SLOTS],
                                Hs[:, 256 * c + par:256 * c + 256:2], stack[:], start=True, stop=True)
            if c == KC - 1:
                ins.then_inc(S("hidden_turned"), 1)

        def step(i, w1, w2, scat, last=False):
            if w1:
                pe.wait_ge(S("xg_parts_out"), i + 1)
                if not (isinstance(i, int) and i == 0):
                    pe.wait_ge(S("hidden_out"), i)
            for k in range(PARTS_W1):
                if w1:
                    multiply_parts(*part(i, k), xgr[:, k // 2], 2 * (k % 2), k < 2, k >= PARTS_W1 - 2)
                if scat and k == AT_TURN:
                    turn_hot(i - 2)
                if scat and k in AT_SCATTER:
                    scatter(i - 2, AT_SCATTER.index(k))
                if w1 and k >= PARTS_W1 - 1 - KC and k < PARTS_W1 - 1:
                    gather(i + 1, k - (PARTS_W1 - 1 - KC))
            if w2:
                pe.wait_ge(S("act_ready"), i)
                if scat:
                    pe.wait_ge(S("given_out"), 2 * (i - 1))
                for cc in range(KC):
                    multiply_parts(*part(i, cc, True, last), actr[:, cc], 6, cc == 0, cc == KC - 1)
                    if w1 and cc >= KC // 2:
                        turn_hidden(i, 2 * (cc - KC // 2))
                        turn_hidden(i, 2 * (cc - KC // 2) + 1)
            elif w1:
                for c in range(KC):
                    turn_hidden(i, c)

        pe.wait_ge(S("tables_clear"), 1)
        pe.wait_ge(S("h_used"), 1)
        pe.wait_ge(S("b2_added"), 1)
        pe.wait_ge(S("turned_out"), turn.n)
        for c in range(KC):
            gather(0, c)
        step(0, True, False, False)
        step(1, True, True, False)
        nn = pe.value_load(more_i[0:1, 0:1], min_val=0, max_val=STEPS - E) + E
        with pe.Fori(2, nn) as i:
            step(i, True, True, True)
        step(nn, False, True, True, last=True)
        turn_hot(nn - 1)
        scatter(nn - 1, 0)
        scatter(nn - 1, 1)

    block.__exit__(None, None, None)


_INS = ["x", "mem", "positions", "g_mix", "w_in", "b_forget", "g_qa", "g_ka", "g_cq", "g_ckv", "w_uq", "w_ukv",
        "g_qb", "g_kb", "g_qc", "g_kc", "g_group", "w_out", "g_xmem", "g_mem", "w_mq", "w_mkv", "g_qm", "g_km",
        "w_mo", "g_ffn", "w_router", "b_router", "w_e1", "b_e1", "w_e2", "b_e2"]
_OUTS = [((1, T, D), "float32")]


def kernel(**inputs):
    import numpy as _np
    import concourse.bacc as _bacc
    from concourse import mybir as _mybir
    from concourse.bass_utils import run_bass_kernel_spmd as _run

    nc = _bacc.Bacc("TRN2", target_bir_lowering=False, num_devices=1)
    arrays, args = {}, []
    for name in _INS:
        a = _np.ascontiguousarray(inputs[name])
        arrays[f"in_{name}_dram"] = a
        args.append(nc.dram_tensor(f"in_{name}_dram", a.shape, _mybir.dt.from_np(a.dtype), kind="ExternalInput").ap())
    for i, (shape, dtype) in enumerate(_OUTS):
        dt = _mybir.dt.from_np(_np.dtype(dtype))
        args.append(nc.dram_tensor(f"out_{i}_dram", shape, dt, kind="ExternalOutput").ap())
    build(nc, *args)
    r = _run(nc, [arrays], core_ids=[0])
    got = tuple(r.results[0][f"out_{i}_dram"] for i in range(len(_OUTS)))
    return got[0]
```

```python
import math

import numpy as np

import concourse.bass as bass
from concourse import mybir

F32 = mybir.dt.float32
F32R = mybir.dt.float32r
I32 = mybir.dt.int32
ALU = mybir.AluOpType
ACT = mybir.ActivationFunctionType
AX = mybir.AxisListType

P = 128
D = 1024
T = 256
NT = T // P
KC = D // P
HD = 64
FOX_H, MLA_H, DIL_H, MEM_H = 4, 6, 6, 4
Q_RANK, KV_RANK = 384, 256
NOPE, ROPE = 64, 32
QK = NOPE + ROPE
ROT = HD // 4
THETA = 500000.0
EPS = 1e-6
BIG = 1e30
E = 32
F = 1024
SLOTS = 64
MAX_ROUNDS = T // SLOTS
STEPS = E * MAX_ROUNDS
ALPHA, LIMIT = 1.702, 7.0

WIDTHS = [("qa", 256), ("ka", 256), ("va", 256), ("fa", 4), ("cq", Q_RANK), ("ckv", KV_RANK),
          ("kr", ROPE), ("qc", 384), ("kc", 384), ("vc", 384)]
COL = {}
_at = 0
for _name, _w in WIDTHS:
    COL[_name] = (_at, _at + _w)
    _at += _w
IN_W = _at
CHUNKS = [("cq", "cq", 65536), ("ckv", "kr", 77824), ("qa", "ka", 0), ("va", "fa", 16384),
          ("qc", "qc", 24704), ("kc", "kc", 36992), ("vc", "vc", 49280)]
CHUNKS = [(COL[a][0], COL[b][1], at) for a, b, at in CHUNKS]

UNIT = 2048
W1_UNITS, W2_UNITS = KC, F // P // 2
UNITS = W1_UNITS + W2_UNITS
MM_SELF = 29
FIRST = FOX_H + MLA_H
MM_MEM = 67
HALF = UNIT // 2
PARTS_W1, PARTS_W2 = 2 * W1_UNITS, 2 * W2_UNITS
PARTS = PARTS_W1 + PARTS_W2
BUFFERS = 6
assert PARTS % BUFFERS == 0
EARLY = 4
AT_TURN, AT_SCATTER, GIVE = 2, (4, 8), (10, 14)


def build(nc, x, mem, positions, g_mix, w_in, b_forget, g_qa, g_ka, g_cq, g_ckv, w_uq, w_ukv,
          g_qb, g_kb, g_qc, g_kc, g_group, w_out, g_xmem, g_mem, w_mq, w_mkv, g_qm, g_km,
          w_mo, g_ffn, w_router, b_router, w_e1, b_e1, w_e2, b_e2, out):
    base = 16512

    def at(name, shape, off, dt=F32):
        return nc.alloc_sbuf_tensor_at(name, shape, dt, offset=base + off)

    ring = at("ring", [P, UNITS, UNIT], 0)
    win = [at(f"w_in{n}", [P, KC, b - a], o) for n, (a, b, o) in enumerate(CHUNKS)]
    QKb = at("mla_qk", [P, 2, NT, MLA_H, QK], 87040)
    mlaT = at("mla_T", [P, 2, MLA_H, T], 65536)
    dilT = at("dil_T", [P, 2, 3, T], 77824)
    Vb = at("mla_v", [P, NT, MLA_H, HD], 83968)
    wout = at("w_out_sb", [P, KC, D], 0)
    R = UNITS * UNIT * 4
    X = at("x_sb", [P, NT, D], R)
    H = at("h_sb", [P, NT, D], R + 8192)
    hT = at("h_T", [P, KC, T], R + 16384)
    proj = at("proj", [P, NT, IN_W], R + 24576)
    gain = at("gains", [P, 2, D], R + 45376)
    SG = {}
    small_at = 0
    small_list = [("b_router", b_router), ("g_qa", g_qa), ("g_ka", g_ka), ("g_qc", g_qc), ("g_kc", g_kc), ("g_qm", g_qm),
                  ("g_km", g_km), ("g_cq", g_cq), ("g_ckv", g_ckv), ("g_qb", g_qb), ("g_kb", g_kb),
                  ("b_forget", b_forget)]
    smalls = at("small_gains", [P, 1256], R + 53568)
    for n_, a_ in small_list:
        SG[n_] = smalls[:, small_at:small_at + a_.shape[-1]]
        small_at += a_.shape[-1]
    wuq = at("w_uq_sb", [P, 3, MLA_H * QK], R + 58592)
    rtmp = at("rope_tmp", [P, 2, 2, MLA_H, ROPE], R + 58592)
    wukv = at("w_ukv_sb", [P, 2, MLA_H * 128], R + 65504)
    wmkv = at("w_mkv_sb", [P, KC, 512], R + 71648)
    cqT = at("cq_T", [P, 3, T], R + 71648)
    ckvT = at("ckv_T", [P, 2, T], R + 74720)
    foxNB = at("fox_bias", [P, FOX_H, 384], R + 76768)
    foxT = at("fox_T", [P, 2, 2, T], R + 82912)
    KVm = at("mem_kv", [P, NT, 512], R + 88032)
    memT = at("mem_kT", [P, 2, T], R + 92128)
    NBs = at("mask_bias", [P, 2, 384], R + 94176)
    SCR = at("scratch", [P, 3072], R + 97248)
    Sb, Pb, PTb = (SCR[:, 1024 * k:1024 * k + 1024].rearrange("p (b n) -> p b n", b=2) for k in range(3))
    rope = at("rope_tab", [P, 8, NT, 16], R + 109536)
    U = at("upper", [P, 3, P], R + 110560)
    ident = at("ident", [P, P], R + 113888)
    stat = at("stat", [P, 448], R + 112096)
    wmq = at("w_mq_sb", [P, KC, 256], R + 65504)
    wmo = at("w_mo_sb", [P, 2, D], R + 24576)
    qm = at("mem_q", [P, NT, 256], R + 32768)
    qmT = at("mem_qT", [P, 2, T], R + 34816)
    om = at("mem_o", [P, NT, 256], R + 36864)
    omT = at("mem_oT", [P, 2, T], R + 38912)
    router_w = at("w_router_sb", [P, KC, E], R + 43136)
    slot_of = at("slot_table", [P, NT, STEPS + 4], R + 8192)
    gate_of = at("gate_table", [P, NT, STEPS + 4], R + 9248)
    iota = at("iota", [P, P], R + 10304)
    pick = at("picked", [P, 3, NT], R + 10816)
    hotg = at("hot_gate", [P, NT, P], R + 11840)
    hotr = at("hot_r", [P, NT, SLOTS], R + 12864, F32R)
    hotT = at("hot_gate_T", [P, T], R + 13376)
    rt = at("route", [P, 12, NT, 36], R + 16384)
    Ys = at("y_sb", [P, D], R + 14400)
    given = at("given", [P, D], R + 18496)
    b1s = at("b1_rows", [P, 512], R + 19840)
    b1T = at("b1_T", [P, E, 16], R + 22592)
    XR = at("h_parts", [P, 2, NT, D], R + 24640, F32R)
    split = at("w_parts", [P, BUFFERS, 2, HALF], R + 41024, F32R)
    xgr = at("xg_parts", [P, KC, 2, SLOTS], R + 90176, F32R)
    Hs = at("hidden", [P, 2 * F], R + 94272)
    glu = at("glu", [P, KC, SLOTS], R + 102464)
    lin = at("lin", [P, KC, SLOTS], R + 104512)
    actr = at("act_parts", [P, KC, 2, SLOTS], R + 106560, F32R)
    sig = at("sig", [P, KC, SLOTS], R + 110656)
    stack = at("stacked_ident", [P, SLOTS], R + 112704)
    more_i = at("more_steps", [P, 1], R + 112960, I32)
    b2s = at("b2_sb", [E, D], R + 104448)
    PS = nc.alloc_psum_tensor("banks", [P, 8, 512], F32)

    sems = {}

    def S(name):
        if name not in sems:
            sems[name] = nc.alloc_semaphore(name)
        return sems[name]

    V, G, A, TE = nc.vector, nc.gpsimd, nc.scalar, nc.tensor

    REQ = [2, 2, 8, 4, 16, 24, 24, 4, 2, 1, 1, 4, 4, 1, 1]
    NREQ = sum(REQ)

    def cols_of(kind, k):
        a = kind * NREQ + sum(REQ[:k])
        return stat[:, a:a + REQ[k]]

    o = 4 * NREQ
    rowmax, rowsum, rowinv = stat[:, o:o + 4], stat[:, o + 4:o + 12], stat[:, o + 12:o + 16]
    logf, fz, fa2, cumq, fe = (stat[:, o + 16 + 8 * k:o + 24 + 8 * k].rearrange("p (t h) -> p t h", t=2)
                               for k in range(5))
    rowtmp = stat[:, 3 * NREQ:3 * NREQ + 4]
    logfb = SCR[:, 0:1024].rearrange("p (t h m) -> p t h m", t=2, h=4)

    def units():
        for h in range(FOX_H):
            r, j = 64 * (h % 2), h // 2
            yield (foxT[r:r + 64, 0, j, :], foxT[r:r + 64, 1, j, :],
                   [proj[:, t, COL["va"][0] + 64 * h:COL["va"][0] + 64 * h + 64] for t in range(NT)],
                   foxNB[:, h, :], HD ** -0.5, H[:, :, 64 * h:64 * h + 64])
        for h in range(MLA_H):
            yield (mlaT[0:QK, 0, h, :], mlaT[0:QK, 1, h, :], [Vb[:, t, h, :] for t in range(NT)],
                   NBs[:, 0, :], QK ** -0.5, H[:, :, 256 + 64 * h:320 + 64 * h])
        for h in range(DIL_H):
            r, j = 64 * (h % 2), h // 2
            yield (dilT[r:r + 64, 0, j, :], dilT[r:r + 64, 1, j, :],
                   [proj[:, t, COL["vc"][0] + 64 * h:COL["vc"][0] + 64 * h + 64] for t in range(NT)],
                   NBs[:, 1, :], HD ** -0.5, H[:, :, 640 + 64 * h:704 + 64 * h])

    SELF = list(units())
    MEM = [(qmT[64 * (h % 2):64 * (h % 2) + 64, h // 2, :], memT[64 * (h % 2):64 * (h % 2) + 64, h // 2, :],
            [KVm[:, t, 256 + 64 * h:320 + 64 * h] for t in range(NT)], None, HD ** -0.5,
            om[:, :, 64 * h:64 * h + 64]) for h in range(MEM_H)]

    memx = at("mem_sb", [P, NT, D], R + 24576 + 12288)
    mtmp = at("mask_tmp", [P, 8, 384], R + 24576)
    mtmp_i = at("mask_tmp_int", [P, 8, 384], R + 24576, I32)
    rope_i = at("rope_int", [P, 8, NT, 16], R + 109536, I32)
    pos_i = rope_i[:, 5, 0, 0:NT]
    rt_gateT = at("gate_T", [E, T], R + 16384 + 8 * 72 * 4)

    def order(n):
        for s in range(n + 3):
            if s < n:
                yield "score", s
            if 0 <= s - 2 < n:
                yield "turn", s - 2
            if 0 <= s - 3 < n:
                yield "value", s - 3

    class Banks:

        def __init__(self, first):
            self.first, self.n = first, 0

        def next(self):
            self.n += 1
            return PS[:, self.first + (self.n - 1) % 4, :]

    def heads(ap, h):
        return ap.rearrange("p t (h d) -> p t h d", h=h)

    def part(i, k, w2=False, last=False):
        if isinstance(i, int) and i == 0:
            return k + 1, (k - EARLY) % BUFFERS
        k += PARTS_W1 if w2 and not last else 0
        return PARTS * i - PARTS_W2 + k + 1, (k - PARTS_W2 - EARLY) % BUFFERS

    block = nc.Block()
    blk = block.__enter__()

    @blk.sync
    def _(sp):
        sp.dma_start(memx[:], mem[0].rearrange("(t p) d -> p t d", p=P)).then_inc(S("mem_in"), 16)
        sp.dma_start(X[:], x[0].rearrange("(t p) d -> p t d", p=P)).then_inc(S("x_in"), 16)
        sp.dma_start(wmkv[:], w_mkv[0].rearrange("(c p) n -> p c n", p=P)).then_inc(S("w_mkv_in"), 16)
        w_in_v = w_in[0].rearrange("(c p) n -> p c n", p=P)
        for n, (a, b, _) in enumerate(CHUNKS):
            sp.dma_start(win[n][:], w_in_v[:, :, a:b]).then_inc(S(f"w_in{n}_in"), 16)
            if n == 2:
                sp.dma_start(wuq[:], w_uq[0].rearrange("(c p) n -> p c n", p=P)).then_inc(S("w_uq_in"), 16)
                sp.dma_start(wukv[:], w_ukv[0].rearrange("(c p) n -> p c n", p=P)).then_inc(S("w_ukv_in"), 16)
        sp.wait_ge(S("projected"), 1)
        sp.dma_start(wout[:], w_out[0].rearrange("(c p) n -> p c n", p=P)).then_inc(S("w_out_in"), 16)
        sp.dma_start(wmq[:], w_mq[0].rearrange("(c p) n -> p c n", p=P)).then_inc(S("w_mq_in"), 16)

        def load_w1(e, c):
            sp.dma_start(ring[:, c, :], w1_v[e, c]).then_inc(S(f"landed{c}"), 16)

        def load_w2(e, k):
            sp.dma_start(ring[:, W1_UNITS + k, :].rearrange("p (j n) -> p j n", j=2),
                         w2_v[e, k]).then_inc(S(f"landed{W1_UNITS + k}"), 16)

        def w1_free(j, c):
            sp.wait_ge(S("parts_made"), part(j, 2 * c + 1)[0])

        w1_v = w_e1[0].rearrange("e (c p) n -> e c p n", p=P)
        w2_v = w_e2[0].rearrange("e (k j p) n -> e k p j n", p=P, j=2)
        sp.wait_ge(S("self_done"), 2)
        sp.dma_start(wmo[:], w_mo[0].rearrange("(c p) n -> p c n", p=P)).then_inc(S("w_mo_in"), 16)
        sp.dma_start(router_w[:], w_router[0].rearrange("(c p) n -> p c n", p=P)).then_inc(S("router_in"), 16)
        for c in range(4, W1_UNITS):
            load_w1(0, c)
        for k in range(W2_UNITS):
            load_w2(0, k)
        sp.wait_ge(S("merged_out"), NT)
        for c in range(4):
            load_w1(0, c)
        for c in range(EARLY // 2):
            w1_free(0, c)
            load_w1(1, c)
        sp.wait_ge(S("routed"), NT)
        sp.dma_start(b1s[:], b_e1[0].rearrange("e (q n) -> (e q) n", q=4)).then_inc(S("b1_in"), 16)
        sp.dma_start(b2s[:], b_e2[0]).then_inc(S("b2_in"), 16)

        for c in range(EARLY // 2, W1_UNITS):
            w1_free(0, c)
            load_w1(1, c)

        sp.wait_ge(S("more_known"), 1)
        n = sp.value_load(more_i[0:1, 0:1], min_val=0, max_val=STEPS - E) + E
        with sp.Fori(1, n - 1) as j:
            for c in range(W1_UNITS):
                w1_free(j, c)
                load_w1(bass.ds((j + 1) % E, 1), c)
            for k in range(W2_UNITS):
                sp.wait_ge(S("parts_made"), part(j, 2 * k + 1, True)[0])
                load_w2(bass.ds(j % E, 1), k)
        for k in range(W2_UNITS):
            sp.wait_ge(S("parts_made"), part(n - 1, 2 * k + 1, True)[0])
            load_w2(E - 1, k)
        for t in range(NT):
            sp.wait_ge(S("tile_done"), t + 1)
            sp.dma_start(out[0, t * P:(t + 1) * P, :], X[:, t, :]).then_inc(S("stored"), 16)
        sp.wait_ge(S("stored"), 16 * NT)

    @blk.gpsimd
    def _(pool):
        n = [0]

        def link(ins):
            n[0] += 1
            ins.then_inc(S("pool_chain"), 1)
            pool.wait_ge(S("pool_chain"), n[0])

        inv = rope[:, 7, 0, :]
        for i in range(16):
            f = float(np.float32(THETA) ** np.float32(-2 * i / 32))
            G.memset(inv[:, i:i + 1], f)
        G.memset(U[:], 1.0)
        G.memset(NBs[:, 0, :], 0.0)
        G.memset(mtmp[:, 3, :], 1.0)
        G.iota(mtmp_i[:, 0, 0:P], pattern=[[-1, P]], base=1024, channel_multiplier=1)
        G.iota(mtmp_i[:, 0, P:3 * P], pattern=[[-1, 2 * P]], base=1024 + P, channel_multiplier=1)
        link(G.memset(ident[:], 0.0))
        G.affine_select(out=ident[:], in_=ident[:], pattern=[[-1, P]], compare_op=ALU.not_equal, fill=1.0,
                        base=0, channel_multiplier=1)
        G.affine_select(out=NBs[:, 0, 0:P], in_=NBs[:, 0, 0:P], pattern=[[-1, P]], compare_op=ALU.is_ge,
                        fill=BIG, base=0, channel_multiplier=1)
        G.affine_select(out=NBs[:, 0, P:], in_=NBs[:, 0, P:], pattern=[[-1, 2 * P]], compare_op=ALU.is_ge,
                        fill=BIG, base=P, channel_multiplier=1)
        G.affine_select(out=mtmp[:, 3, P:], in_=mtmp[:, 3, P:], pattern=[[1, 2 * P]], compare_op=ALU.is_ge,
                        fill=0.0, base=0, channel_multiplier=-1)
        G.affine_select(out=U[:, 0, :], in_=U[:, 0, :], pattern=[[1, P]], compare_op=ALU.is_ge, fill=0.0,
                        base=0, channel_multiplier=-1)
        G.affine_select(out=U[:, 1, :], in_=U[:, 1, :], pattern=[[1, P]], compare_op=ALU.is_ge, fill=0.0,
                        base=-1, channel_multiplier=-1).then_inc(S("constants"), 1)

        def rotate(xv, cosv, sinv, a, b, width):
            half = width // 2
            G.tensor_tensor(a, xv, cosv, ALU.mult)
            link(G.tensor_tensor(b, xv, sinv, ALU.mult))
            G.tensor_tensor(xv[:, :, 0, :], a[:, :, 0, :], b[:, :, 1, :], ALU.subtract)
            return G.tensor_tensor(xv[:, :, 1, :], a[:, :, 1, :], b[:, :, 0, :], ALU.add)

        pool.wait_ge(S("rope_tables"), 1)
        pool.wait_ge(S("mla_normed"), 1)
        for w in range(2):
            for t in range(NT):
                xv = QKb[:, w, t, :, NOPE:].rearrange("p h (a r) -> p h a r", a=2)
                cosv, sinv = (rope[:, k, t, :].unsqueeze(1).unsqueeze(1).to_broadcast([P, MLA_H, 2, 16])
                              for k in (6, 4))
                a, b = (rtmp[:, k, (2 * w + t) % 2].rearrange("p h (a r) -> p h a r", a=2) for k in (0, 1))
                last = rotate(xv, cosv, sinv, a, b, 32)
                if (w, t) == (1, 1):
                    last.then_inc(S("mla_rotated"), 1)
                else:
                    link(last)
        pool.wait_ge(S("dil_normed"), 1)
        pool.wait_ge(S("mla_rotated"), 1)
        q0 = COL["qc"][0]
        for t in range(NT):
            xv = proj[:, t, q0:q0 + 768].rearrange("p (h d) -> p h d", d=HD)[:, :, 0:ROT] \
                .rearrange("p h (a r) -> p h a r", a=2)
            cosv, sinv = (rope[:, k, t, 0:16:2].unsqueeze(1).unsqueeze(1).to_broadcast([P, 12, 2, 8])
                          for k in (6, 4))
            a, b = (rtmp[:, k, t].rearrange("p h r -> p (h r)").rearrange("p (h a r) -> p h a r", a=2, r=8)
                    for k in (0, 1))
            last = rotate(xv, cosv, sinv, a, b, 16)
            if t == 1:
                last.then_inc(S("dil_rotated"), 1)
            else:
                link(last)

        pool.wait_ge(S("h_used"), 1)
        pool.wait_ge(S("h_turned"), 1)
        G.iota(iota[:], pattern=[[0, 2], [1, SLOTS]], base=0, channel_multiplier=0,
               allow_small_or_imprecise_dtypes=True)
        G.memset(slot_of[:], -5.0)
        G.memset(gate_of[:], 0.0)
        pool.wait_ge(S("routed"), NT)
        G.tensor_tensor(stack[:], ident[:, 0:SLOTS], ident[:, SLOTS:], ALU.add).then_inc(S("tables_clear"), 1)
        pool.wait_ge(S("tables_clear"), 1)
        pool.wait_ge(S("tables_made"), 1)

        def hot_for_gather(i):
            if not (isinstance(i, int) and i == 0):
                pool.wait_ge(S("gathered"), i)
            G.tensor_copy(pick[:, 0, :], slot_of[:, :, bass.ds(i, 1)].rearrange("p t a -> p (t a)"))
            pool.drain()
            for t in range(NT):
                ins = G.tensor_scalar(hotr[:, t, :], iota[:, 0:SLOTS], pick[:, 0, t:t + 1], None, ALU.is_equal)
            ins.then_inc(S("hot_made"), 1)

        def hot_for_scatter(i, first=False):
            if not first:
                pool.wait_ge(S("hot_turned"), i)
            G.tensor_copy(pick[:, 1, :], slot_of[:, :, bass.ds(i, 1)].rearrange("p t a -> p (t a)"))
            G.tensor_copy(pick[:, 2, :], gate_of[:, :, bass.ds(i, 1)].rearrange("p t a -> p (t a)"))
            pool.drain()
            for t in range(NT):
                ins = G.tensor_scalar(hotg[:, t, :], iota[:], pick[:, 1, t:t + 1], pick[:, 2, t:t + 1],
                                      ALU.is_equal, ALU.mult)
            ins.then_inc(S("hotg_made"), 1)

        hot_for_gather(0)
        hot_for_gather(1)
        hot_for_gather(2)
        hot_for_scatter(0, first=True)
        pool.wait_ge(S("b2_added"), NT)

        def add(j, t):
            pool.wait_ge(S("given_out"), 2 * j + t + 1)
            G.tensor_tensor(X[:, t, :], X[:, t, :], given[:], ALU.add).then_inc(S("added"), 1)

        nn = pool.value_load(more_i[0:1, 0:1], min_val=0, max_val=STEPS - E) + E
        with pool.Fori(2, nn) as i:
            hot_for_gather(i + 1)
            hot_for_scatter(i - 1)
            for t in range(NT):
                add(i - 2, t)
        hot_for_scatter(nn - 1)
        for t in range(NT):
            add(nn - 2, t)

    @blk.scalar
    def _(act):
        turned = Banks(0)
        squares_n = [0]

        act.dma_start(pos_i[:], positions[0].rearrange("(t p) -> p t", p=P),
                      allow_slow_non_contiguous=True).then_inc(S("pos_in"), 16)
        act.dma_start(gain[:, 0, :], g_mem[0].partition_broadcast(P)).then_inc(S("g_mem_in"), 16)
        act.dma_start(gain[:, 1, :], g_mix[0].partition_broadcast(P)).then_inc(S("g_mix_in"), 16)

        def leave(out_ap, k, cols, rows=P):
            src = turned.next()
            act.wait_ge(S("turned"), turned.n)
            A.copy(out_ap, src[0:rows, 0:cols] if k is None else
                   src[0:rows, 0:cols].rearrange("p (a b) -> p a b", a=k)).then_inc(S("turned_out"), 1)

        def square(pieces):
            if squares_n[0]:
                act.wait_ge(S("squared"), squares_n[0])
            squares_n[0] += 1
            for out_ap, in_ap, col in pieces:
                ins = A.activation(out_ap, in_ap, ACT.Square, accum_out=col) if col is not None else \
                    A.activation(out_ap, in_ap, ACT.Square)
            ins.then_inc(S("squared"), 1)

        def square_tile(src, t, col):
            return SCR[:, 1024 * t:1024 * t + 1024], src[:, t, :], col

        def turned_rows(tiles=range(NT)):
            for t in tiles:
                for half in range(2):
                    leave(hT[:, 4 * half:4 * half + 4, t * P:(t + 1) * P], 4, 512)

        act.wait_ge(S("mem_in"), 16)
        square([square_tile(memx, t, cols_of(0, 0)[:, t:t + 1]) for t in range(NT)])
        act.wait_ge(S("x_in"), 16)
        square([square_tile(X, t, cols_of(0, 1)[:, t:t + 1]) for t in range(NT)])
        for name, a in small_list:
            act.dma_start(SG[name], a[0].partition_broadcast(P)).then_inc(S("smalls_in"), 16)
        act.wait_ge(S("angles"), 1)
        A.activation(rope[:, 5], rope[:, 3], ACT.Sin, scale=0.5)
        A.activation(rope[:, 4], rope[:, 3], ACT.Sin).then_inc(S("sines"), 1)
        turned_rows()
        act.dma_start(gain[:, 0, :], g_group[0].partition_broadcast(P)).then_inc(S("g_group_in"), 16)
        act.wait_ge(S("mem_kv_ready"), 1)
        square([(SCR[:, 0:512].rearrange("p (t n) -> p t n", t=2), KVm[:, :, 0:256], None)])
        act.wait_ge(S("mem_projected"), 1)
        turned_rows()
        act.dma_start(gain[:, 1, :], g_xmem[0].partition_broadcast(P)).then_inc(S("g_xmem_in"), 16)
        leave(memT[:], 2, 512)
        act.wait_ge(S("latents_ready"), 1)
        act.wait_ge(S("squares_read"), 1)
        pieces = []
        for t in range(NT):
            pieces.append((SCR[:, 512 * t:512 * t + Q_RANK], proj[:, t, COL["cq"][0]:COL["cq"][1]],
                           cols_of(0, 3)[:, t:t + 1]))
            pieces.append((SCR[:, 1024 + 512 * t:1024 + 512 * t + KV_RANK],
                           proj[:, t, COL["ckv"][0]:COL["ckv"][1]], cols_of(0, 3)[:, 2 + t:3 + t]))
        square(pieces)
        act.wait_ge(S("mem_projected"), 1)
        for t in range(NT):
            leave(cqT[:, :, t * P:(t + 1) * P], 3, Q_RANK)
        leave(ckvT[:], 2, 512)
        act.wait_ge(S("fox_ready"), 1)
        square([(SCR[:, 0:1024].rearrange("p (t n) -> p t n", t=2), proj[:, :, 0:512], None)])
        act.wait_ge(S("forget_abs"), 1)
        A.activation(fe, fe, ACT.Exp, scale=-1.0).then_inc(S("forget_exped"), 1)
        act.wait_ge(S("forget_exped"), 1)
        A.activation(fe, fe, ACT.Ln, bias=1.0).then_inc(S("forget_log"), 1)
        act.wait_ge(S("mla_ready"), 1)
        act.wait_ge(S("squares_read"), 2)
        square([(SCR[:, 0:2304], QKb[:].rearrange("p w t h d -> p (w t h d)"), None)])
        leave(foxT[:, 0], 2, 512)
        leave(foxT[:, 1], 2, 512)
        act.wait_ge(S("dil_ready"), 1)
        act.wait_ge(S("squares_read"), 3)
        square([(SCR[:, 0:1536].rearrange("p (t n) -> p t n", t=2), proj[:, :, COL["qc"][0]:COL["kc"][1]], None)])
        act.wait_ge(S("latents_projected"), 1)
        for w in range(2):
            for pair in range(3):
                leave(mlaT[0:QK, w, 2 * pair:2 * pair + 2, :], 2, 512, QK)

        scored = [0]

        def attend(units_, cols, mm_before):
            mm, at_value = mm_before, {}
            for what, u in order(len(units_)):
                if what != "turn":
                    mm += 1
                if what == "value":
                    at_value[u] = mm
            spans = [(0, cols - 256), (cols - 256, cols)]
            for s in range(len(units_) + 2):
                if 0 <= s - 2 < len(units_):
                    if s - 4 >= 0:
                        act.wait_ge(S("mm_done"), at_value[s - 4])
                    leave(PTb[:, s % 2, 0:cols], None, cols)
                if s < len(units_):
                    scored[0] += 1
                    act.wait_ge(S("scored"), scored[0])
                    if s >= 2:
                        act.wait_ge(S("turned"), turned.n)
                    for t, (a, b) in enumerate(spans):
                        c = 2 * (s % 2) + t
                        ins = A.activation(Pb[:, s % 2, a:b], Sb[:, s % 2, a:b], ACT.Exp,
                                           bias=rowmax[:, c:c + 1], accum_out=rowsum[:, 2 * (s % 4) + t:2 * (s % 4) + t + 1])
                    ins.then_inc(S("exped"), 1)

        def high(i, k, w2=False, last=False):
            slot = k // 2 + (W1_UNITS if w2 else 0)
            n, b = part(i, k, w2, last)
            act.wait_ge(S(f"landed{slot}"), 16 * (i if w2 else i + 1))
            if not isinstance(n, int) or n > BUFFERS:
                act.wait_ge(S("parts_used"), n - BUFFERS)
            A.copy(split[:, b, 0, :], ring[:, slot, HALF * (k % 2):HALF * (k % 2) + HALF]) \
                .then_inc(S("high_made"), 1)

        act.wait_ge(S("fox_bias_made"), 1)
        attend(SELF[:FIRST], 384, MM_SELF)
        act.wait_ge(S("mm_done"), MM_SELF + 2 * FIRST)
        for w in range(2):
            leave(dilT[:, w, 0:2, :], 2, 512)
            leave(dilT[:, w, 2, :], None, 256)
        groups = ((0, 256), (256, 640), (640, 1024))
        junk = foxNB[:].rearrange("p h n -> p (h n)")
        act.wait_ge(S("self_done"), 1)
        square([(junk[:, 640 * t + a:640 * t + b], H[:, t, a:b], cols_of(0, 7)[:, 2 * k + t:2 * k + t + 1])
                for t in range(NT) for k, (a, b) in enumerate(groups[:2])])
        attend(SELF[FIRST:], 384, MM_SELF + 2 * FIRST)
        act.wait_ge(S("self_done"), 2)
        square([(junk[:, 384 * t:384 * t + 384], H[:, t, 640:1024], cols_of(0, 8)[:, t:t + 1])
                for t in range(NT)])
        for t in range(NT):
            leave(hT[:, 0:4, t * P:(t + 1) * P], 4, 512)
            leave(hT[:, 4, t * P:(t + 1) * P], None, P)
        for t in range(NT):
            leave(hT[:, 5:8, t * P:(t + 1) * P], 3, 384)
        act.dma_start(gain[:, 0, :], g_ffn[0].partition_broadcast(P)).then_inc(S("g_ffn_in"), 16)
        for t in range(NT):
            act.wait_ge(S("x1_ready"), t + 1)
            square([square_tile(X, t, cols_of(0, 9 + t))])
        for t in range(NT):
            act.wait_ge(S("merged_out"), t + 1)
            turned_rows([t])
        for t in range(NT):
            act.wait_ge(S("mem_q_ready"), t + 1)
            square([(SCR[:, 256 * t:256 * t + 256], qm[:, t, :], None)])
        for t in range(NT):
            leave(qmT[:, :, t * P:(t + 1) * P], 2, 256)
        attend(MEM, 512, MM_MEM)
        leave(omT[:], 2, 512)
        for k in range(EARLY):
            high(0, k)
        for t in range(NT):
            act.wait_ge(S("x2_ready"), t + 1)
            square([square_tile(X, t, cols_of(0, 13 + t))])
        for t in range(NT):
            turned_rows([t])
        act.wait_ge(S("h_ready"), NT)
        for t in range(NT):
            ins = A.copy(XR[:, 0, t, :], H[:, t, :])
        ins.then_inc(S("h_high"), 1)
        act.wait_ge(S("logits_ready"), 1)
        for t in range(NT):
            ins = A.activation(rt[:, 4, t, 0:E], rt[:, 0, t, 0:E], ACT.Exp, bias=rt[:, 2, t, 0:1])
        ins.then_inc(S("gates_exped"), 1)
        leave(rt_gateT[:], None, 256, E)
        leave(b1T[:].rearrange("p e (q k) -> p k (e q)", q=4), 4, 512)

        def y_leaves(j, last=False):
            act.wait_ge(S("parts_used"), part(j + 1, PARTS_W2 - 1, True, last)[0])
            if not (isinstance(j, int) and j == 0):
                act.wait_ge(S("scattered"), 2 * j)
            A.copy(Ys[:], PS[:, 6:8, :].rearrange("p b n -> p (b n)")).then_inc(S("y_out"), 1)

        def hot_leaves(j):
            act.wait_ge(S("hot_turned"), j + 1)
            A.copy(hotT[:], PS[:, 6, 0:T]).then_inc(S("hotT_out"), 1)

        def given_leaves(j, t):
            act.wait_ge(S("scattered"), 2 * j + t + 1)
            if t or not (isinstance(j, int) and j == 0):
                act.wait_ge(S("added"), 2 * j + t)
            A.copy(given[:], PS[:, 6:8, :].rearrange("p b n -> p (b n)")).then_inc(S("given_out"), 1)

        def step(i, w1, w2, scat, last=False):
            def highs(a, b, w2_=False):
                for k in range(a, b):
                    done = {0: BUFFERS, 1: 0 if w2_ else 5}.get(i, 0) if isinstance(i, int) else 0
                    if (w1 or w2_) and k >= done:
                        high(i, k, w2_, last)

            highs(0, 5)
            if scat:
                y_leaves(i - 2)
            at = 8 if isinstance(i, int) and i == 1 else 6
            highs(5, at)
            if w2:
                act.wait_ge(S("glu_ready"), i)
                A.activation(sig[:], glu[:], ACT.Sigmoid, scale=ALPHA).then_inc(S("sig_ready"), 1)
            highs(at, 7)
            if scat:
                hot_leaves(i - 2)
            highs(max(at, 7), GIVE[0])
            if last:
                highs(0, 3, True)
            if scat:
                given_leaves(i - 2, 0)
            highs(GIVE[0], GIVE[1])
            if last:
                highs(3, BUFFERS, True)
            if scat:
                given_leaves(i - 2, 1)
            highs(GIVE[1], PARTS_W1)
            if last:
                highs(BUFFERS, PARTS_W2, True)
            elif w2:
                highs(0, 5, True)
            elif w1:
                for k in range(5):
                    high(1, k)
            if w1:
                act.wait_ge(S("parts_used"), part(i, PARTS_W1 - 1)[0])
                if not (isinstance(i, int) and i == 0):
                    act.wait_ge(S("hidden_turned"), i)
                A.copy(Hs[:], PS[:, 0:4, :].rearrange("p b n -> p (b n)")).then_inc(S("hidden_out"), 1)
                act.wait_ge(S("gathered"), i + 2)
                A.copy(xgr[:].rearrange("p c w s -> p (c w s)"),
                       PS[:, 4:6, :].rearrange("p b n -> p (b n)")).then_inc(S("xg_parts_out"), 1)
            if w2 and not last:
                highs(5, PARTS_W2, True)

        for k in range(EARLY, BUFFERS):
            high(0, k)
        act.wait_ge(S("gathered"), 1)
        A.copy(xgr[:].rearrange("p c w s -> p (c w s)"),
               PS[:, 4:6, :].rearrange("p b n -> p (b n)")).then_inc(S("xg_parts_out"), 1)
        step(0, True, False, False)
        step(1, True, True, False)
        nn = act.value_load(more_i[0:1, 0:1], min_val=0, max_val=STEPS - E) + E
        with act.Fori(2, nn) as i:
            step(i, True, True, True)
        step(nn, False, True, True, last=True)
        y_leaves(nn - 1, last=True)
        hot_leaves(nn - 1)

    @blk.vector
    def _(dve):
        product = Banks(4)
        chain = [0]
        req = [0]

        def link(ins):
            chain[0] += 1
            ins.then_inc(S("dve_chain"), 1)
            dve.wait_ge(S("dve_chain"), chain[0])

        def take():
            bank = product.next()
            dve.wait_ge(S("mm_done"), product.n)
            return bank

        def leave(out_ap, in_ap):
            V.tensor_copy(out_ap, in_ap).then_inc(S("mm_out"), 1)

        def after_leaving():
            dve.wait_ge(S("mm_out"), product.n)

        def roots(parts):
            k = req[0]
            req[0] += 1
            ss, v, y, w = (cols_of(kind, k) for kind in range(4))
            v_bits, y_bits, w_bits = (ap.bitcast(I32) for ap in (v, y, w))
            for a, b, count in parts:
                ins = V.tensor_scalar(v[:, a:b], ss[:, a:b], 1.0 / count, EPS, ALU.mult, ALU.add)
            link(ins)
            link(V.tensor_scalar(w_bits, v_bits, 1, None, ALU.logical_shift_right))
            link(V.tensor_scalar(y_bits, w_bits, -1.0, float(0x5f3759df), ALU.mult, ALU.add))
            for _ in range(3):
                link(V.tensor_tensor(w, y, y, ALU.mult))
                link(V.scalar_tensor_tensor(out=w, in0=w, scalar=-0.5, in1=v, op0=ALU.mult, op1=ALU.mult))
                link(V.scalar_tensor_tensor(out=y, in0=w, scalar=1.5, in1=y, op0=ALU.add, op1=ALU.mult))
            return y

        def squared():
            dve.wait_ge(S("squared"), req[0] + 1)

        def norm_rows(src, y, g, sem, tiles=range(NT)):
            for t in tiles:
                ins = V.scalar_tensor_tensor(out=H[:, t, :], in0=src[:, t, :], scalar=y[:, t - tiles[0]:t - tiles[0] + 1],
                                             in1=gain[:, g, :], op0=ALU.mult, op1=ALU.mult)
            ins.then_inc(S(sem), 1)

        ang, ki, kf, r = rope[:, 0], rope_i[:, 1], rope[:, 2], rope[:, 3]
        dve.wait_ge(S("pos_in"), 16)
        dve.wait_ge(S("constants"), 1)
        link(V.tensor_copy(kf[:, :, 0], pos_i[:]))
        link(V.tensor_tensor(ang, kf[:, :, 0:1].to_broadcast([P, NT, 16]),
                             rope[:, 7, 0:1, :].to_broadcast([P, NT, 16]), ALU.mult))
        link(V.tensor_scalar(kf, ang, 1.0 / (2 * math.pi), None, ALU.mult))
        link(V.tensor_copy(ki, kf))
        link(V.tensor_copy(kf, ki))
        c1 = 6.28125
        c2 = float(np.float32(np.floor((2 * math.pi - c1) * 2 ** 20) / 2 ** 20))
        c3 = 2 * math.pi - c1 - c2
        link(V.scalar_tensor_tensor(out=r, in0=kf, scalar=-c1, in1=ang, op0=ALU.mult, op1=ALU.add))
        link(V.scalar_tensor_tensor(out=r, in0=kf, scalar=-c2, in1=r, op0=ALU.mult, op1=ALU.add))
        link(V.scalar_tensor_tensor(out=r, in0=kf, scalar=-c3, in1=r, op0=ALU.mult, op1=ALU.add))
        V.tensor_scalar(r, r, 3.1415925, -3.1415925, ALU.min, ALU.max).then_inc(S("angles"), 1)
        squared()
        y = roots([(0, 2, D)])
        dve.wait_ge(S("g_mem_in"), 16)
        norm_rows(memx, y, 0, "rows_ready")
        squared()
        y = roots([(0, 2, D)])
        dve.wait_ge(S("turned"), 4)
        dve.wait_ge(S("g_mix_in"), 16)
        norm_rows(X, y, 1, "rows_ready")
        V.tensor_scalar(mtmp_i[:, 1, :], mtmp_i[:, 0, :], 3, None, ALU.bitwise_and)
        link(V.tensor_scalar(mtmp_i[:, 2, :], mtmp_i[:, 0, :], 15, None, ALU.bitwise_and))
        V.tensor_scalar(mtmp[:, 4, :], mtmp_i[:, 1, :], 0.0, None, ALU.is_equal)
        link(V.tensor_scalar(mtmp[:, 5, :], mtmp_i[:, 2, :], 0.0, None, ALU.is_equal))
        link(V.tensor_tensor(mtmp[:, 3, :], mtmp[:, 3, :], mtmp[:, 4, :], ALU.add))
        link(V.tensor_tensor(mtmp[:, 3, :], mtmp[:, 3, :], mtmp[:, 5, :], ALU.add))
        V.tensor_scalar(mtmp[:, 4, :], mtmp[:, 3, :], 0.0, BIG, ALU.is_equal, ALU.mult)
        V.tensor_scalar(mtmp[:, 5, :], mtmp[:, 3, :], 2.0, -math.log(2), ALU.is_equal, ALU.mult)
        link(V.tensor_scalar(mtmp[:, 6, :], mtmp[:, 3, :], 3.0, -math.log(3), ALU.is_equal, ALU.mult))
        link(V.tensor_tensor(mtmp[:, 4, :], mtmp[:, 4, :], mtmp[:, 5, :], ALU.add))
        link(V.tensor_tensor(mtmp[:, 4, :], mtmp[:, 4, :], mtmp[:, 6, :], ALU.add))
        link(V.tensor_tensor(NBs[:, 1, :], NBs[:, 0, :], mtmp[:, 4, :], ALU.add))
        dve.wait_ge(S("sines"), 1)
        link(V.tensor_tensor(rope[:, 6], rope[:, 5], rope[:, 5], ALU.mult))
        V.tensor_scalar(rope[:, 6], rope[:, 6], -2.0, 1.0, ALU.mult, ALU.add).then_inc(S("rope_tables"), 1)
        for t in range(NT):
            leave(KVm[:, t, :], take())
        after_leaving()
        dve.sem_inc(S("mem_kv_ready"), 1)

        def head_sums(src, out_ap):
            squared()
            V.tensor_reduce(out_ap, src, AX.X, ALU.add).then_inc(S("squares_read"), 1)
            head_sums.n += 1
            dve.wait_ge(S("squares_read"), head_sums.n)
        head_sums.n = 0

        def scale_heads(ap, y, h, d):
            link(V.tensor_tensor(ap, ap, y.rearrange("p (t h) -> p t h", t=NT).unsqueeze(3)
                                 .to_broadcast([P, NT, h, d]), ALU.mult))

        def gain_heads(ap, g, h, d):
            return V.tensor_tensor(ap, ap, g.unsqueeze(1).unsqueeze(1).to_broadcast([P, NT, h, d]), ALU.mult)

        def project(n):
            a, b, _ = CHUNKS[n]
            for t in range(NT):
                leave(proj[:, t, a:b], take()[:, 0:b - a])

        head_sums(SCR[:, 0:512].rearrange("p (t h d) -> p t h d", t=NT, h=MEM_H),
                  cols_of(0, 2).rearrange("p (t h) -> p t h", t=NT))
        y = roots([(0, 8, HD)])
        dve.wait_ge(S("smalls_in"), 16 * len(small_list))
        kv = heads(KVm[:, :, 0:256], MEM_H)
        scale_heads(kv, y, MEM_H, HD)
        gain_heads(kv, SG["g_km"], MEM_H, HD).then_inc(S("mem_keys_normed"), 1)
        project(0)
        project(1)
        after_leaving()
        dve.sem_inc(S("latents_ready"), 1)
        squared()
        y = roots([(0, 2, Q_RANK), (2, 4, KV_RANK)])
        for t in range(NT):
            for k, name, w in ((0, "cq", Q_RANK), (2, "ckv", KV_RANK)):
                ap = proj[:, t, COL[name][0]:COL[name][1]]
                ins = V.scalar_tensor_tensor(out=ap, in0=ap, scalar=y[:, k + t:k + t + 1], in1=SG["g_" + name],
                                             op0=ALU.mult, op1=ALU.mult)
        ins.then_inc(S("latents_normed"), 1)
        project(2)
        after_leaving()
        dve.sem_inc(S("fox_ready"), 1)
        head_sums(SCR[:, 0:1024].rearrange("p (t h d) -> p t h d", t=NT, h=8),
                  cols_of(0, 4).rearrange("p (t h) -> p t h", t=NT))
        y = roots([(0, 16, HD)])
        fox = heads(proj[:, :, 0:512], 8)
        scale_heads(fox, y, 8, HD)
        gain_heads(fox[:, :, 0:4], SG["g_qa"], 4, HD)
        gain_heads(fox[:, :, 4:8], SG["g_ka"], 4, HD).then_inc(S("fox_normed"), 1)
        project(3)
        after_leaving()
        link(V.tensor_tensor(fz, proj[:, :, COL["fa"][0]:COL["fa"][1]],
                             SG["b_forget"].unsqueeze(1).to_broadcast([P, NT, FOX_H]), ALU.add))
        link(V.tensor_scalar(fa2, fz, -1.0, None, ALU.mult))
        V.tensor_tensor(fe, fz, fa2, ALU.max).then_inc(S("forget_abs"), 1)
        dve.wait_ge(S("forget_abs"), 1)
        link(V.tensor_scalar(fz, fz, 0.0, None, ALU.min))
        dve.wait_ge(S("forget_log"), 1)
        V.tensor_tensor(logf, fz, fe, ALU.subtract).then_inc(S("logf_ready"), 1)
        for t in range(NT):
            for half in range(2):
                leave(QKb[:, 0, t, 3 * half:3 * half + 3, :], take()[:, 0:3 * QK].rearrange("p (h d) -> p h d", d=QK))
        for t in range(NT):
            for half in range(2):
                b = take()[:, 0:384].rearrange("p (h d) -> p h d", d=128)
                V.tensor_copy(QKb[:, 1, t, 3 * half:3 * half + 3, 0:NOPE], b[:, :, 0:NOPE])
                leave(Vb[:, t, 3 * half:3 * half + 3, :], b[:, :, NOPE:])
        V.tensor_copy(QKb[:, 1, :, :, NOPE:], proj[:, :, COL["kr"][0]:COL["kr"][1]].unsqueeze(2)
                      .to_broadcast([P, NT, MLA_H, ROPE])).then_inc(S("mla_ready"), 1)
        head_sums(SCR[:, 0:2304].rearrange("p (w h d) -> p w h d", w=2, d=QK),
                  cols_of(0, 5).rearrange("p (w h) -> p w h", w=2))
        y = roots([(0, 24, QK)])
        project(4)
        for w, g in ((0, "g_qb"), (1, "g_kb")):
            ap = QKb[:, w]
            link(V.tensor_tensor(ap, ap, y[:, 12 * w:12 * w + 12].rearrange("p (t h) -> p t h", t=NT).unsqueeze(3)
                                 .to_broadcast([P, NT, MLA_H, QK]), ALU.mult))
            ins = gain_heads(ap, SG[g], MLA_H, QK)
        ins.then_inc(S("mla_normed"), 1)
        project(5)
        after_leaving()
        dve.sem_inc(S("dil_ready"), 1)
        dve.wait_ge(S("logf_ready"), 1)
        dve.wait_ge(S("squares_read"), 3)
        head_sums(SCR[:, 0:1536].rearrange("p (t h d) -> p t h d", t=NT, h=12),
                  cols_of(0, 6).rearrange("p (t h) -> p t h", t=NT))
        V.tensor_copy(logfb, logf.unsqueeze(3).to_broadcast([P, NT, FOX_H, P])).then_inc(S("logf_wide"), 1)
        y = roots([(0, 24, HD)])
        dil = heads(proj[:, :, COL["qc"][0]:COL["kc"][1]], 12)
        scale_heads(dil, y, 12, HD)
        gain_heads(dil[:, :, 0:6], SG["g_qc"], 6, HD)
        gain_heads(dil[:, :, 6:12], SG["g_kc"], 6, HD).then_inc(S("dil_normed"), 1)
        project(6)
        leave(cumq, take()[:, 0:8].rearrange("p (t h) -> p t h", t=NT))
        after_leaving()
        for h in range(FOX_H):
            b = take()
            V.scalar_tensor_tensor(out=foxNB[:, h, 0:P], in0=b[:, 0:P], scalar=cumq[:, 0, h:h + 1],
                                   in1=NBs[:, 0, 0:P], op0=ALU.subtract, op1=ALU.add)
            V.scalar_tensor_tensor(out=foxNB[:, h, P:], in0=b[:, 0:2 * P], scalar=cumq[:, 1, h:h + 1],
                                   in1=NBs[:, 0, P:], op0=ALU.subtract, op1=ALU.add).then_inc(S("mm_out"), 1)
        after_leaving()
        dve.sem_inc(S("fox_bias_made"), 1)

        scored = [0]

        def attend(units_, cols, between=()):
            first = scored[0]
            between = list(between)
            spans = [(0, cols - 256), (cols - 256, cols)]
            for what, u in order(len(units_)):
                q, k, v, nb, scale, o_ap = units_[u]
                c = 2 * (u % 2)
                if what == "score":
                    b = take()
                    if first + u >= 2:
                        dve.wait_ge(S("exped"), first + u - 1)
                    if nb is None:
                        V.tensor_scalar(Sb[:, u % 2, 0:cols], b[:, 0:cols], scale, None,
                                        ALU.mult).then_inc(S("mm_out"), 1)
                    else:
                        V.scalar_tensor_tensor(out=Sb[:, u % 2, 0:cols], in0=b[:, 0:cols], scalar=scale, in1=nb,
                                               op0=ALU.mult, op1=ALU.subtract).then_inc(S("mm_out"), 1)
                    after_leaving()
                    for t, (a, e) in enumerate(spans):
                        ins = V.tensor_reduce(rowtmp[:, c + t:c + t + 1], Sb[:, u % 2, a:e], AX.X, ALU.max)
                    link(ins)
                    V.tensor_scalar(rowmax[:, c:c + 2], rowtmp[:, c:c + 2], -1.0, None,
                                    ALU.mult).then_inc(S("scored"), 1)
                    scored[0] += 1
                if what == "value":
                    b = take()
                    link(V.reciprocal(rowinv[:, c:c + 2], rowsum[:, 2 * (u % 4):2 * (u % 4) + 2]))
                    V.tensor_tensor(o_ap, b[:, 0:2 * HD].rearrange("p (t d) -> p t d", t=NT),
                                    rowinv[:, c:c + 2].unsqueeze(2).to_broadcast([P, NT, HD]),
                                    ALU.mult).then_inc(S("mm_out"), 1)
                    if between:
                        between.pop(0)()
            after_leaving()

        dve.wait_ge(S("turned"), 8)
        attend(SELF[:FIRST], 384)
        dve.sem_inc(S("self_done"), 1)
        dve.wait_ge(S("g_group_in"), 16)

        def norm_group(t, a, e, y):
            return V.scalar_tensor_tensor(out=H[:, t, a:e], in0=H[:, t, a:e], scalar=y, in1=gain[:, 0, a:e],
                                          op0=ALU.mult, op1=ALU.mult)

        def first_roots():
            squared()
            roots([(0, 2, 256), (2, 4, 384)])

        def norm_first(t):
            y = cols_of(2, 7)
            norm_group(t, 0, 256, y[:, t:t + 1])
            norm_group(t, 256, 640, y[:, 2 + t:3 + t]).then_inc(S("rows_ready"), 1)

        attend(SELF[FIRST:], 384, [first_roots, lambda: norm_first(0), lambda: norm_first(1)])
        dve.sem_inc(S("self_done"), 1)
        squared()
        y = roots([(0, 2, 384)])
        for t in range(NT):
            ins = norm_group(t, 640, 1024, y[:, t:t + 1])
        ins.then_inc(S("rows_ready"), 1)

        def add_tile(t, sem):
            for half in range(2):
                b = take()
                ap = X[:, t, 512 * half:512 * half + 512]
                V.tensor_tensor(ap, ap, b, ALU.add).then_inc(S("mm_out"), 1)
            after_leaving()
            dve.sem_inc(S(sem), 1)

        def add_and_norm(g, left, after, sem):
            for t in range(NT):
                add_tile(t, after)
                squared()
                y = roots([(0, 1, D)])
                if t == 0:
                    dve.wait_ge(*left)
                norm_rows(X, y, g, sem, [t])

        dve.wait_ge(S("g_xmem_in"), 16)
        add_and_norm(1, (S("rows_left"), 1), "x1_ready", "rows_ready")
        for t in range(NT):
            leave(qm[:, t, :], take()[:, 0:256])
            after_leaving()
            dve.sem_inc(S("mem_q_ready"), 1)
            head_sums(SCR[:, 256 * t:256 * t + 256].rearrange("p (h d) -> p h d", h=MEM_H), cols_of(0, 11 + t))
            y = roots([(0, MEM_H, HD)])
            q4 = qm[:, t, :].rearrange("p (h d) -> p h d", h=MEM_H)
            link(V.tensor_tensor(q4, q4, y.unsqueeze(2).to_broadcast([P, MEM_H, HD]), ALU.mult))
            V.tensor_tensor(q4, q4, SG["g_qm"].unsqueeze(1).to_broadcast([P, MEM_H, HD]),
                            ALU.mult).then_inc(S("mem_q_normed"), 1)
        attend(MEM, 512)
        dve.sem_inc(S("mem_attended"), 1)

        def low(i, k, w2=False, last=False):
            slot = k // 2 + (W1_UNITS if w2 else 0)
            n, b = part(i, k, w2, last)
            dve.wait_ge(S("high_made"), n)
            V.tensor_tensor(split[:, b, 1, :], ring[:, slot, HALF * (k % 2):HALF * (k % 2) + HALF],
                            split[:, b, 0, :].bitcast(F32), ALU.subtract).then_inc(S("parts_made"), 1)

        for k in range(EARLY):
            low(0, k)
        dve.wait_ge(S("g_ffn_in"), 16)
        add_and_norm(0, (S("rows_left"), 2), "x2_ready", "h_ready")
        dve.wait_ge(S("h_high"), 1)
        for t in range(NT):
            ins = V.tensor_tensor(XR[:, 1, t, :], H[:, t, :], XR[:, 0, t, :].bitcast(F32), ALU.subtract)
        ins.then_inc(S("h_used"), 1)

        L, top, rep, ex, mask, gate, rank = rt[:, 0], rt[:, 1], rt[:, 3], rt[:, 4], rt[:, 5], rt[:, 6], rt[:, 7]
        for t in range(NT):
            V.tensor_tensor(L[:, t, 0:E], take()[:, 0:E], SG["b_router"], ALU.add).then_inc(S("mm_out"), 1)
        link(V.memset(L[:, :, E:], 3e38))
        for t in range(NT):
            ins = V.max(out=top[:, t, 0:8], in_=L[:, t, :])
        link(ins)
        for t in range(NT):
            V.match_replace(out=rep[:, t, :], in_to_replace=top[:, t, 0:8], in_values=L[:, t, :], imm_value=-3e38)
        V.tensor_scalar(rt[:, 2, :, 0:1], top[:, :, 4:5], -1.0, None, ALU.mult).then_inc(S("logits_ready"), 1)
        dve.wait_ge(S("logits_ready"), 1)
        V.tensor_tensor(mask[:, :, 0:E], L[:, :, 0:E], rep[:, :, 0:E], ALU.not_equal).then_inc(S("mask_ready"), 1)
        dve.wait_ge(S("mask_ready"), 1)
        dve.wait_ge(S("gates_exped"), 1)
        link(V.tensor_tensor(ex[:, :, 0:E], ex[:, :, 0:E], mask[:, :, 0:E], ALU.mult))
        link(V.tensor_reduce(rt[:, 2, :, 8], ex[:, :, 0:E], AX.X, ALU.add))
        link(V.reciprocal(rt[:, 2, :, 9], rt[:, 2, :, 8]))
        V.tensor_tensor(gate[:, :, 0:E], ex[:, :, 0:E], rt[:, 2, :, 9:10].to_broadcast([P, NT, E]),
                        ALU.mult).then_inc(S("gate_ready"), 1)
        b = take()
        link(V.scalar_tensor_tensor(out=rank[:, :, 0:E], in0=b[:, 0:2 * E].rearrange("p (t e) -> p t e", t=NT),
                                    scalar=1.0, in1=mask[:, :, 0:E], op0=ALU.add, op1=ALU.mult))
        most = rt[:, 2, 0, 12:20]
        link(V.tensor_reduce(most[:, 0:1], b[:, 2 * E:3 * E], AX.X, ALU.max))
        for r in range(1, MAX_ROUNDS):
            ins = V.tensor_scalar(most[:, r:r + 1], most[:, 0:1], SLOTS * r + 0.5, float(E), ALU.is_gt, ALU.mult)
        link(ins)
        link(V.tensor_tensor(most[:, 4:5], most[:, 1:2], most[:, 2:3], ALU.add))
        V.tensor_tensor(more_i[:], most[:, 4:5], most[:, 3:4], ALU.add).then_inc(S("more_known"), 1)
        dve.wait_ge(S("more_known"), 1)
        dve.sem_inc(S("mask_read"), 1)
        dve.wait_ge(S("tables_clear"), 1)
        dve.wait_ge(S("gate_ready"), 1)
        for r in range(MAX_ROUNDS):
            V.tensor_scalar(slot_of[:, :, E * r:E * r + E], rank[:, :, 0:E], -1.0 - SLOTS * r, None, ALU.add)
            ins = V.tensor_copy(gate_of[:, :, E * r:E * r + E], gate[:, :, 0:E])
        ins.then_inc(S("tables_made"), 1)
        def add_bias(t):
            dve.wait_ge(S("b2_done"), t + 1)
            V.tensor_tensor(X[:, t, :], X[:, t, :], PS[:, 6:8, :].rearrange("p b n -> p (b n)"),
                            ALU.add).then_inc(S("b2_added"), 1)

        def glu_sum(j):
            e = j % E
            n = j + 1
            bias = [b1T[:, bass.ds(e, 1), par:16:2].rearrange("p a c -> p (a c)").unsqueeze(2)
                    .to_broadcast([P, KC, SLOTS]) for par in range(2)]
            turned = [PS[:, 4 + par, :].rearrange("p (c s) -> p c s", c=KC) for par in range(2)]
            dve.wait_ge(S("hidden_turned"), n)
            V.tensor_tensor(glu[:], turned[0], bias[0], ALU.add).then_inc(S("glu_summed"), 1)
            V.tensor_tensor(lin[:], turned[1], bias[1], ALU.add).then_inc(S("lin_summed"), 1)
            dve.wait_ge(S("glu_summed"), n)
            V.tensor_scalar(glu[:], glu[:], LIMIT, None, ALU.min).then_inc(S("glu_ready"), 1)

        def glu_times_lin(j):
            n = j + 1
            dve.wait_ge(S("lin_summed"), n)
            V.tensor_scalar(lin[:], lin[:], LIMIT, -LIMIT, ALU.min, ALU.max).then_inc(S("lin_ready"), 1)
            dve.wait_ge(S("lin_ready"), n)
            dve.wait_ge(S("glu_ready"), n)
            V.scalar_tensor_tensor(out=lin[:], in0=lin[:], scalar=1.0, in1=glu[:], op0=ALU.add,
                                   op1=ALU.mult).then_inc(S("glu_lin_ready"), 1)

        def activate(j):
            n = j + 1
            dve.wait_ge(S("sig_ready"), n)
            dve.wait_ge(S("glu_lin_ready"), n)
            V.tensor_tensor(lin[:], lin[:], sig[:], ALU.mult).then_inc(S("act_full_ready"), 1)
            dve.wait_ge(S("act_full_ready"), n)
            V.tensor_copy(actr[:, :, 0, :], lin[:]).then_inc(S("act_high_ready"), 1)
            dve.wait_ge(S("act_high_ready"), n)
            V.tensor_tensor(actr[:, :, 1, :], lin[:], actr[:, :, 0, :].bitcast(F32),
                            ALU.subtract).then_inc(S("act_ready"), 1)

        def step(i, w1, w2, last=False):
            def lows(a, b, w2_=False):
                for k in range(a, b):
                    if (w1 or w2_) and not (isinstance(i, int) and i == 0 and k < EARLY):
                        low(i, k, w2_, last)

            at = 7 if isinstance(i, int) and i == 1 else 4
            lows(0, at)
            if w2:
                glu_sum(i - 1)
            lows(at, at + 1)
            if w2:
                glu_times_lin(i - 1)
            lows(at + 1, 8)
            if w2:
                activate(i - 1)
            if isinstance(i, int) and i == 0:
                lows(8, 10)
                add_bias(0)
                lows(10, 14)
                add_bias(1)
                lows(14, PARTS_W1)
            else:
                lows(8, PARTS_W1)
            if w2:
                lows(0, PARTS_W2, True)

        dve.wait_ge(S("tables_clear"), 1)
        step(0, True, False)
        step(1, True, True)
        nn = dve.value_load(more_i[0:1, 0:1], min_val=0, max_val=STEPS - E) + E
        with dve.Fori(2, nn) as i:
            step(i, True, True)
        step(nn, False, True, last=True)
        dve.wait_ge(S("added"), 2 * (nn - 1))
        for t in range(NT):
            dve.wait_ge(S("scattered"), 2 * (nn - 1) + t + 1)
            V.tensor_tensor(X[:, t, :], X[:, t, :], PS[:, 6 - 2 * t:8 - 2 * t, :].rearrange("p b n -> p (b n)"),
                            ALU.add).then_inc(S("tile_done"), 1)

    @blk.tensor
    def _(pe):
        product, turn = Banks(4), Banks(0)

        def into():
            bank = product.next()
            if product.n > 4:
                pe.wait_ge(S("mm_out"), product.n - 4)
            return bank

        def turn_into():
            bank = turn.next()
            if turn.n > 4:
                pe.wait_ge(S("turned_out"), turn.n - 4)
            return bank

        def turn_blocks(blocks, rows=P):
            bank = turn_into()
            for k, src in enumerate(blocks):
                ins = TE.transpose(bank[0:rows, P * k:P * k + P], src, ident[:])
            ins.then_inc(S("turned"), 1)

        def turn_rows(src, tiles=range(NT)):
            for t in tiles:
                for half in range(2):
                    turn_blocks([src[:, t, P * c:P * c + P] for c in range(4 * half, 4 * half + 4)])

        def multiply(lhs, rhs, n, out_cols=None):
            bank = into()
            for c in range(n):
                l, r = lhs(c), rhs(c)
                ins = TE.matmul(bank[:, 0:r.shape[-1]], l, r, start=(c == 0), stop=(c == n - 1))
            ins.then_inc(S("mm_done"), 1)

        def rows(t):
            return lambda c: hT[:, c, t * P:(t + 1) * P]

        def signal(sem):
            pe.wait_ge(S("mm_done"), product.n)
            pe.sem_inc(S(sem), 1)

        pe.wait_ge(S("constants"), 1)
        pe.wait_ge(S("rows_ready"), 1)
        turn_rows(H)
        pe.wait_ge(S("turned_out"), 4)
        pe.wait_ge(S("w_mkv_in"), 16)
        for t in range(NT):
            multiply(rows(t), lambda c: wmkv[:, c, :], KC)
        signal("mem_projected")
        pe.wait_ge(S("rows_ready"), 2)
        turn_rows(H)
        pe.wait_ge(S("turned_out"), 8)

        def project(n):
            pe.wait_ge(S(f"w_in{n}_in"), 16)
            for t in range(NT):
                multiply(rows(t), lambda c: win[n][:, c, :], KC)

        project(0)
        project(1)
        pe.wait_ge(S("mem_keys_normed"), 1)
        turn_blocks([KVm[:, t, P * j:P * j + P] for j in range(2) for t in range(NT)])
        project(2)
        pe.wait_ge(S("latents_normed"), 1)
        cq0, ckv0 = COL["cq"][0], COL["ckv"][0]
        for t in range(NT):
            turn_blocks([proj[:, t, cq0 + P * c:cq0 + P * c + P] for c in range(3)])
        turn_blocks([proj[:, t, ckv0 + P * c:ckv0 + P * c + P] for c in range(2) for t in range(NT)])
        project(3)
        pe.wait_ge(S("turned_out"), turn.n)
        pe.wait_ge(S("w_uq_in"), 16)
        for t in range(NT):
            for half in range(2):
                multiply(lambda c: cqT[:, c, t * P:(t + 1) * P],
                         lambda c: wuq[:, c, 288 * half:288 * half + 288], 3)
        pe.wait_ge(S("w_ukv_in"), 16)
        for t in range(NT):
            for half in range(2):
                multiply(lambda c: ckvT[:, c, t * P:(t + 1) * P],
                         lambda c: wukv[:, c, 384 * half:384 * half + 384], 2)
        signal("latents_projected")
        project(4)
        pe.wait_ge(S("fox_normed"), 1)
        for w in range(2):
            turn_blocks([proj[:, t, 256 * w + P * j:256 * w + P * j + P] for j in range(2) for t in range(NT)])
        project(5)
        project(6)
        signal("projected")
        pe.wait_ge(S("logf_wide"), 1)
        bank = into()
        TE.matmul(bank[:, 0:4], U[:, 0, :], logf[:, 0, :], start=True, stop=True)
        TE.matmul(bank[:, 4:8], U[:, 2, :], logf[:, 0, :], start=True, stop=False)
        TE.matmul(bank[:, 4:8], U[:, 0, :], logf[:, 1, :], start=False, stop=True).then_inc(S("mm_done"), 1)
        for h in range(FOX_H):
            bank = into()
            TE.matmul(bank[:, 0:P], logfb[:, 0, h, :], U[:, 0, :], start=True, stop=True)
            TE.matmul(bank[:, P:2 * P], logfb[:, 0, h, :], U[:, 2, :], start=True, stop=False)
            TE.matmul(bank[:, P:2 * P], logfb[:, 1, h, :], U[:, 0, :], start=False,
                      stop=True).then_inc(S("mm_done"), 1)
        pe.wait_ge(S("mla_rotated"), 1)
        for w in range(2):
            for pair in range(3):
                turn_blocks([QKb[:, w, t, h, :] for h in (2 * pair, 2 * pair + 1) for t in range(NT)], QK)
        pe.wait_ge(S("turned_out"), turn.n)

        exped = [0]

        def attend(units_, cols):
            first = exped[0]
            turned_at = {}
            full = cols == 512
            for what, u in order(len(units_)):
                q, k, v, nb, scale, o_ap = units_[u]
                if what == "score":
                    bank = into()
                    TE.matmul(bank[:, 0:cols - 256], q[:, 0:P], k[:, 0:cols - 256], start=True, stop=True)
                    TE.matmul(bank[:, cols - 256:cols], q[:, P:2 * P], k[:, 0:256], start=True,
                              stop=True).then_inc(S("mm_done"), 1)
                if what == "turn":
                    pe.wait_ge(S("exped"), first + u + 1)
                    turn_blocks([Pb[:, u % 2, a:a + P] for a in range(0, cols, P)])
                    turned_at[u] = turn.n
                if what == "value":
                    pe.wait_ge(S("turned_out"), turned_at[u])
                    bank = into()
                    n0 = 2 if full else 1
                    for t, n_, at_ in ((0, n0, 0), (1, 2, n0)):
                        for c in range(n_):
                            a = P * (at_ + c)
                            ins = TE.matmul(bank[:, HD * t:HD * t + HD], PTb[:, u % 2, a:a + P], v[c],
                                            start=(c == 0), stop=(c == n_ - 1))
                    ins.then_inc(S("mm_done"), 1)
            exped[0] += len(units_)

        assert product.n == MM_SELF
        attend(SELF[:FIRST], 384)
        pe.wait_ge(S("dil_rotated"), 1)
        q0 = COL["qc"][0]
        for w in range(2):
            turn_blocks([proj[:, t, q0 + 384 * w + P * j:q0 + 384 * w + P * j + P] for j in range(2)
                         for t in range(NT)])
            turn_blocks([proj[:, t, q0 + 384 * w + 2 * P:q0 + 384 * w + 3 * P] for t in range(NT)])
        pe.wait_ge(S("turned_out"), turn.n)
        attend(SELF[FIRST:], 384)
        pe.wait_ge(S("rows_ready"), 4)
        for t in range(NT):
            turn_blocks([H[:, t, P * c:P * c + P] for c in range(4)])
            turn_blocks([H[:, t, 4 * P:5 * P]])
        pe.wait_ge(S("turned_out"), turn.n)
        pe.wait_ge(S("w_out_in"), 16)
        merged = [into() for _ in range(2 * NT)]

        def merge(t, chunks):
            for half in range(2):
                for c in chunks:
                    ins = TE.matmul(merged[2 * t + half][:, :], hT[:, c, t * P:(t + 1) * P],
                                    wout[:, c, 512 * half:512 * half + 512], start=(c == 0), stop=(c == KC - 1))
                if c == KC - 1:
                    ins.then_inc(S("mm_done"), 1)

        for t in range(NT):
            merge(t, range(5))
        pe.wait_ge(S("rows_ready"), 5)
        for t in range(NT):
            turn_blocks([H[:, t, P * c:P * c + P] for c in range(5, KC)])
        pe.wait_ge(S("turned_out"), turn.n)
        pe.sem_inc(S("rows_left"), 1)
        for t in range(NT):
            merge(t, range(5, KC))
            pe.wait_ge(S("mm_done"), product.n - 2 * (NT - 1 - t))
            pe.sem_inc(S("merged_out"), 1)
        pe.wait_ge(S("w_mq_in"), 16)
        for t in range(NT):
            pe.wait_ge(S("rows_ready"), 6 + t)
            turn_rows(H, [t])
            pe.wait_ge(S("turned_out"), turn.n)
            multiply(rows(t), lambda c: wmq[:, c, :], KC)
            signal("mem_queried")
        pe.sem_inc(S("rows_left"), 1)
        for t in range(NT):
            pe.wait_ge(S("mem_q_normed"), t + 1)
            turn_blocks([qm[:, t, P * j:P * j + P] for j in range(2)])
        pe.wait_ge(S("turned_out"), turn.n)
        assert product.n == MM_MEM
        attend(MEM, 512)
        pe.wait_ge(S("mem_attended"), 1)
        turn_blocks([om[:, t, P * j:P * j + P] for j in range(2) for t in range(NT)])
        pe.wait_ge(S("turned_out"), turn.n)
        pe.wait_ge(S("w_mo_in"), 16)
        for t in range(NT):
            for half in range(2):
                multiply(lambda c: omT[:, c, t * P:(t + 1) * P],
                         lambda c: wmo[:, c, 512 * half:512 * half + 512], 2)
            signal("mem_out")
        pe.wait_ge(S("router_in"), 16)
        for t in range(NT):
            pe.wait_ge(S("h_ready"), t + 1)
            turn_rows(H, [t])
            pe.wait_ge(S("turned_out"), turn.n)
            multiply(rows(t), lambda c: router_w[:, c, :], KC)
            signal("routed")
        pe.sem_inc(S("h_turned"), 1)
        pe.wait_ge(S("mask_ready"), 1)
        mask = rt[:, 5]
        bank = into()
        TE.matmul(bank[:, 0:E], U[:, 1, :], mask[:, 0, 0:E], start=True, stop=True)
        TE.matmul(bank[:, E:2 * E], U[:, 2, :], mask[:, 0, 0:E], start=True, stop=False)
        TE.matmul(bank[:, E:2 * E], U[:, 1, :], mask[:, 1, 0:E], start=False, stop=True)
        TE.matmul(bank[:, 2 * E:3 * E], U[:, 2, :], mask[:, 0, 0:E], start=True, stop=False)
        TE.matmul(bank[:, 2 * E:3 * E], U[:, 2, :], mask[:, 1, 0:E], start=False,
                  stop=True).then_inc(S("mm_done"), 1)
        pe.wait_ge(S("gate_ready"), 1)
        turn_blocks([rt[:, 6, t, 0:E] for t in range(NT)], E)
        pe.wait_ge(S("b1_in"), 16)
        turn_blocks([b1s[:, 256 * c + par:256 * c + 256:2] for c in range(2) for par in range(2)])

        def gather(i, c):
            if c == 0:
                pe.wait_ge(S("hot_made"), i + 1)
                if not (isinstance(i, int) and i < 2):
                    pe.wait_ge(S("act_ready"), i - 1)
            for w in range(2):
                a = P * (c % 4) + SLOTS * w
                for t in range(NT):
                    ins = TE.matmul(PS[:, 4 + c // 4, a:a + SLOTS], XR[:, w, t, P * c:P * c + P], hotr[:, t, :],
                                    start=(t == 0), stop=(t == NT - 1))
            if c == KC - 1:
                ins.then_inc(S("gathered"), 1)

        def turn_hot(j):
            pe.wait_ge(S("y_out"), j + 1)
            pe.wait_ge(S("hotg_made"), j + 1)
            for t in range(NT):
                ins = TE.transpose(PS[:, 6, t * P:(t + 1) * P], hotg[:, t, :], ident[:])
            ins.then_inc(S("hot_turned"), 1)

        def scatter(j, t, bank=6):
            pe.wait_ge(S("hotT_out"), j + 1)
            if t and bank == 6:
                pe.wait_ge(S("given_out"), 2 * j + 1)
            for b in range(2):
                ins = TE.matmul(PS[:, bank + b, :], hotT[:, t * P:(t + 1) * P], Ys[:, 512 * b:512 * b + 512],
                                start=True, stop=True)
            ins.then_inc(S("scattered"), 1)

        def give_biases(t):
            if t:
                pe.wait_ge(S("b2_added"), t)
            for b in range(2):
                ins = TE.matmul(PS[:, 6 + b, :], rt_gateT[:, t * P:(t + 1) * P], b2s[:, 512 * b:512 * b + 512],
                                start=True, stop=True)
            ins.then_inc(S("b2_done"), 1)

        def multiply_parts(n, buf, left, bank, first, final):
            pe.wait_ge(S("parts_made"), n)
            for w in range(2):
                for b in range(2):
                    ins = TE.matmul(PS[:, bank + b, :], left.rearrange("p w s -> p (w s)"),
                                    split[:, buf, w, 512 * b:512 * b + 512],
                                    start=(first and w == 0), stop=(final and w == 1))
            ins.then_inc(S("parts_used"), 1)

        def turn_hidden(i, c):
            if c == 0:
                pe.wait_ge(S("hidden_out"), i + 1)
                pe.wait_ge(S("xg_parts_out"), i + 2)
            for par in range(2):
                ins = TE.matmul(PS[:, 4 + par, SLOTS * c:SLOTS * c + SLOTS],
                                Hs[:, 256 * c + par:256 * c + 256:2], stack[:], start=True, stop=True)
            if c == KC - 1:
                ins.then_inc(S("hidden_turned"), 1)

        def step(i, w1, w2, scat, last=False):
            if w1:
                pe.wait_ge(S("xg_parts_out"), i + 1)
                if not (isinstance(i, int) and i == 0):
                    pe.wait_ge(S("hidden_out"), i)
            for k in range(PARTS_W1):
                if w1:
                    multiply_parts(*part(i, k), xgr[:, k // 2], 2 * (k % 2), k < 2, k >= PARTS_W1 - 2)
                if isinstance(i, int) and i == 1 and k < 4:
                    turn_hidden(0, 2 * k)
                    turn_hidden(0, 2 * k + 1)
                if isinstance(i, int) and i == 0 and k in AT_SCATTER:
                    give_biases(AT_SCATTER.index(k))
                if scat and k == AT_TURN:
                    turn_hot(i - 2)
                if scat and k in AT_SCATTER:
                    scatter(i - 2, AT_SCATTER.index(k))
                if w1 and k >= PARTS_W1 - 1 - KC and k < PARTS_W1 - 1:
                    gather(i + 1, k - (PARTS_W1 - 1 - KC))
            if w2:
                pe.wait_ge(S("act_ready"), i)
                if scat:
                    pe.wait_ge(S("given_out"), 2 * (i - 1))
                else:
                    pe.wait_ge(S("b2_added"), NT)
                for cc in range(KC):
                    multiply_parts(*part(i, cc, True, last), actr[:, cc], 6, cc == 0, cc == KC - 1)
                    if w1 and cc >= KC // 2:
                        turn_hidden(i, 2 * (cc - KC // 2))
                        turn_hidden(i, 2 * (cc - KC // 2) + 1)

        pe.wait_ge(S("tables_clear"), 1)
        pe.wait_ge(S("h_used"), 1)
        pe.wait_ge(S("b2_in"), 16)
        pe.wait_ge(S("turned_out"), turn.n)
        pe.wait_ge(S("mask_read"), 1)
        for c in range(KC):
            gather(0, c)
        step(0, True, False, False)
        step(1, True, True, False)
        nn = pe.value_load(more_i[0:1, 0:1], min_val=0, max_val=STEPS - E) + E
        with pe.Fori(2, nn) as i:
            step(i, True, True, True)
        step(nn, False, True, True, last=True)
        turn_hot(nn - 1)
        scatter(nn - 1, 0)
        scatter(nn - 1, 1, bank=4)

    block.__exit__(None, None, None)


_INS = ["x", "mem", "positions", "g_mix", "w_in", "b_forget", "g_qa", "g_ka", "g_cq", "g_ckv", "w_uq", "w_ukv",
        "g_qb", "g_kb", "g_qc", "g_kc", "g_group", "w_out", "g_xmem", "g_mem", "w_mq", "w_mkv", "g_qm", "g_km",
        "w_mo", "g_ffn", "w_router", "b_router", "w_e1", "b_e1", "w_e2", "b_e2"]
_OUTS = [((1, T, D), "float32")]


def kernel(**inputs):
    import numpy as _np
    import concourse.bacc as _bacc
    from concourse import mybir as _mybir
    from concourse.bass_utils import run_bass_kernel_spmd as _run

    nc = _bacc.Bacc("TRN2", target_bir_lowering=False, num_devices=1)
    arrays, args = {}, []
    for name in _INS:
        a = _np.ascontiguousarray(inputs[name])
        arrays[f"in_{name}_dram"] = a
        args.append(nc.dram_tensor(f"in_{name}_dram", a.shape, _mybir.dt.from_np(a.dtype), kind="ExternalInput").ap())
    for i, (shape, dtype) in enumerate(_OUTS):
        dt = _mybir.dt.from_np(_np.dtype(dtype))
        args.append(nc.dram_tensor(f"out_{i}_dram", shape, dt, kind="ExternalOutput").ap())
    build(nc, *args)
    r = _run(nc, [arrays], core_ids=[0])
    got = tuple(r.results[0][f"out_{i}_dram"] for i in range(len(_OUTS)))
    return got[0]
```
